# Optimizing a Trainium2 kernel written in Bass

```python
import math
import jax
import jax.numpy as jnp
from jax import lax
import numpy as np

D_MODEL = 1024
BATCH = 1
SEQ = 128
DEPTH = 2
DEC_BATCH = 1
DEC_SEQ = 256
PAST_LEN = 128

GRID_W = 64
GDN_HEADS = 4
GDN_DK = 128
GDN_DV = 128
GDN_W = GDN_HEADS * GDN_DV
SHORT_CONV = 5
GDN_CHUNK = 64
GLA_HEADS = 4
GLA_DK = 64
GLA_DV = 128
GLA_KW = GLA_HEADS * GLA_DK
GLA_VW = GLA_HEADS * GLA_DV
GLA_RANK = 16
GLA_TAU = 16.0
GLA_CHUNK = 64
DIFF_HEADS = 4
DIFF_DH = 64
DIFF_VD = 2 * DIFF_DH
DIFF_QW = DIFF_HEADS * 2 * DIFF_DH
DIFF_VW = DIFF_HEADS * DIFF_VD
Q_BLOCK = 128
ROPE_THETA = 10000.0
MIX_W = 512
N_BRANCH = 3
N_EXPERTS = 16
N_GROUPS = 4
GROUP_SIZE = N_EXPERTS // N_GROUPS
TOP_K = 2
D_FF = 512
ALPHA = (2 * DEPTH) ** 0.25
BETA_INIT = (8 * DEPTH) ** -0.25
EPS = 1e-6
IN_SIZES = (3 * GDN_W, GDN_W, 2 * GDN_HEADS, 2 * GDN_HEADS,
            GLA_KW, GLA_KW, GLA_VW, GLA_VW, 2 * GLA_RANK,
            DIFF_QW, DIFF_QW, DIFF_VW, N_BRANCH * D_MODEL)
IN_SPLITS = tuple(sum(IN_SIZES[:i + 1]) for i in range(len(IN_SIZES) - 1))
D_IN = sum(IN_SIZES)

kernel_name = 'hybrid_diffusion_gdn_gla_diffattn_moe_step'

def _layernorm(x, g, b):
    xf = x.astype(jnp.float32)
    mu = jnp.mean(xf, -1, keepdims=True)
    var = jnp.mean(jnp.square(xf - mu), -1, keepdims=True)
    return ((xf - mu) * lax.rsqrt(var + EPS) * g + b).astype(x.dtype)

def _rmsnorm(x, g):
    xf = x.astype(jnp.float32)
    return xf * lax.rsqrt(jnp.mean(xf * xf, -1, keepdims=True) + EPS) * g.astype(jnp.float32)

def _l2norm(x):
    return x * lax.rsqrt(jnp.sum(x * x, -1, keepdims=True) + EPS)

def _flip(a):
    return jnp.flip(a, axis=2)

def _short_conv(x, w):
    K, C = w.shape
    return lax.conv_general_dilated(x, w[:, None, :], window_strides=(1,), padding=[(K // 2, K // 2)],
                                    dimension_numbers=('NWC', 'WIO', 'NWC'), feature_group_count=C)

def _gated_delta_chunked(q, k, v, beta, g, s0):
    B, H, T, dk = q.shape
    dv = v.shape[-1]
    C = GDN_CHUNK
    n = T // C
    q = q.reshape(B, H, n, C, dk)
    k = k.reshape(B, H, n, C, dk)
    v = v.reshape(B, H, n, C, dv)
    beta = beta.reshape(B, H, n, C)
    gc = jnp.cumsum(g.reshape(B, H, n, C), axis=-1)
    incl = jnp.tril(jnp.ones((C, C), dtype=bool))
    strict = jnp.tril(jnp.ones((C, C), dtype=bool), k=-1)
    rel = gc[..., :, None] - gc[..., None, :]
    decay = jnp.where(incl, jnp.exp(jnp.where(incl, rel, 0.0)), 0.0)
    k_beta = k * beta[..., None]
    lower = jnp.where(strict, jnp.einsum('bhnid,bhnjd->bhnij', k_beta, k) * decay, 0.0)
    rhs = jnp.concatenate([v * beta[..., None], k_beta * jnp.exp(gc)[..., None]], axis=-1)
    sol = lax.linalg.triangular_solve(lower + jnp.eye(C, dtype=q.dtype), rhs, left_side=True, lower=True)
    u, w = sol[..., :dv], sol[..., dv:]
    a_intra = jnp.where(incl, jnp.einsum('bhnid,bhnjd->bhnij', q, k) * decay, 0.0)
    q_dec = q * jnp.exp(gc)[..., None]
    k_tail = k * jnp.exp(gc[..., -1:] - gc)[..., None]
    g_tail = jnp.exp(gc[..., -1])

    def step(S, xs):
        u_c, w_c, a_c, qd_c, kt_c, gt_c = xs
        v_new = u_c - jnp.einsum('bhcd,bhde->bhce', w_c, S)
        o = jnp.einsum('bhcd,bhde->bhce', qd_c, S) + jnp.einsum('bhij,bhje->bhie', a_c, v_new)
        S = S * gt_c[..., None, None] + jnp.einsum('bhcd,bhce->bhde', kt_c, v_new)
        return S, o

    xs = tuple(jnp.moveaxis(a, 2, 0) for a in (u, w, a_intra, q_dec, k_tail, g_tail))
    s_fin, o = lax.scan(step, s0, xs)
    return jnp.moveaxis(o, 0, 2).reshape(B, H, T, dv), s_fin

def _gla_chunked(q, k, v, glog, s0):
    B, H, T, dk = q.shape
    dv = v.shape[-1]
    C = GLA_CHUNK
    n = T // C
    q = q.reshape(B, H, n, C, dk)
    k = k.reshape(B, H, n, C, dk)
    v = v.reshape(B, H, n, C, dv)
    b = jnp.cumsum(glog.reshape(B, H, n, C, dk), axis=3)
    b_ref = b[..., C // 2:C // 2 + 1, :]
    incl = jnp.tril(jnp.ones((C, C), dtype=bool))
    a_intra = jnp.where(incl, jnp.einsum('bhnid,bhnjd->bhnij', q * jnp.exp(b - b_ref), k * jnp.exp(b_ref - b)), 0.0)
    q_dec = q * jnp.exp(b)
    k_tail = k * jnp.exp(b[..., -1:, :] - b)
    g_tail = jnp.exp(b[..., -1, :])

    def step(S, xs):
        v_c, a_c, qd_c, kt_c, gt_c = xs
        o = jnp.einsum('bhcd,bhde->bhce', qd_c, S) + jnp.einsum('bhij,bhje->bhie', a_c, v_c)
        S = S * gt_c[..., :, None] + jnp.einsum('bhcd,bhce->bhde', kt_c, v_c)
        return S, o

    xs = tuple(jnp.moveaxis(a, 2, 0) for a in (v, a_intra, q_dec, k_tail, g_tail))
    s_fin, o = lax.scan(step, s0, xs)
    return jnp.moveaxis(o, 0, 2).reshape(B, H, T, dv), s_fin

def _axial_rope(x):
    n_tok = x.shape[1]
    rows = n_tok // GRID_W
    row_id = jnp.repeat(jnp.arange(rows), GRID_W).astype(jnp.float32)
    col_id = jnp.tile(jnp.arange(GRID_W), rows).astype(jnp.float32)
    half = DIFF_DH // 2
    inv = ROPE_THETA ** (-jnp.arange(0, half, 2, dtype=jnp.float32) / half)

    def rot(part, pos):
        ang = pos[:, None] * inv[None, :]
        cos = jnp.cos(ang)[None, :, None, None, :]
        sin = jnp.sin(ang)[None, :, None, None, :]
        p1, p2 = jnp.split(part, 2, axis=-1)
        return jnp.concatenate([p1 * cos - p2 * sin, p1 * sin + p2 * cos], axis=-1)

    xr, xc = jnp.split(x.astype(jnp.float32), 2, axis=-1)
    return jnp.concatenate([rot(xr, row_id), rot(xc, col_id)], axis=-1).astype(x.dtype)

def _diff_attention(q, k, v, lam):
    B, Tq, H = q.shape[:3]
    n_blk = Tq // Q_BLOCK
    q_blocks = jnp.moveaxis(q.astype(jnp.float32).reshape(B, n_blk, Q_BLOCK, H, 2, DIFF_DH), 1, 0)
    kf = k.astype(jnp.float32)
    vf = v.astype(jnp.float32)

    def block(qb):
        s = jnp.einsum('bqhsd,bkhsd->bshqk', qb, kf) * DIFF_DH ** -0.5
        p = jax.nn.softmax(s, axis=-1)
        w = p[:, 0] - lam * p[:, 1]
        return jnp.einsum('bhqk,bkhe->bqhe', w, vf)

    o = lax.map(block, q_blocks)
    return jnp.moveaxis(o, 0, 1).reshape(B, Tq, H, DIFF_VD)

def _mixer(u, w_in, conv_w, a_log, dt_bias, gdn_g, gla_wg, gla_bg, gla_g, lam_p, diff_g, w_branch, w_out,
           lam_init, gdn_s0, gla_s0, ctx_k, ctx_v):
    B, T, _ = u.shape
    f32 = jnp.float32
    (gdn_qkv, gdn_z, gdn_b, gdn_a, gla_q, gla_k, gla_v, gla_r, gla_lr,
     diff_q, diff_k, diff_v, merge_logit) = jnp.split(jnp.einsum('btd,dn->btn', u, w_in), IN_SPLITS, axis=-1)

    def heads(a, d):
        return a.reshape(B, T, -1, d).transpose(0, 2, 1, 3)

    qkv = jax.nn.silu(_short_conv(gdn_qkv, conv_w)).astype(f32)
    q, k, v = jnp.split(qkv, 3, axis=-1)
    q = _l2norm(heads(q, GDN_DK)) * GDN_DK ** -0.5
    k = _l2norm(heads(k, GDN_DK))
    v = heads(v, GDN_DV)
    beta = jax.nn.sigmoid(gdn_b.astype(f32)).reshape(B, T, 2, GDN_HEADS).transpose(2, 0, 3, 1)
    g = -jnp.exp(a_log.astype(f32))[:, None, :, None] * jax.nn.softplus(
        gdn_a.astype(f32).reshape(B, T, 2, GDN_HEADS).transpose(2, 0, 3, 1) + dt_bias.astype(f32)[:, None, :, None])
    s0 = gdn_s0.astype(f32)
    o_f, s_f = _gated_delta_chunked(q, k, v, beta[0], g[0], s0[:, 0])
    o_b, s_b = _gated_delta_chunked(_flip(q), _flip(k), _flip(v), _flip(beta[1]), _flip(g[1]), s0[:, 1])
    o_gdn = (o_f + _flip(o_b)).transpose(0, 2, 1, 3)
    o_gdn = (_rmsnorm(o_gdn, gdn_g) * jax.nn.silu(gdn_z.astype(f32)).reshape(B, T, GDN_HEADS, GDN_DV)).reshape(B, T, MIX_W)
    gdn_fin = jnp.stack([s_f, s_b], axis=1)

    q = heads(gla_q.astype(f32), GLA_DK) * GLA_DK ** -0.5
    k = heads(gla_k.astype(f32), GLA_DK)
    v = heads(gla_v.astype(f32), GLA_DV)
    lr = gla_lr.astype(f32).reshape(B, T, 2, GLA_RANK)
    logits = jnp.einsum('btsr,srk->sbtk', lr, gla_wg.astype(f32)) + gla_bg.astype(f32)[:, None, None, :]
    glog = (jax.nn.log_sigmoid(logits) / GLA_TAU).reshape(2, B, T, GLA_HEADS, GLA_DK).transpose(0, 1, 3, 2, 4)
    s0 = gla_s0.astype(f32)
    o_f, s_f = _gla_chunked(q, k, v, glog[0], s0[:, 0])
    o_b, s_b = _gla_chunked(_flip(q), _flip(k), _flip(v), _flip(glog[1]), s0[:, 1])
    o_gla = (o_f + _flip(o_b)).transpose(0, 2, 1, 3)
    o_gla = (_rmsnorm(o_gla, gla_g) * jax.nn.silu(gla_r.astype(f32)).reshape(B, T, GLA_HEADS, GLA_DV)).reshape(B, T, MIX_W)
    gla_fin = jnp.stack([s_f, s_b], axis=1)

    q = diff_q.reshape(B, T, DIFF_HEADS, 2, DIFF_DH)
    k = diff_k.reshape(B, T, DIFF_HEADS, 2, DIFF_DH)
    v = diff_v.reshape(B, T, DIFF_HEADS, DIFF_VD)
    k_own = k.reshape(B, T, DIFF_HEADS, 2 * DIFF_DH)
    v_own = v
    if ctx_k is not None:
        q = _axial_rope(q)
        k = jnp.concatenate([_axial_rope(k), ctx_k.reshape(B, -1, DIFF_HEADS, 2, DIFF_DH).astype(k.dtype)], axis=1)
        v = jnp.concatenate([v, ctx_v.astype(v.dtype)], axis=1)
    lp = lam_p.astype(f32)
    lam = jnp.exp(jnp.sum(lp[0] * lp[1])) - jnp.exp(jnp.sum(lp[2] * lp[3])) + lam_init
    o_diff = _diff_attention(q, k, v, lam)
    o_diff = (_rmsnorm(o_diff, diff_g) * (1.0 - lam_init)).reshape(B, T, MIX_W)

    branches = jnp.stack([o_gdn, o_gla, o_diff], axis=2).astype(u.dtype)
    proj = jnp.einsum('btsm,smd->btsd', branches, w_branch)
    gates = jax.nn.sigmoid(merge_logit.reshape(B, T, N_BRANCH, D_MODEL))
    out = jnp.einsum('btd,de->bte', jnp.sum(gates * proj, axis=2), w_out)
    return out, gdn_fin, gla_fin, k_own, v_own

def _moe(h, router_w, router_b, w_gate, w_up, w_down):
    B, T, D = h.shape
    tok = h.reshape(B * T, D)
    scores = jax.nn.sigmoid(jnp.dot(tok, router_w).astype(jnp.float32))
    biased = scores + router_b.astype(jnp.float32)
    grp_score = jnp.sum(lax.top_k(biased.reshape(-1, N_GROUPS, GROUP_SIZE), TOP_K)[0], axis=-1)
    best = jnp.argmax(grp_score, axis=-1)
    in_grp = (jnp.arange(N_EXPERTS) // GROUP_SIZE)[None, :] == best[:, None]
    _, idx = lax.top_k(jnp.where(in_grp, biased, -jnp.inf), TOP_K)
    w = jnp.take_along_axis(scores, idx, axis=-1)
    w = w / jnp.sum(w, axis=-1, keepdims=True)
    gates = jnp.sum(jax.nn.one_hot(idx, N_EXPERTS, dtype=jnp.float32) * w[..., None], axis=1)
    act = jax.nn.silu(jnp.einsum('nd,edf->nef', tok, w_gate)) * jnp.einsum('nd,edf->nef', tok, w_up)
    out = jnp.einsum('nef,efd->nd', act * gates[..., None].astype(act.dtype), w_down)
    return out.reshape(B, T, D).astype(h.dtype)

def setup_inputs(seed: int = 0) -> dict:
    key = jax.random.key(seed)
    ks = jax.random.split(key, 32)
    f32 = jnp.float32
    D = D_MODEL

    def nrm(k, shape, s):
        return jax.random.normal(k, shape, f32) * s

    dt = jnp.exp(jax.random.uniform(ks[13], (DEPTH, 2, GDN_HEADS), f32, math.log(1e-3), math.log(1e-1)))
    return {
        'x_prompt': nrm(ks[0], (BATCH, SEQ, D), 1.0),
        'x_sample': nrm(ks[1], (DEC_BATCH, DEC_SEQ, D), 1.0),
        'c': nrm(ks[2], (DEC_BATCH, D), 1.0),
        'state_gdn': nrm(ks[3], (DEC_BATCH, DEPTH, 2, GDN_HEADS, GDN_DK, GDN_DV), 0.1),
        'state_gla': nrm(ks[4], (DEC_BATCH, DEPTH, 2, GLA_HEADS, GLA_DK, GLA_DV), 0.5),
        'cache_k': nrm(ks[5], (DEC_BATCH, DEPTH, PAST_LEN, DIFF_HEADS, 2 * DIFF_DH), 1.0),
        'cache_v': nrm(ks[6], (DEC_BATCH, DEPTH, PAST_LEN, DIFF_HEADS, DIFF_VD), 1.0),
        'c_ctx': nrm(ks[7], (D,), 1.0),
        'w_mod': nrm(ks[8], (DEPTH, D, 6 * D), 0.5 * D ** -0.5),
        'b_mod': nrm(ks[9], (DEPTH, 6 * D), 0.02),
        'w_in': nrm(ks[10], (DEPTH, D, D_IN), D ** -0.5),
        'gdn_conv': nrm(ks[11], (DEPTH, SHORT_CONV, 3 * GDN_W), SHORT_CONV ** -0.5),
        'gdn_a_log': jnp.log(jax.random.uniform(ks[12], (DEPTH, 2, GDN_HEADS), f32, 1.0, 16.0)),
        'gdn_dt_bias': dt + jnp.log(-jnp.expm1(-dt)),
        'gdn_norm': 1.0 + nrm(ks[14], (DEPTH, GDN_DV), 0.02),
        'gla_w_gate': nrm(ks[15], (DEPTH, 2, GLA_RANK, GLA_KW), GLA_RANK ** -0.5),
        'gla_b_gate': nrm(ks[16], (DEPTH, 2, GLA_KW), 0.1),
        'gla_norm': 1.0 + nrm(ks[17], (DEPTH, GLA_DV), 0.02),
        'diff_lambda': nrm(ks[18], (DEPTH, 4, DIFF_DH), 0.1),
        'diff_norm': 1.0 + nrm(ks[19], (DEPTH, DIFF_VD), 0.02),
        'w_branch': nrm(ks[20], (DEPTH, N_BRANCH, MIX_W, D), MIX_W ** -0.5),
        'w_out': nrm(ks[21], (DEPTH, D, D), BETA_INIT * D ** -0.5),
        'ln_g': 1.0 + nrm(ks[22], (DEPTH, 2, D), 0.02),
        'ln_b': nrm(ks[23], (DEPTH, 2, D), 0.02),
        'router_w': nrm(ks[24], (D, N_EXPERTS), D ** -0.5),
        'router_b': nrm(ks[25], (N_EXPERTS,), 0.01),
        'exp_w_gate': nrm(ks[26], (DEPTH, N_EXPERTS, D, D_FF), D ** -0.5),
        'exp_w_up': nrm(ks[27], (DEPTH, N_EXPERTS, D, D_FF), D ** -0.5),
        'exp_w_down': nrm(ks[28], (DEPTH, N_EXPERTS, D_FF, D), BETA_INIT * D_FF ** -0.5),
    }

def reference(x_prompt, x_sample, c, state_gdn, state_gla, cache_k, cache_v, c_ctx, w_mod, b_mod, w_in,
              gdn_conv, gdn_a_log, gdn_dt_bias, gdn_norm, gla_w_gate, gla_b_gate, gla_norm, diff_lambda,
              diff_norm, w_branch, w_out, ln_g, ln_b, router_w, router_b, exp_w_gate, exp_w_up, exp_w_down):
    def layer(x, mod, l, gdn_s0, gla_s0, ctx_k, ctx_v):
        shift1, scale1, gate1, shift2, scale2, gate2 = jnp.split(mod.astype(x.dtype), 6, axis=-1)
        u = x * (1 + scale1) + shift1
        lam_init = 0.8 - 0.6 * math.exp(-0.3 * l)
        m, gdn_fin, gla_fin, k_own, v_own = _mixer(
            u, w_in[l], gdn_conv[l], gdn_a_log[l], gdn_dt_bias[l], gdn_norm[l], gla_w_gate[l], gla_b_gate[l],
            gla_norm[l], diff_lambda[l], diff_norm[l], w_branch[l], w_out[l], lam_init, gdn_s0, gla_s0, ctx_k, ctx_v)
        x = _layernorm(ALPHA * x + gate1 * m.astype(x.dtype), ln_g[l, 0], ln_b[l, 0])
        h = x * (1 + scale2) + shift2
        f = _moe(h, router_w, router_b, exp_w_gate[l], exp_w_up[l], exp_w_down[l])
        x = _layernorm(ALPHA * x + gate2 * f, ln_g[l, 1], ln_b[l, 1])
        return x, gdn_fin, gla_fin, k_own, v_own

    bp = x_prompt.shape[0]
    gdn_zero = jnp.zeros((bp, 2, GDN_HEADS, GDN_DK, GDN_DV), jnp.float32)
    gla_zero = jnp.zeros((bp, 2, GLA_HEADS, GLA_DK, GLA_DV), jnp.float32)
    hp = x_prompt
    gdn_states, gla_states, ks, vs = [], [], [], []
    for l in range(DEPTH):
        mod = (jax.nn.silu(c_ctx) @ w_mod[l] + b_mod[l])[None, None, :]
        hp, s_gdn, s_gla, k_l, v_l = layer(hp, mod, l, gdn_zero, gla_zero, None, None)
        gdn_states.append(s_gdn)
        gla_states.append(s_gla)
        ks.append(k_l)
        vs.append(v_l)
    y_prompt = hp

    hs = x_sample
    for l in range(DEPTH):
        mod = (jax.nn.silu(c) @ w_mod[l] + b_mod[l])[:, None, :]
        hs = layer(hs, mod, l, state_gdn[:, l], state_gla[:, l], cache_k[:, l], cache_v[:, l])[0]
    y_sample = hs

    return (y_prompt, y_sample, jnp.stack(gdn_states, axis=1), jnp.stack(gla_states, axis=1),
            jnp.stack(ks, axis=1), jnp.stack(vs, axis=1))


_drawn_inputs = setup_inputs


def setup_inputs(seed=0):
    import zlib

    import numpy as np

    out = dict(_drawn_inputs(seed))
    spreads = {}
    factors = {'state_gdn': 6.384,
     'state_gla': 8.0,
     'gdn_norm': 29.338,
     'gla_norm': 39.798,
     'diff_lambda': 4.051,
     'diff_norm': 29.717}
    for name, (base, spread) in spreads.items():
        noise = np.random.default_rng([zlib.crc32(name.encode()), seed]).standard_normal(out[name].shape)
        drawn = base * np.exp(spread * noise) if base else spread * noise
        out[name] = jnp.asarray(drawn.astype(out[name].dtype))
    for name, factor in factors.items():
        out[name] = (out[name] * factor).astype(out[name].dtype)
    return out
```

```python
from contextlib import ExitStack

import concourse.bass as bass
import numpy as np
from concourse import mybir

F32 = mybir.dt.float32
U32 = mybir.dt.uint32
ALU = mybir.AluOpType
ACT = mybir.ActivationFunctionType
AX = mybir.AxisListType

P = 128
D = 1024
KC = D // P
DEPTH = 2
SEQ, DEC = 128, 256
T = (SEQ + DEC) // P
TOK = T * P
H = 4
W5 = 512
GLA_DK = 64
HALF = 64
RANK = 16
DH = 64
PAST = 128
KEYS = DEC + PAST
TAPS = 5
E = 16
NG = 4
ALPHA = (2 * DEPTH) ** 0.25
EPS = 1e-6
TAU = 16.0
DIR = 2
LEVELS = 7
CW = TOK + 2
COL = (0, SEQ + 2, SEQ + 2 + P)
IN_COL = dict(qkv=0, z=1536, ba=2048, gqk=2064, gv=2576, r=3088, lr=3600, dq=3632, dk=4144, dv=4656, merge=5168)
RING = 3
LOOP_BANKS = 7
CHUNK_W = KC * W5
PAIRS = ((0, 0), (1, 2), (2, 1))


def lam_init(l):
    return 0.8 - 0.6 * float(np.exp(-0.3 * l))


def constants():
    k, i = np.arange(P)[:, None], np.arange(P)[None, :]
    same = (k // HALF) == (i // HALF)
    mats = dict(ident=k == i, tri0=k <= i, tri1=k >= i, ones=np.ones((P, P)))
    for n in range(LEVELS):
        b = 1 << n
        lower = (k // (2 * b) == i // (2 * b)) & (k // b % 2 == 0) & (i // b % 2 == 1)
        mats[f"level0_{n}"], mats[f"level1_{n}"] = lower, lower.T
    base = i // HALF * HALF
    for d in range(DIR):
        upto = lambda t: same & ((k <= t) if d == 0 else (k >= t))
        ref = base + (HALF // 2 if d == 0 else HALF // 2 - 1)
        mats[f"sum{d}"] = upto(i)
        mats[f"rel{d}"] = upto(i).astype(float) - upto(ref).astype(float)
        mats[f"tail{d}"] = same.astype(float) - upto(i).astype(float)
    cols = {n: np.asarray(m, np.float32) for n, m in mats.items()}
    cols["chunks"] = (k // HALF == np.arange(2)[None, :]).astype(np.float32)
    sel = np.zeros((P, 2 * P), np.float32)
    sel[0, :P], sel[1, P:] = 1.0, 1.0
    cols["sel"] = sel
    e, f = np.arange(4)[:, None], np.arange(4)[None, :]
    cols["before"] = np.broadcast_to((f < e).astype(np.float32).reshape(1, 16), (P, 16))
    pos = np.arange(DEC)
    inv = np.float32(10000.0) ** (-np.arange(0, 32, 2, dtype=np.float32) / np.float32(32))
    rot = np.zeros((DEC, 2, 2, 2, 16), np.float32)
    for half, where in enumerate((pos // 64, pos % 64)):
        ang = where.astype(np.float32)[:, None] * inv[None, :]
        rot[:, 0, half] = np.cos(ang)[:, None, :]
        rot[:, 1, half, 0], rot[:, 1, half, 1] = -np.sin(ang), np.sin(ang)
    cols["rope"] = rot.reshape(2, P, 128).transpose(1, 0, 2).reshape(P, 256)
    at, where = 0, {}
    for n, m in cols.items():
        where[n] = (at, m.shape[1])
        at += m.shape[1]
    return np.ascontiguousarray(np.concatenate(list(cols.values()), axis=1), np.float32), where


def weight_stream():
    order = []
    for l in range(DEPTH):
        order += [("mod", l, j) for j in range(6)]
        order += [("qkv", l, j) for j in range(3)]
        order += [(n, l, 0) for n in ("z", "gqk", "gv", "r", "dq", "dk", "dv")]
        for s in range(3):
            order += [("merge", l, 2 * s), ("merge", l, 2 * s + 1), ("branch", l, s)]
        order += [("out", l, 0), ("out", l, 1)]
        order += [("mod", l, j) for j in range(6, 12)]
        order += [(n, l, e) for e in range(E) for n in ("gate", "up", "down")]
    return order


def program(nc, a, consts, y_prompt, y_sample, new_gdn, new_gla, new_k, new_v):
    order = weight_stream()
    place = {key: n for n, key in enumerate(order)}
    _, cwhere = constants()

    with ExitStack() as ctx:
        def sb(name, width, parts=P):
            return ctx.enter_context(nc.sbuf_tensor(name, [parts, width], F32))

        sems = {}

        def sem(name):
            if name not in sems:
                sems[name] = ctx.enter_context(nc.semaphore(name))
            return sems[name]

        cst = sb("cst", sum(w for _, w in cwhere.values()))
        x = sb("x", T * D)
        xt = sb("xt", KC * TOK)
        ring = sb("ring", RING * CHUNK_W)
        gate = sb("gate", 2 * D)
        modt = sb("modt", 48 * 2)
        brow = sb("brow", 2 * W5)
        crow = sb("crow", P, 16)
        scol = sb("scol", 16)
        router = sb("router", KC * E)
        rbias = sb("rbias", E)
        wsmall = sb("wsmall", DEPTH * KC * 48)
        convrow = sb("convrow", DEPTH * P, 12 * TAPS)
        convc = sb("convc", 12 * TAPS)
        par = sb("par", DEPTH * 656)
        wgate = sb("wgate", DEPTH * W5, 33)
        lrt = sb("lrt", TOK, 33)
        small = sb("small", 1100)
        s_gdn = sb("s_gdn", DIR * W5)
        s_gla = sb("s_gla", 2 * DIR * W5)
        qkvp = sb("qkvp", 12 * 390)
        otok = sb("otok", T * W5)
        shared = sb("shared", 13312)
        late = shared[:, 0:4608]
        proj = shared[:, 4608:10752]
        tail = shared[:, 10752:13312]
        lnp, mtmp = tail[:, 0:2 * D], tail[:, 2 * D:]
        mrow = late[:, T * D:T * D + 2 * W5]
        ckv = tail[:, 0:2 * W5]
        u_gdn = shared[:, 6144:13312]
        u_gla = shared[:, 0:6144]
        u_att = proj

        banks = [ctx.enter_context(nc.psum_tensor(f"bank{b}", [P, W5], F32)) for b in range(8)]
        bank_full = [sem(f"bank{b}_full") for b in range(8)]
        bank_free = [sem(f"bank{b}_free") for b in range(8)]
        slot_in = [sem(f"slot{s}_in") for s in range(RING)]

        def c(name, a0=None, a1=None):
            at, w = cwhere[name]
            return cst[:, at + (a0 or 0):at + (w if a1 is None else a1)]

        def fan(ap, n):
            return ap.unsqueeze(1).broadcast_to([ap.shape[0], n, ap.shape[-1]])

        def wide(ap, w):
            return ap.unsqueeze(2).broadcast_to([ap.shape[0], ap.shape[1], w])

        xv = x[:, :].rearrange("p (t d) -> p t d", t=T)
        xtv = xt[:, :].rearrange("p (k t) -> p k t", k=KC)
        gatev = gate[:, :].rearrange("p (c d) -> p c d", c=2)
        modv = modt[:, :].rearrange("p (j c) -> p j c", c=2)
        qk = qkvp[:, :].rearrange("p (m w) -> p m w", m=12)
        ot = qkvp[:, 0:12 * TOK].rearrange("p (m t) -> p m t", m=12)
        zv = proj[:, 0:T * W5].rearrange("p (t w) -> p t w", t=T)
        rv = proj[:, T * W5:2 * T * W5].rearrange("p (t w) -> p t w", t=T)
        gqkv = proj[:, 2 * T * W5:3 * T * W5].rearrange("p (t w) -> p t w", t=T)
        gvv = proj[:, 3 * T * W5:].rearrange("p (t w) -> p t w", t=T)
        mix = proj[:, 0:T * D].rearrange("p (t d) -> p t d", t=T)
        yacc = proj[:, T * D:].rearrange("p (t d) -> p t d", t=T)
        ktok = late[:, 0:T * W5].rearrange("p (t w) -> p t w", t=T)
        vtok = late[:, T * W5:2 * T * W5].rearrange("p (t w) -> p t w", t=T)
        dqv = late[:, 0:T * W5].rearrange("p (t w) -> p t w", t=T)
        dkv = late[:, T * W5:2 * T * W5].rearrange("p (t w) -> p t w", t=T)
        dvv = late[:, 2 * T * W5:].rearrange("p (t w) -> p t w", t=T)
        mg = late[:, 0:T * D].rearrange("p (t d) -> p t d", t=T)
        ov = otok[:, :].rearrange("p (t w) -> p t w", t=T)
        ring_in = [ring[:, s * CHUNK_W:(s + 1) * CHUNK_W].rearrange("p (k n) -> p k n", k=KC) for s in range(RING)]
        ring_dn = [ring[:, s * CHUNK_W:(s + 1) * CHUNK_W].rearrange("p (m n) -> p m n", m=4) for s in range(RING)]
        smv = wsmall[:, :].rearrange("p (l k n) -> p l k n", l=DEPTH, k=KC)
        rtv = router[:, :].rearrange("p (k e) -> p k e", k=KC)
        ag = late[:, 0:4 * TOK].rearrange("p (m t) -> p m t", m=4)
        hact = late[:, 4 * TOK:8 * TOK].rearrange("p (m t) -> p m t", m=4)

        def col(at, n):
            return small[:, at:at + n]

        BETA, GG, GC, TOTC, EGC, ETOT, ETAIL, BEGC = (24 * n for n in range(8))
        AB, EXPA, LAM, LPROD, SS, RS, NM, SUMP, RP, ST, MV, RTR = 192, 216, 224, 228, 360, 376, 392, 396, 400, 404, 428, 440

        filled = [0] * 8
        fills = {}
        turn = [0]
        chunk_end = {}

        def take(pe, key):
            b = turn[0] % 8
            turn[0] += 1
            if filled[b]:
                pe.wait_ge(bank_free[b], filled[b])
            filled[b] += 1
            fills[key] = (b, filled[b])
            return banks[b], bank_full[b]

        def value(n, e, step):
            return n if e is None else e * step + n

        def full(eng, key, e=None):
            b, n = fills[key]
            eng.wait_ge(bank_full[b], value(n, e, 2))
            return banks[b], bank_free[b]

        def drained(eng, key, e=None):
            b, n = fills[key]
            eng.wait_ge(bank_free[b], value(n, e, 2))

        def arrived(eng, key, e=None):
            n = place[key]
            eng.wait_ge(slot_in[n % RING], value(16 * (n // RING + 1), e, 16))
            return n % RING


        GD = dict(dt=0, a=1, lt=2, m=3, x=4, xt=5, y=6)

        def gd(d, name, h=None):
            at = (d * len(GD) + GD[name]) * W5
            return u_gdn[:, at:at + W5] if h is None else u_gdn[:, at + h * P:at + (h + 1) * P]

        def square(m):
            return u_gdn[:, m % 2 * 388:m % 2 * 388 + CW]

        def conv_out(m):
            return u_gdn[:, 776 + m % 2 * 388:776 + m % 2 * 388 + CW]

        def qnorm(m):
            return u_gdn[:, 1552 + m * CW:1552 + (m + 1) * CW]

        def st_out(d):
            return s_gla[:, d * W5:(d + 1) * W5]

        def glog(t, d):
            return u_gla[:, t * W5 + d * 256:t * W5 + (d + 1) * 256]

        GL = dict(q_in=3, k_in=4, q_dec=5, k_tail=6)

        def gl(name):
            return u_gla[:, GL[name] * W5:(GL[name] + 1) * W5]

        gl_qz, gl_k, gl_dec = u_gla[:, 3584:4608], u_gla[:, 4608:5120], u_gla[:, 5120:5632]
        gl_ln = u_gla[:, 5632:6144]

        def gla_at(d):
            return tail[:, d * W5:(d + 1) * W5]

        def gla_state(p, d):
            at = (min(p, 1) * DIR + d) * W5
            return s_gla[:, at:at + W5]

        def gla_gt(p):
            return col(1030 + 8 * p, 8)

        dk_all = u_att[:, 1024:3072].rearrange("p (h k) -> p h k", h=H)

        def dq_z(s, h):
            return u_att[:, s * W5 + h * P:s * W5 + (h + 1) * P]

        def dp(s):
            return u_att[:, 3584 + s * KEYS:3584 + (s + 1) * KEYS]

        def dw(i):
            return u_att[:, 4352 + i * KEYS:4352 + (i + 1) * KEYS]

        def dwt(i):
            return u_att[:, 5120 + i * KEYS:5120 + (i + 1) * KEYS]

        def level_count(l, p, d, v):
            return ((l * 3 + p) * LEVELS + v) * DIR + d + 1

        def silu(act, l, m):
            act.wait_ge(sem("conv_done"), l * 12 + m + 1)
            act.activation(qk[:, m, 0:CW], conv_out(m), ACT.Silu).then_inc(sem("silu_done"), 1)

        def gate_in(act, name, l, v):
            for t in range(T):
                ps, free = full(act, (name, l, t))
                act.activation(v[:, t, :], ps[:, :], ACT.Silu).then_inc(free, 1)

        def branch_root(act, l, br):
            act.wait_ge(sem("branch_var"), l * 3 + br + 1)
            act.activation(col(SS, 12), col(SS, 12), ACT.Sqrt).then_inc(sem("branch_std"), 1)

        def branch_ot(act, l, br):
            for h in range(H):
                ps, free = full(act, ("ot", l, br, h))
                act.activation(ot[:, br * 4 + h, :], ps[:, 0:TOK], ACT.Copy).then_inc(free, 1)

        block = ctx.enter_context(nc.Block())

        def batch(l, p, d):
            return (l * 3 + p) * 2 + d

        @block.tensor
        def _(pe):
            pe.wait_ge(sem("consts_in"), 16)
            pe.wait_ge(sem("cond_in"), 32)
            ps, ready = take(pe, "cond")
            pe.transpose(ps[:, 0:16], crow[0:16, :], c("ident")[0:16, 0:16]).then_inc(ready, 1)
            drained(pe, "cond")
            scv = scol[:, :].rearrange("p (c k) -> p k c", c=2)

            def tokens_product(key, l, w_of, width=W5, scale_key=None):
                for t in range(T):
                    ps, ready = take(pe, (key, l, t))
                    for k in range(KC):
                        mm = pe.matmul(ps[:, 0:width], xtv[:, k, t * P:(t + 1) * P], w_of(k),
                                       start=(k == 0), stop=(k == KC - 1))
                    mm.then_inc(ready, 1)

            def transpose_x(l, which):
                for k in range(KC):
                    ps, ready = take(pe, ("xt", l, which, k))
                    for t in range(T):
                        if k == 0:
                            n = (l * 2 + which) * T
                            if n:
                                pe.wait_ge(sem("x_ready"), n - T + t + 1)
                            elif t == 0:
                                pe.wait_ge(sem("x_in"), 32)
                        mm = pe.transpose(ps[:, t * P:(t + 1) * P], xv[:, t, k * P:(k + 1) * P], c("ident"))
                    mm.then_inc(ready, 1)
                drained(pe, ("xt", l, which, KC - 1))

            def finish_branch(l, br):
                pe.wait_ge(sem("branch_normed"), l * 3 + br + 1)
                for h in range(H):
                    ps, ready = take(pe, ("ot", l, br, h))
                    for t in range(T):
                        mm = pe.transpose(ps[:, t * P:(t + 1) * P], ov[:, t, h * P:(h + 1) * P], c("ident"))
                    mm.then_inc(ready, 1)

            def modulation(l, first):
                for j in range(first, first + 7):
                    if j < first + 6:
                        ps, ready = take(pe, ("mod", l, j))
                        slot = arrived(pe, ("mod", l, j))
                        for k in range(KC):
                            mm = pe.matmul(ps[0:2, :], scv[:, k, :], ring_in[slot][:, k, :],
                                           start=(k == 0), stop=(k == KC - 1))
                        mm.then_inc(ready, 1)
                        chunk_end["mod", l, j] = ("mod", l, j)
                    if j == first:
                        continue
                    i = j - 1
                    row = mrow[0:2, i % 2 * W5:(i % 2 + 1) * W5]
                    drained(pe, ("mod", l, i))
                    if i // 2 in (2, 5):
                        for cond in range(2):
                            ps, ready = take(pe, ("modg", l, i, cond))
                            pe.matmul(ps[:, :], c("sel", cond * P, (cond + 1) * P)[0:2, :], row,
                                      start=True, stop=True).then_inc(ready, 1)
                    else:
                        ps, ready = take(pe, ("modc", l, i))
                        for b in range(4):
                            mm = pe.transpose(ps[:, 2 * b:2 * b + 2], row[:, b * P:(b + 1) * P],
                                              c("ident")[0:2, 0:2])
                        mm.then_inc(ready, 1)
            for l in range(DEPTH):
                modulation(l, 0)
                pe.wait_ge(sem(f"params{l}_in"), 16 * 7)
                ps, ready = take(pe, ("taps", l))
                pe.transpose(ps[:, 0:60], convrow[:, l * P:(l + 1) * P], c("ident")[0:60, 0:60]).then_inc(ready, 1)
                transpose_x(l, 0)

                for m in range(12):
                    ps, ready = take(pe, ("qkv", l, m))
                    slot = arrived(pe, ("qkv", l, m // 4))
                    for k in range(KC):
                        mm = pe.matmul(ps[:, 0:TOK], ring_in[slot][:, k, m % 4 * P:(m % 4 + 1) * P],
                                       xtv[:, k, :], start=(k == 0), stop=(k == KC - 1))
                    mm.then_inc(ready, 1)
                    chunk_end["qkv", l, m // 4] = ("qkv", l, m)
                ps, ready = take(pe, ("ba", l))
                for t in range(T):
                    for k in range(KC):
                        mm = pe.matmul(ps[:, t * 16:(t + 1) * 16], xtv[:, k, t * P:(t + 1) * P],
                                       smv[:, l, k, 0:16], start=(k == 0), stop=(k == KC - 1))
                mm.then_inc(ready, 1)
                ps, ready = take(pe, ("lr", l))
                for k in range(KC):
                    mm = pe.matmul(ps[0:32, 0:TOK], smv[:, l, k, 16:48], xtv[:, k, :],
                                   start=(k == 0), stop=(k == KC - 1))
                mm.then_inc(ready, 1)
                for name in ("z",):
                    slot = arrived(pe, (name, l, 0))
                    tokens_product(name, l, lambda k: ring_in[slot][:, k, :])
                    chunk_end[name, l, 0] = (name, l, T - 1)

                for m in range(8):
                    ps, ready = take(pe, ("ss", l, m))
                    pe.wait_ge(sem("squares"), l * 8 + m + 1)
                    pe.matmul(ps[:, 0:CW], c("ones"), square(m),
                              start=True, stop=True).then_inc(ready, 1)
                ps, ready = take(pe, ("gc", l))
                pe.wait_ge(sem("log_decay"), l + 1)
                for t in range(T):
                    for d in range(DIR):
                        at = t * 8 + d * 4
                        pe.matmul(ps[:, at:at + 4], c(f"tri{d}"), col(GG + at, 4), start=True, stop=True)
                pe.matmul(ps[:, 32:56], c("ones"), col(GG, 24), start=True, stop=True).then_inc(ready, 1)
                pe.wait_ge(sem("qk_normed"), l + 1)
                for t in range(T):
                    for n, first in (("k", 4), ("v", 8)):
                        ps, ready = take(pe, (n + "tok", l, t))
                        for h in range(H):
                            mm = pe.transpose(ps[:, h * P:(h + 1) * P], qk[:, first + h, COL[t]:COL[t] + P],
                                              c("ident"))
                        mm.then_inc(ready, 1)

                def heads(ps, lhs, rhs, ready):
                    for h in range(H):
                        mm = pe.matmul(ps[:, h * P:(h + 1) * P], lhs(h), rhs(h), start=True, stop=True)
                    mm.then_inc(ready, 1)

                for p, tiles in enumerate(PAIRS):
                    for d, t in enumerate(tiles):
                        n = batch(l, p, d)
                        k_t = lambda h, t=t: qk[:, 4 + h, COL[t]:COL[t] + P]
                        q_t = lambda h, t=t: qk[:, h, COL[t]:COL[t] + P]
                        ps, ready = take(pe, ("gcrow", n))
                        pe.wait_ge(sem("gdn_rows"), n + 1)
                        pe.matmul(ps[:, :], c("ones"), gd(d, "y"), start=True, stop=True).then_inc(ready, 1)
                        ps, ready = take(pe, ("brow", n))
                        pe.matmul(ps[:, :], c("ones"), gd(d, "m"), start=True, stop=True).then_inc(ready, 1)
                        ps, ready = take(pe, ("qk", n))
                        heads(ps, k_t, q_t, ready)
                        ps, ready = take(pe, ("kk", n))
                        heads(ps, k_t, k_t, ready)
                    for d, t in enumerate(tiles):
                        n = batch(l, p, d)
                        ps, ready = take(pe, ("x0", n))
                        pe.wait_ge(sem("inv_start"), n + 1)
                        for h in range(H):
                            mm = pe.transpose(ps[:, h * P:(h + 1) * P], gd(d, "xt", h), c("ident"))
                        mm.then_inc(ready, 1)
                    for v in range(1, LEVELS):
                        for d, t in enumerate(tiles):
                            n = batch(l, p, d)
                            ps, ready = take(pe, ("y", n, v))
                            pe.wait_ge(sem("level_part"), level_count(l, p, d, v))
                            if v == 1:
                                drained(pe, ("x0", n))
                            else:
                                drained(pe, ("xty", n, v - 1))
                            heads(ps, lambda h: gd(d, "m", h), lambda h: gd(d, "x", h), ready)
                        for d, t in enumerate(tiles):
                            n = batch(l, p, d)
                            if v < LEVELS - 1:
                                ps, ready = take(pe, ("xy", n, v))
                                drained(pe, ("y", n, v))
                                heads(ps, lambda h: gd(d, "xt", h), lambda h: gd(d, "y", h), ready)
                            ps, ready = take(pe, ("xty", n, v))
                            if v == LEVELS - 1:
                                drained(pe, ("y", n, v))
                            heads(ps, lambda h: gd(d, "y", h), lambda h: gd(d, "xt", h), ready)
                    for d, t in enumerate(tiles):
                        n = batch(l, p, d)
                        if p:
                            state = lambda h, d=d: s_gdn[:, d * W5 + h * P:d * W5 + (h + 1) * P]
                            ps, ready = take(pe, ("ks", n))
                            if p == 1:
                                pe.wait_ge(sem("gdn_state_in"), 32 * (l + 1))
                            else:
                                drained(pe, ("ds", batch(l, 1, d)))
                            heads(ps, lambda h: qk[:, 4 + h, COL[t]:COL[t] + P], state, ready)
                            ps, ready = take(pe, ("qs", n))
                            heads(ps, lambda h: qk[:, h, COL[t]:COL[t] + P], state, ready)
                    for d, t in enumerate(tiles):
                        n = batch(l, p, d)
                        ps, ready = take(pe, ("vnew", n))
                        pe.wait_ge(sem("gdn_rhs"), n + 1)
                        drained(pe, ("xty", n, LEVELS - 1))
                        heads(ps, lambda h: gd(d, "xt", h), lambda h: gd(d, "y", h), ready)
                    for d, t in enumerate(tiles):
                        n = batch(l, p, d)
                        ps, ready = take(pe, ("av", n))
                        drained(pe, ("vnew", n))
                        heads(ps, lambda h: gd(d, "a", h), lambda h: gd(d, "x", h), ready)
                        if p < 2:
                            ps, ready = take(pe, ("ds", n))
                            heads(ps, lambda h: ktok[:, t, h * P:(h + 1) * P], lambda h: gd(d, "m", h), ready)
                finish_branch(l, 0)

                for name in ("gqk", "gv", "r"):
                    slot = arrived(pe, (name, l, 0))
                    tokens_product(name, l, lambda k: ring_in[slot][:, k, :])
                    chunk_end[name, l, 0] = (name, l, T - 1)
                for t in range(T):
                    ps, ready = take(pe, ("glog", l, t))
                    if t == 0:
                        drained(pe, ("lr", l))
                        pe.wait_ge(sem("fixed_set"), 1)
                    pe.matmul(ps[:, :], lrt[0:33, t * P:(t + 1) * P], wgate[0:33, l * W5:(l + 1) * W5],
                              start=True, stop=True).then_inc(ready, 1)
                for p, tiles in enumerate(PAIRS):
                    for name in ("rel", "sum", "tail"):
                        ps, ready = take(pe, ("gla_" + name, l, p))
                        if name == "rel" and p == 0:
                            drained(pe, ("glog", l, T - 1))
                        for d, t in enumerate(tiles):
                            mm = pe.matmul(ps[:, d * 256:(d + 1) * 256], c(f"{name}{d}"), glog(t, d),
                                           start=True, stop=True)
                        mm.then_inc(ready, 1)
                    ps, ready = take(pe, ("gla_gt", l, p))
                    for d, t in enumerate(tiles):
                        for hp in range(2):
                            at = (d * 2 + hp) * 2
                            mm = pe.matmul(ps[:, at:at + 2], glog(t, d)[:, hp * P:(hp + 1) * P], c("chunks"),
                                           start=True, stop=True)
                    mm.then_inc(ready, 1)
                    for i, name in enumerate(("q_in", "k_in", "q_dec")):
                        ps, ready = take(pe, (name, l, p))
                        pe.wait_ge(sem("gla_decayed"), (l * 3 + p) * 4 + i + 1)
                        for d in range(DIR):
                            for hp in range(2):
                                at = (d * 2 + hp) * P
                                mm = pe.transpose(ps[:, at:at + P], gl(name)[:, at:at + P], c("ident"))
                        mm.then_inc(ready, 1)
                    for d, t in enumerate(tiles):
                        ps, ready = take(pe, ("gla_a", l, p, d))
                        if d == 0:
                            drained(pe, ("q_in", l, p))
                            drained(pe, ("k_in", l, p))
                        for h in range(H):
                            hp, par_ = h // 2, h % 2
                            mm = pe.matmul(ps[:, h * P:(h + 1) * P], gl_k[:, (d * 2 + hp) * P:(d * 2 + hp + 1) * P], gl_qz[:, par_ * W5 + (d * 2 + hp) * P:par_ * W5 + (d * 2 + hp + 1) * P],
                                           start=True, stop=True)
                        mm.then_inc(ready, 1)
                    for d, t in enumerate(tiles):
                        ps, ready = take(pe, ("gla_av", l, p, d))
                        drained(pe, ("gla_a", l, p, d))
                        for h in range(H):
                            mm = pe.matmul(ps[:, h * P:(h + 1) * P], gla_at(d)[:, h * P:(h + 1) * P],
                                           gvv[:, t, h * P:(h + 1) * P], start=True, stop=True)
                        mm.then_inc(ready, 1)
                    for step in range(2):
                        for d, t in enumerate(tiles):
                            ch = step if d == 0 else 1 - step
                            tok = slice(ch * HALF, (ch + 1) * HALF)
                            ps, ready = take(pe, ("gla_inter", l, p, d, step))
                            if step == 0 and d == 0:
                                drained(pe, ("q_dec", l, p))
                            if step == 1:
                                drained(pe, ("gla_ds", l, p, d, 0))
                            elif p == 1 and d == 0:
                                pe.wait_ge(sem("gla_state_in"), 64 * (l + 1))
                            elif p == 2:
                                drained(pe, ("gla_ds", l, 1, d, 1))
                            elif d == 0:
                                pe.wait_ge(sem("gla_zeroed"), l + 1)
                            for hp in range(2):
                                at = (d * 2 + hp) * P
                                mm = pe.matmul(ps[tok, hp * 256:(hp + 1) * 256], gl_dec[:, at + ch * HALF:at + (ch + 1) * HALF],
                                               gla_state(p, d)[:, hp * 256:(hp + 1) * 256], start=True, stop=True)
                            mm.then_inc(ready, 1)
                            if p == 2 and step == 1:
                                continue
                            ps, ready = take(pe, ("gla_ds", l, p, d, step))
                            if step == 0 and d == 0:
                                pe.wait_ge(sem("gla_decayed"), (l * 3 + p) * 4 + 4)
                            for hp in range(2):
                                at = (d * 2 + hp) * P
                                mm = pe.matmul(ps[:, hp * 256:(hp + 1) * 256], gl("k_tail")[tok, at:at + P],
                                               gvv[tok, t, hp * 256:(hp + 1) * 256], start=True, stop=True)
                            mm.then_inc(ready, 1)
                finish_branch(l, 1)

                for name in ("dq", "dk", "dv"):
                    slot = arrived(pe, (name, l, 0))
                    tokens_product(name, l, lambda k: ring_in[slot][:, k, :])
                    chunk_end[name, l, 0] = (name, l, T - 1)
                for t in range(T + 1):
                    ps, ready = take(pe, ("kt", l, t))
                    if t == T:
                        pe.wait_ge(sem("cache_in"), 32 * (l + 1))
                    elif t:
                        pe.wait_ge(sem("roped"), (l * 2 + t - 1) * 2 + 2)
                    else:
                        drained(pe, ("dk", l, 0))
                    for h in range(H):
                        src = ckv[:, h * P:(h + 1) * P] if t == T else dkv[:, t, h * P:(h + 1) * P]
                        mm = pe.transpose(ps[:, h * P:(h + 1) * P], src, c("ident"))
                    mm.then_inc(ready, 1)
                for t in range(T):
                    ps, ready = take(pe, ("qt", l, t))
                    if t == 0:
                        drained(pe, ("dq", l, 0))
                    for h in range(H):
                        mm = pe.transpose(ps[:, h * P:(h + 1) * P], dqv[:, t, h * P:(h + 1) * P], c("ident"))
                    mm.then_inc(ready, 1)
                    lo, hi = (0, P) if t == 0 else (P, P + KEYS)
                    tiles_k = [0] if t == 0 else [1, 2, 3]
                    for hh in range(H + 1):
                        if hh < H:
                            for s in range(2):
                                ps, ready = take(pe, ("sc", l, t, hh, s))
                                if hh == 0 and s == 0:
                                    drained(pe, ("qt", l, t))
                                    drained(pe, ("kt", l, T))
                                pe.matmul(ps[:, 0:hi - lo], dq_z(s, hh), dk_all[:, hh, :][:, lo:hi],
                                          start=True, stop=True).then_inc(ready, 1)
                        if hh == 0:
                            continue
                        h = hh - 1
                        n = (l * T + t) * H + h
                        ps, ready = take(pe, ("wt", l, t, h))
                        pe.wait_ge(sem("attn_weights"), n + 1)
                        for i in range(len(tiles_k)):
                            mm = pe.transpose(ps[:, i * P:(i + 1) * P], dw(n % 2)[:, i * P:(i + 1) * P], c("ident"))
                        mm.then_inc(ready, 1)
                        ps, ready = take(pe, ("att", l, t, h))
                        drained(pe, ("wt", l, t, h))
                        for i, kt in enumerate(tiles_k):
                            val = ckv[:, W5 + h * P:W5 + (h + 1) * P] if kt == 3 else dvv[:, kt, h * P:(h + 1) * P]
                            mm = pe.matmul(ps[:, 0:P], dwt(n % 2)[:, i * P:(i + 1) * P], val,
                                           start=(i == 0), stop=(i == len(tiles_k) - 1))
                        mm.then_inc(ready, 1)
                finish_branch(l, 2)

                for s in range(3):
                    for half in range(2):
                        slot = arrived(pe, ("merge", l, 2 * s + half))
                        tokens_product(("mergel", 2 * s + half), l, lambda k: ring_in[slot][:, k, :])
                        chunk_end["merge", l, 2 * s + half] = (("mergel", 2 * s + half), l, T - 1)
                    slot = arrived(pe, ("branch", l, s))
                    drained(pe, ("ot", l, s, H - 1))
                    for t in range(T):
                        for half in range(2):
                            ps, ready = take(pe, ("branch", l, s, t, half))
                            for h in range(H):
                                mm = pe.matmul(ps[:, :], ot[:, s * 4 + h, t * P:(t + 1) * P],
                                               ring_dn[slot][:, h, half * W5:(half + 1) * W5],
                                               start=(h == 0), stop=(h == H - 1))
                            mm.then_inc(ready, 1)
                    chunk_end["branch", l, s] = ("branch", l, s, T - 1, 1)
                for k in range(KC):
                    ps, ready = take(pe, ("mixt", l, k))
                    if k == 0:
                        drained(pe, ("branch", l, 2, T - 1, 1))
                        pe.wait_ge(sem("mixed"), l + 1)
                    for t in range(T):
                        mm = pe.transpose(ps[:, t * P:(t + 1) * P], mix[:, t, k * P:(k + 1) * P], c("ident"))
                    mm.then_inc(ready, 1)
                drained(pe, ("mixt", l, KC - 1))
                for half in range(2):
                    slot = arrived(pe, ("out", l, half))
                    tokens_product(("outl", half), l, lambda k: ring_in[slot][:, k, :])
                    chunk_end["out", l, half] = (("outl", half), l, T - 1)

                modulation(l, 6)

                transpose_x(l, 1)
                ps, ready = take(pe, ("router", l))
                pe.wait_ge(sem("router_in"), 32)
                for t in range(T):
                    for k in range(KC):
                        mm = pe.matmul(ps[:, t * E:(t + 1) * E], xtv[:, k, t * P:(t + 1) * P], rtv[:, k, :],
                                       start=(k == 0), stop=(k == KC - 1))
                mm.then_inc(ready, 1)

                base = list(filled)
                names = [("gatep", l, m) for m in range(4)] + [("upp", l, m) for m in range(4)]
                names += [("downp", l, t, half) for t in range(T) for half in range(2)]
                for i, key in enumerate(names):
                    b = i % LOOP_BANKS
                    fills[key] = (b, base[b] + i // LOOP_BANKS + 1)
                for name, last in (("gate", names[3]), ("up", names[7]), ("down", names[13])):
                    chunk_end[name, l, 0] = last
                with pe.Fori(0, E) as e:
                    def open_bank(key):
                        b, n = fills[key]
                        pe.wait_ge(bank_free[b], e * 2 + (n - 1))
                        return banks[b], bank_full[b]

                    for name, fill in (("gate", "gatep"), ("up", "upp")):
                        slot = arrived(pe, (name, l, 0), e)
                        for m in range(4):
                            ps, ready = open_bank((fill, l, m))
                            for k in range(KC):
                                mm = pe.matmul(ps[:, 0:TOK], ring_in[slot][:, k, m * P:(m + 1) * P], xtv[:, k, :],
                                               start=(k == 0), stop=(k == KC - 1))
                            mm.then_inc(ready, 1)
                    slot = arrived(pe, ("down", l, 0), e)
                    for m in range(4):
                        drained(pe, ("upp", l, m), e)
                    for t in range(T):
                        for half in range(2):
                            ps, ready = open_bank(("downp", l, t, half))
                            for m in range(4):
                                mm = pe.matmul(ps[:, :], hact[:, m, t * P:(t + 1) * P],
                                               ring_dn[slot][:, m, half * W5:(half + 1) * W5],
                                               start=(m == 0), stop=(m == 3))
                            mm.then_inc(ready, 1)
                for b in range(LOOP_BANKS):
                    filled[b] += 2 * E
                turn[0] = 0

        @block.sync
        def _(sp):
            sp.dma_start(cst[:, :], consts).then_inc(sem("consts_in"), 16)
            sp.dma_start(crow[0:8, :], a["c_ctx"].rearrange("(k p) -> k p", p=P)).then_inc(sem("cond_in"), 16)
            sp.dma_start(crow[8:16, :], a["c"].rearrange("b (k p) -> (b k) p", p=P)).then_inc(sem("cond_in"), 16)
            sp.dma_start(xv[:, 0, :], a["x_prompt"][0]).then_inc(sem("x_in"), 16)
            sp.dma_start(xv[:, 1:3, :], a["x_sample"][0].rearrange("(t p) d -> p t d", p=P)).then_inc(sem("x_in"), 16)

            rows = lambda w: w.rearrange("(k p) n -> p k n", p=P)
            source = {
                "mod": lambda l, j: rows(a["w_mod"][l])[:, :, j * W5:(j + 1) * W5],
                "qkv": lambda l, j: rows(a["w_in"][l])[:, :, j * W5:(j + 1) * W5],
                "merge": lambda l, j: rows(a["w_in"][l])[:, :, IN_COL["merge"] + j * W5:IN_COL["merge"] + (j + 1) * W5],
                "out": lambda l, j: rows(a["w_out"][l])[:, :, j * W5:(j + 1) * W5],
                "branch": lambda l, s: a["w_branch"][l, s].rearrange("(m p) n -> p m n", p=P),
                "gate": lambda l, e: rows(a["exp_w_gate"][l, e]),
                "up": lambda l, e: rows(a["exp_w_up"][l, e]),
                "down": lambda l, e: a["exp_w_down"][l, e].rearrange("(m p) n -> p m n", p=P),
            }
            for name in ("gqk", "gv", "z", "r", "dq", "dk", "dv"):
                source[name] = lambda l, j, name=name: rows(a["w_in"][l])[:, :, IN_COL[name]:IN_COL[name] + W5]

            def load(key, e=None):
                name, l, j = key
                slot = place[key] % RING
                dst = (ring_dn if name in ("branch", "down") else ring_in)[slot]
                sp.dma_start(dst, source[name](l, j if e is None else e)).then_inc(slot_in[slot], 16)

            def reusable(key):
                n = place[key] - RING
                if n < 0:
                    return
                name, l, j = order[n]
                if name in ("gate", "up", "down"):
                    b, first = fills[chunk_end[name, l, 0]]
                    sp.wait_ge(bank_full[b], first + 2 * (E - 1))
                else:
                    full(sp, chunk_end[order[n]])

            for l in range(DEPTH):
                for key in order[place["mod", l, 0]:place["gate", l, 0]]:
                    if key[0] == "mod":
                        j = key[2]
                        if l or j > 1:
                            drained(sp, ("mod", l, j - 2) if j > 1 else ("mod", l - 1, 10 + j))
                        sp.dma_start(brow[0:2, j % 2 * W5:(j % 2 + 1) * W5],
                                     a["b_mod"][l, j * W5:(j + 1) * W5].partition_broadcast(2))\
                            .then_inc(sem(f"bias_row{j % 2}_in"), 16)
                    reusable(key)
                    load(key)
                for name in ("gate", "up", "down"):
                    reusable((name, l, 0))
                    load((name, l, 0))
                with sp.Fori(0, E - 1) as e:
                    for name in ("gate", "up", "down"):
                        full(sp, chunk_end[name, l, 0], e)
                        load((name, l, 0), e + 1)

        @block.gpsimd
        def _(pool):
            steps = [0]

            def link(ins):
                steps[0] += 1
                ins.then_inc(sem("pool_steps"), 1)
                pool.wait_ge(sem("pool_steps"), steps[0])

            for l in range(DEPTH):
                pin = sem(f"params{l}_in")
                pool.dma_start(smv[:, l, :, 0:16], a["w_in"][l, :, IN_COL["ba"]:IN_COL["ba"] + 16].rearrange("(k p) n -> p k n", p=P)).then_inc(pin, 16)
                pool.dma_start(smv[:, l, :, 16:48], a["w_in"][l, :, IN_COL["lr"]:IN_COL["lr"] + 32].rearrange("(k p) n -> p k n", p=P)).then_inc(pin, 16)
                pool.dma_start(convrow[:, l * P:(l + 1) * P], a["gdn_conv"][l].rearrange("k (c p) -> (k c) p", p=P)).then_inc(pin, 16)
                at = l * 656
                for name, w in (("gdn_a_log", 8), ("gdn_dt_bias", 8)):
                    pool.dma_start(par[:, at:at + w], a[name][l].rearrange("d h -> (d h)").partition_broadcast(P)).then_inc(pin, 16)
                    at += w
                at = l * 656 + 16 + 384
                pool.dma_start(par[:, at:at + 256], a["diff_lambda"][l].rearrange("s d -> (s d)").partition_broadcast(P)).then_inc(pin, 16)
                pool.dma_start(wgate[32:33, l * W5:(l + 1) * W5], a["gla_b_gate"][l].rearrange("(o d) k -> o (d k)", o=1)).then_inc(pin, 16)
                at = l * 656 + 16
                for name in ("gdn_norm", "gla_norm", "diff_norm"):
                    pool.dma_start(par[:, at:at + 128], a[name][l].partition_broadcast(P)).then_inc(sem("norms_in"), 16)
                    at += 128
            pool.dma_start(rtv, a["router_w"].rearrange("(k p) e -> p k e", p=P)).then_inc(sem("router_in"), 16)
            pool.dma_start(rbias[:, :], a["router_b"].partition_broadcast(P)).then_inc(sem("router_in"), 16)
            link(pool.memset(wgate[0:32, :], 0.0))
            for l in range(DEPTH):
                for d in range(DIR):
                    pool.dma_start(wgate[d * RANK:(d + 1) * RANK, l * W5 + d * 256:l * W5 + (d + 1) * 256],
                                   a["gla_w_gate"][l, d]).then_inc(sem("gate_w_in"), 16)
            link(pool.memset(lrt[32:33, :], 1.0))
            link(pool.memset(s_gla[:, :], 0.0))
            pool.wait_ge(sem("gate_w_in"), 64)
            link(pool.memset(small[:, 1000:1001], 0.0))
            pool.memset(small[:, 1001:1002], 0.0).then_inc(sem("fixed_set"), 1)
            for l in range(DEPTH):
                if l:
                    pool.wait_ge(sem("mixed"), l)
                for at in (0, 130, 388):
                    ins = pool.memset(qk[:, :, at:at + 2], 0.0)
                    if at == 388:
                        ins.then_inc(sem("pads"), 1)
                def ln_params(which):
                    if which:
                        pool.wait_ge(sem("x_ready"), (l * 2 + which) * T)
                    else:
                        pool.wait_ge(sem("branch_normed"), l * 3 + 3)
                    for i, name in enumerate(("ln_g", "ln_b")):
                        pool.dma_start(lnp[:, i * D:(i + 1) * D], a[name][l, which].partition_broadcast(P)).then_inc(sem("ln_in"), 16)
                for m in range(8):
                    pool.wait_ge(sem("silu_done"), l * 12 + m + 1)
                    if m == 0:
                        pool.wait_ge(sem("silu_done"), l * 12 + 12)
                    if m > 1:
                        full(pool, ("ss", l, m - 2))
                    pool.tensor_tensor(square(m), qk[:, m, 0:CW], qk[:, m, 0:CW], ALU.mult)\
                        .then_inc(sem("squares"), 1)
                def scale_gate(i):
                    name, v, at = (("z", zv, 16), ("r", rv, 144))[i]
                    if i == 0 and l == 0:
                        pool.wait_ge(sem("norms_in"), 16 * 3 * DEPTH)
                    drained(pool, (name, l, T - 1))
                    vv = v.rearrange("p t (h w) -> p (t h) w", h=H)
                    pool.tensor_tensor(vv, vv, fan(par[:, l * 656 + at:l * 656 + at + P], T * H), ALU.mult)\
                        .then_inc(sem("gates_scaled"), 1)
                scale_gate(0)
                if l:
                    for d in range(DIR):
                        full(pool, ("qs", batch(l - 1, 2, d)))
                for d in range(DIR):
                    pool.dma_start(s_gdn[:, d * W5:(d + 1) * W5].rearrange("p (h e) -> p h e", h=H),
                                   a["state_gdn"][0, l, d].rearrange("h d e -> d h e")).then_inc(sem("gdn_state_in"), 16)
                for p, tiles in enumerate(PAIRS):
                    for d, t in enumerate(tiles):
                        n = batch(l, p, d)
                        if p == 0 and d == 0:
                            pool.wait_ge(sem("log_decay"), l + 1)
                            pool.wait_ge(sem("qk_normed"), l + 1)
                        if p:
                            m = batch(l, p - 1, d)
                            full(pool, ("av", m))
                            full(pool, ("ds", m))
                            full(pool, ("vnew", m))
                        pool.tensor_tensor(gd(d, "y").rearrange("p (h i) -> p h i", h=H), fan(c(f"tri{d}"), H),
                                           wide(col(GG + t * 8 + d * 4, 4), P), ALU.mult)
                        pool.tensor_tensor(gd(d, "m").rearrange("p (h i) -> p h i", h=H), fan(c("ident"), H),
                                           wide(col(BETA + t * 8 + d * 4, 4), P), ALU.mult).then_inc(sem("gdn_rows"), 1)
                    for v in range(LEVELS):
                        for d, t in enumerate(tiles):
                            n = batch(l, p, d)
                            if v == 0:
                                drained(pool, ("brow", n))
                            elif v > 1:
                                full(pool, ("y", n, v - 1))
                            else:
                                pool.wait_ge(sem("inv_start"), n + 1)
                            pool.tensor_tensor(gd(d, "m").rearrange("p (h i) -> p h i", h=H),
                                               gd(d, "lt").rearrange("p (h i) -> p h i", h=H),
                                               fan(c(f"level{d}_{v}"), H), ALU.mult).then_inc(sem("level_part"), 1)
                for d in range(DIR):
                    drained(pool, ("ds", batch(l, 0, d)))
                    pool.dma_start(new_gdn[0, l, d].rearrange("h d e -> d h e"),
                                   st_out(d).rearrange("p (h e) -> p h e", h=H)).then_inc(sem("outputs"), 16)
                for d in range(DIR):
                    for hh in range(2):
                        if l:
                            full(pool, ("gla_inter", l - 1, 2, d, 1))
                        rows_ = slice(hh * 64, hh * 64 + 64)
                        pool.dma_start(gla_state(1, d)[rows_, :].rearrange("p (a b e) -> p a b e", a=2, b=2)[:, :, hh, :],
                                       a["state_gla"][0, l, d].rearrange("(a b) k e -> b k a e", b=2)[hh])\
                            .then_inc(sem("gla_state_in"), 16)
                pool.wait_ge(sem("outputs"), 32 * (l + 1))
                pool.wait_ge(sem("branch_normed"), l * 3 + 1)
                link(pool.memset(gla_at(0), 0.0))
                link(pool.memset(gla_at(1), 0.0))
                link(pool.memset(gl_qz, 0.0))
                pool.memset(s_gla[:, 0:2 * W5], 0.0).then_inc(sem("gla_zeroed"), 1)
                scale_gate(1)
                for d in range(DIR):
                    drained(pool, ("gla_ds", l, 0, d, 1))
                    for hh in range(2):
                        rows_ = slice(hh * 64, hh * 64 + 64)
                        pool.dma_start(new_gla[0, l, d].rearrange("(a b) k e -> b k a e", b=2)[hh],
                                       gla_state(0, d)[rows_, :].rearrange("p (a b e) -> p a b e", a=2, b=2)[:, :, hh, :])\
                            .then_inc(sem("gla_out"), 16)
                pool.wait_ge(sem("branch_normed"), l * 3 + 2)
                pool.memset(u_att[:, 0:2 * W5], 0.0).then_inc(sem("dq_zeroed"), 1)
                pool.dma_start(ckv[:, 0:W5], a["cache_k"][0, l].rearrange("s h d -> s (h d)")).then_inc(sem("cache_in"), 16)
                pool.dma_start(ckv[:, W5:], a["cache_v"][0, l].rearrange("s h d -> s (h d)")).then_inc(sem("cache_in"), 16)
                for name, v, dst in (("dk", dkv, new_k), ("dv", dvv, new_v)):
                    drained(pool, (name, l, 0))
                    pool.dma_start(dst[0, l].rearrange("s h d -> s (h d)"), v[:, 0, :]).then_inc(sem("kv_out"), 16)
                ln_params(0)
                ln_params(1)
            pool.wait_ge(sem("x_ready"), DEPTH * 2 * T)
            pool.dma_start(y_prompt[0], xv[:, 0, :]).then_inc(sem("outputs"), 16)
            pool.dma_start(y_sample[0].rearrange("(t p) d -> p t d", p=P), xv[:, 1:3, :]).then_inc(sem("outputs"), 16)
            pool.wait_ge(sem("outputs"), 16 * (2 * DEPTH + 2))
            pool.wait_ge(sem("kv_out"), 32 * DEPTH)
            pool.wait_ge(sem("gla_out"), 64 * DEPTH)

        @block.scalar
        def _(act):
            steps = [0]

            def link(ins):
                steps[0] += 1
                ins.then_inc(sem("act_steps"), 1)
                act.wait_ge(sem("act_steps"), steps[0])

            def root(at, n, name, k):
                act.wait_ge(sem(name + "_var"), k)
                act.activation(col(at, n), col(at, n), ACT.Sqrt).then_inc(sem(name + "_std"), 1)

            def gates_out(l, which):
                n = (l * 2 + which) * T
                if n:
                    act.wait_ge(sem("x_ready"), n)
                for i in (4 + 6 * which, 5 + 6 * which):
                    for cond in range(2):
                        ps, free = full(act, ("modg", l, i, cond))
                        act.activation(gatev[:, cond, i % 2 * W5:(i % 2 + 1) * W5], ps[:, :], ACT.Copy).then_inc(free, 1)

            ps, free = full(act, "cond")
            act.activation(scol[:, :], ps[:, 0:16], ACT.Silu).then_inc(free, 1)
            for l in range(DEPTH):
                gates_out(l, 0)
                for m in range(12):
                    ps, free = full(act, ("qkv", l, m))
                    if m == 0:
                        if l:
                            act.wait_ge(sem("mixed"), l)
                        act.wait_ge(sem("pads"), l + 1)
                    act.activation(qk[:, m, 2:2 + SEQ], ps[:, 0:SEQ], ACT.Copy)
                    act.activation(qk[:, m, 4 + SEQ:4 + TOK], ps[:, SEQ:TOK], ACT.Copy).then_inc(free, 1)
                    if m > 1:
                        silu(act, l, m - 2)
                silu(act, l, 10)
                silu(act, l, 11)
                ps, free = full(act, ("ba", l))
                bav = ps[:, 0:48].rearrange("p (t c) -> p t c", t=T)
                act.activation(col(BETA, 24).rearrange("p (t c) -> p t c", t=T), bav[:, :, 0:8], ACT.Sigmoid)
                act.activation(col(AB, 24).rearrange("p (t c) -> p t c", t=T), bav[:, :, 8:16], ACT.Copy).then_inc(free, 1)
                ps, free = full(act, ("lr", l))
                act.activation(lrt[0:32, :], ps[0:32, 0:TOK], ACT.Copy).then_inc(free, 1)
                gate_in(act, "z", l, zv)
                act.wait_ge(sem("decay_in"), l + 1)
                link(act.activation(col(GC, 24), col(AB, 24), ACT.Abs))
                link(act.activation(col(GC, 24), col(GC, 24), ACT.Exp, scale=-1.0))
                link(act.activation(col(GC, 24), col(GC, 24), ACT.Ln, bias=1.0))
                act.activation(col(EXPA, 8), par[:, l * 656:l * 656 + 8], ACT.Exp).then_inc(sem("softplus_part"), 1)
                for m in range(8):
                    ps, free = full(act, ("ss", l, m))
                    if m == 0:
                        act.wait_ge(sem("eps_set"), 1)
                    act.activation(qnorm(m), ps[:, 0:CW], ACT.Sqrt, bias=col(1010, 1)).then_inc(free, 1)
                act.wait_ge(sem("decay_sums"), l + 1)
                act.activation(col(EGC, 24), col(GC, 24), ACT.Exp)
                act.activation(col(ETOT, 24), col(TOTC, 24), ACT.Exp)
                act.activation(col(ETAIL, 24), col(ETAIL, 24), ACT.Exp).then_inc(sem("decays"), 1)
                for t in range(T):
                    for n, v in (("k", ktok), ("v", vtok)):
                        ps, free = full(act, (n + "tok", l, t))
                        act.activation(v[:, t, :], ps[:, :], ACT.Copy).then_inc(free, 1)
                for p, tiles in enumerate(PAIRS):
                    for d in range(DIR):
                        n = batch(l, p, d)
                        drained(act, ("gcrow", n))
                        act.activation(gd(d, "dt"), gd(d, "dt"), ACT.Exp).then_inc(sem("dt_exp"), 1)
                    for d in range(DIR):
                        ps, free = full(act, ("x0", batch(l, p, d)))
                        act.activation(gd(d, "x"), ps[:, :], ACT.Copy).then_inc(free, 1)
                    for v in range(1, LEVELS):
                        for d in range(DIR):
                            ps, free = full(act, ("y", batch(l, p, d), v))
                            act.activation(gd(d, "y"), ps[:, :], ACT.Copy).then_inc(free, 1)
                branch_root(act, l, 0)
                branch_ot(act, l, 0)
                for t in range(T):
                    ps, free = full(act, ("gqk", l, t))
                    act.activation(gqkv[:, t, 0:256], ps[:, 0:256], ACT.Copy, scale=GLA_DK ** -0.5)
                    act.activation(gqkv[:, t, 256:512], ps[:, 256:512], ACT.Copy).then_inc(free, 1)
                for t in range(T):
                    ps, free = full(act, ("gv", l, t))
                    act.activation(gvv[:, t, :], ps[:, :], ACT.Copy).then_inc(free, 1)
                gate_in(act, "r", l, rv)
                for t in range(T):
                    ps, _ = full(act, ("glog", l, t))
                    if t:
                        drained(act, ("glog", l, t - 1))
                    else:
                        act.wait_ge(sem("branch_normed"), l * 3 + 1)
                    link(act.activation(gl_ln, ps[:, :], ACT.Abs))
                    link(act.activation(gl_ln, gl_ln, ACT.Exp, scale=-1.0))
                    act.activation(gl_ln, gl_ln, ACT.Ln, bias=1.0).then_inc(sem("gla_ln"), 1)
                for p in range(3):
                    if p:
                        full(act, ("q_dec", l, p - 1))
                        full(act, ("gla_ds", l, p - 1, 1, 1))
                    ps, free = full(act, ("gla_rel", l, p))
                    act.activation(gl("q_in"), ps[:, :], ACT.Exp, scale=1.0 / TAU)
                    act.activation(gl("k_in"), ps[:, :], ACT.Exp, scale=-1.0 / TAU).then_inc(free, 1)
                    ps, free = full(act, ("gla_sum", l, p))
                    act.activation(gl("q_dec"), ps[:, :], ACT.Exp, scale=1.0 / TAU).then_inc(free, 1)
                    ps, free = full(act, ("gla_tail", l, p))
                    act.activation(gl("k_tail"), ps[:, :], ACT.Exp, scale=1.0 / TAU).then_inc(free, 1)
                    ps, free = full(act, ("gla_gt", l, p))
                    act.activation(gla_gt(p), ps[:, 0:8], ACT.Exp, scale=1.0 / TAU).then_inc(free, 1)
                    ps, free = full(act, ("q_in", l, p))
                    if p == 0:
                        act.wait_ge(sem("gla_zeroed"), l + 1)
                    for hh in range(2):
                        ins = act.activation(gl_qz[hh * 64:hh * 64 + 64, hh * W5:(hh + 1) * W5], ps[hh * 64:hh * 64 + 64, :], ACT.Copy)
                    ins.then_inc(free, 1)
                    ps, free = full(act, ("k_in", l, p))
                    act.activation(gl_k, ps[:, :], ACT.Copy).then_inc(free, 1)
                    ps, free = full(act, ("q_dec", l, p))
                    act.activation(gl_dec, ps[:, :], ACT.Copy).then_inc(free, 1)
                branch_root(act, l, 1)
                branch_ot(act, l, 1)
                for name, v in (("dq", dqv), ("dk", dkv), ("dv", dvv)):
                    for t in range(T):
                        ps, free = full(act, (name, l, t))
                        act.activation(v[:, t, :], ps[:, :], ACT.Copy).then_inc(free, 1)
                act.wait_ge(sem("lam_parts"), l + 1)
                act.activation(col(LAM, 2), col(LAM, 2), ACT.Exp).then_inc(sem("lam_exp"), 1)
                for t in range(T + 1):
                    ps, free = full(act, ("kt", l, t))
                    act.activation(dk_all[:, :, t * P:(t + 1) * P], ps[:, :].rearrange("p (h i) -> p h i", h=H), ACT.Copy).then_inc(free, 1)
                for t in range(T):
                    ps, free = full(act, ("qt", l, t))
                    if t == 0:
                        act.wait_ge(sem("dq_zeroed"), l + 1)
                    else:
                        full(act, ("sc", l, t - 1, H - 1, 1))
                    for s in range(2):
                        ins = act.activation(u_att[s * 64:s * 64 + 64, s * W5:(s + 1) * W5], ps[s * 64:s * 64 + 64, :], ACT.Copy)
                    ins.then_inc(free, 1)
                    nk = P if t == 0 else KEYS
                    for hh in range(H + 1):
                        if hh < H:
                            n = (l * T + t) * H + hh
                            for s in range(2):
                                ps, free = full(act, ("sc", l, t, hh, s))
                                act.wait_ge(sem("neg_max"), 2 * n + s + 1)
                                act.activation(dp(s)[:, 0:nk], ps[:, 0:nk], ACT.Exp, bias=col(NM + s, 1), scale=DH ** -0.5,
                                               accum_out=col(SUMP + s, 1)).then_inc(free, 1)
                        if hh:
                            n = (l * T + t) * H + hh - 1
                            ps, free = full(act, ("wt", l, t, hh - 1))
                            if n > 1:
                                m = n - 2
                                full(act, ("att", m // (T * H), m // H % T, m % H))
                            act.activation(dwt(n % 2)[:, 0:nk], ps[:, 0:nk], ACT.Copy).then_inc(free, 1)
                branch_root(act, l, 2)
                branch_ot(act, l, 2)
                for s in range(3):
                    for half in range(2):
                        for t in range(T):
                            ps, free = full(act, (("mergel", 2 * s + half), l, t))
                            if s == half == t == 0:
                                act.wait_ge(sem("kv_out"), 32 * (l + 1))
                            if s and half == 0 and t == 0:
                                drained(act, ("branch", l, s - 1, T - 1, 1))
                            act.activation(mg[:, t, half * W5:(half + 1) * W5], ps[:, :], ACT.Sigmoid).then_inc(free, 1)
                for k in range(KC):
                    ps, free = full(act, ("mixt", l, k))
                    act.activation(xtv[:, k, :], ps[:, 0:TOK], ACT.Copy).then_inc(free, 1)
                root(RS, T, "ln", l * 2 + 1)
                gates_out(l, 1)
                ps, free = full(act, ("router", l))
                act.activation(col(RTR, 48), ps[:, 0:48], ACT.Sigmoid).then_inc(free, 1)
                with act.Fori(0, E) as e:
                    for m in range(4):
                        ps, free = full(act, ("gatep", l, m), e)
                        act.activation(ag[:, m, :], ps[:, 0:TOK], ACT.Silu).then_inc(free, 1)
                root(RS, T, "ln", l * 2 + 2)

        @block.vector
        def _(dve):
            steps = [0]

            def link(ins):
                steps[0] += 1
                ins.then_inc(sem("dve_steps"), 1)
                dve.wait_ge(sem("dve_steps"), steps[0])

            def layer_norm(l, which):
                n = l * 2 + which
                for t in range(T):
                    for half in range(2):
                        ins = dve.bn_stats(col(ST + half * 6, 6), xv[:, t, half * W5:(half + 1) * W5])
                        link(ins)
                    link(dve.bn_aggr(col(MV + 2 * t, 2), col(ST, 12)))
                    ins = dve.tensor_scalar(col(RS + t, 1), col(MV + 2 * t + 1, 1), EPS, None, ALU.add)
                    if t < T - 1:
                        link(ins)
                ins.then_inc(sem("ln_var"), 1)
                dve.wait_ge(sem("ln_std"), n + 1)
                link(dve.reciprocal(col(RS, T), col(RS, T)))
                dve.wait_ge(sem("ln_in"), 32 * (n + 1))
                for t in range(T):
                    link(dve.tensor_scalar(xv[:, t, :], xv[:, t, :], col(MV + 2 * t, 1), col(RS + t, 1), ALU.subtract, ALU.mult))
                for t in range(T):
                    link(dve.tensor_tensor(xv[:, t, :], xv[:, t, :], lnp[:, 0:D], ALU.mult))
                for t in range(T):
                    dve.tensor_tensor(xv[:, t, :], xv[:, t, :], lnp[:, D:2 * D], ALU.add).then_inc(sem("x_ready"), 1)

            def modulate(l, which):
                shift, scale = (0, 8) if which == 0 else (24, 32)
                for k in range(KC):
                    ps, free = full(dve, ("xt", l, which, k))
                    dve.tensor_scalar(xtv[:, k, 0:SEQ], ps[:, 0:SEQ], modv[:, scale + k, 0:1], modv[:, shift + k, 0:1],
                                      ALU.mult, ALU.add)
                    dve.tensor_scalar(xtv[:, k, SEQ:], ps[:, SEQ:TOK], modv[:, scale + k, 1:2], modv[:, shift + k, 1:2],
                                      ALU.mult, ALU.add).then_inc(free, 1)

            def finish(l, br):
                o12 = otok[:, :].rearrange("p (n w) -> p n w", w=P)
                sq = (u_gdn, u_gla, u_att)[br][:, 0:T * W5]
                link(dve.tensor_tensor(sq, otok[:, :], otok[:, :], ALU.mult))
                link(dve.tensor_reduce(col(SS, 12), sq.rearrange("p (n w) -> p n w", w=P), AX.X, ALU.add))
                dve.tensor_scalar(col(SS, 12), col(SS, 12), 1.0 / P, EPS, ALU.mult, ALU.add).then_inc(sem("branch_var"), 1)
                dve.wait_ge(sem("branch_std"), l * 3 + br + 1)
                link(dve.reciprocal(col(SS, 12), col(SS, 12)))
                if br == 2:
                    link(dve.tensor_scalar(col(SS, 12), col(SS, 12), 1.0 - lam_init(l), None, ALU.mult))
                link(dve.tensor_tensor(o12, o12, wide(col(SS, 12), P), ALU.mult))
                if br < 2:
                    dve.wait_ge(sem("gates_scaled"), l * 2 + br + 1)
                    dve.tensor_tensor(ov, ov, (zv, rv)[br], ALU.mult).then_inc(sem("branch_normed"), 1)
                else:
                    dve.tensor_tensor(o12, o12, fan(par[:, l * 656 + 272:l * 656 + 400], 12), ALU.mult).then_inc(sem("branch_normed"), 1)

            def mod_out(l, i):
                if i // 2 in (2, 5):
                    return
                ps, free = full(dve, ("modc", l, i))
                dst = modt[:, i * 8:(i + 1) * 8]
                if i // 2 in (1, 4):
                    dve.tensor_scalar(dst, ps[:, 0:8], 1.0, None, ALU.add).then_inc(free, 1)
                else:
                    dve.tensor_copy(dst, ps[:, 0:8]).then_inc(free, 1)

            def modulation_rows(l, first):
                for j in range(first, first + 6):
                    ps, free = full(dve, ("mod", l, j))
                    dve.wait_ge(sem(f"bias_row{j % 2}_in"), 16 * (l * 6 + j // 2 + 1))
                    if j > first + 1:
                        i = j - 2
                        full(dve, ("modg", l, i, 1) if i // 2 in (2, 5) else ("modc", l, i))
                    dve.tensor_tensor(mrow[0:2, j % 2 * W5:(j % 2 + 1) * W5], ps[0:2, :],
                                      brow[0:2, j % 2 * W5:(j % 2 + 1) * W5], ALU.add).then_inc(free, 1)
                    if j > first:
                        mod_out(l, j - 1)
                mod_out(l, first + 5)

            dve.memset(col(1010, 1), EPS).then_inc(sem("eps_set"), 1)
            for l in range(DEPTH):
                modulation_rows(l, 0)
                ps, free = full(dve, ("taps", l))
                dve.tensor_copy(convc[:, :], ps[:, 0:60]).then_inc(free, 1)
                drained(dve, ("taps", l))
                drained(dve, ("modc", l, 3))
                modulate(l, 0)
                for m in range(12):
                    tmp = conv_out(m)
                    drained(dve, ("qkv", l, m))
                    if m > 1:
                        dve.wait_ge(sem("silu_done"), l * 12 + m - 1)
                    link(dve.tensor_scalar(tmp, qk[:, m, 0:CW], convc[:, m:m + 1], None, ALU.mult))
                    for k in range(1, TAPS):
                        ins = dve.scalar_tensor_tensor(out=tmp, in0=qk[:, m, k:k + CW], scalar=convc[:, 12 * k + m:12 * k + m + 1],
                                                       in1=tmp, op0=ALU.mult, op1=ALU.add)
                        if k < TAPS - 1:
                            link(ins)
                    ins.then_inc(sem("conv_done"), 1)
                drained(dve, ("ba", l))
                ab3 = col(AB, 24).rearrange("p (t c) -> p t c", t=T)
                dve.tensor_tensor(ab3, ab3, fan(par[:, l * 656 + 8:l * 656 + 16], T), ALU.add).then_inc(sem("decay_in"), 1)
                dve.wait_ge(sem("softplus_part"), l + 1)
                link(dve.scalar_tensor_tensor(out=col(GG, 24), in0=col(AB, 24), scalar=0.0, in1=col(GC, 24), op0=ALU.max, op1=ALU.add))
                link(dve.tensor_scalar(col(EXPA, 8), col(EXPA, 8), -1.0, None, ALU.mult))
                gg3 = col(GG, 24).rearrange("p (t c) -> p t c", t=T)
                dve.tensor_tensor(gg3, gg3, fan(col(EXPA, 8), T), ALU.mult).then_inc(sem("log_decay"), 1)
                drained(dve, ("ss", l, 7))
                link(dve.reciprocal(u_gdn[:, 1552:1552 + 8 * CW], u_gdn[:, 1552:1552 + 8 * CW]))
                for m in range(8):
                    if m < 4:
                        ins = dve.scalar_tensor_tensor(out=qk[:, m, 0:CW], in0=qk[:, m, 0:CW], scalar=P ** -0.5, in1=qnorm(m),
                                                       op0=ALU.mult, op1=ALU.mult)
                    else:
                        ins = dve.tensor_tensor(qk[:, m, 0:CW], qk[:, m, 0:CW], qnorm(m), ALU.mult)
                ins.then_inc(sem("qk_normed"), 1)
                ps, free = full(dve, ("gc", l))
                dve.wait_ge(sem("log_decay"), l + 1)
                dve.tensor_copy(col(GC, 24), ps[:, 0:24])
                dve.tensor_copy(col(TOTC, 24), ps[:, 32:56]).then_inc(free, 1)
                drained(dve, ("gc", l))
                dve.tensor_tensor(col(ETAIL, 24), col(TOTC, 24), col(GC, 24), ALU.subtract).then_inc(sem("decay_sums"), 1)
                dve.wait_ge(sem("decays"), l + 1)
                link(dve.tensor_tensor(col(BEGC, 24), col(BETA, 24), col(EGC, 24), ALU.mult))

                def h4(ap):
                    return ap.rearrange("p (h i) -> p h i", h=H)

                seen = set()
                for p, tiles in enumerate(PAIRS):
                    for d, t in enumerate(tiles):
                        n = batch(l, p, d)
                        at = t * 8 + d * 4
                        ps, free = full(dve, ("gcrow", n))
                        for h in range(H):
                            ins = dve.tensor_scalar(gd(d, "dt", h), ps[:, h * P:(h + 1) * P], col(GC + at + h, 1), 0.0,
                                                    ALU.subtract, ALU.min)
                        ins.then_inc(free, 1)
                        dve.wait_ge(sem("dt_exp"), n + 1)
                        link(dve.tensor_tensor(h4(gd(d, "dt")), h4(gd(d, "dt")), fan(c(f"tri{d}"), H), ALU.mult))
                        psb, freeb = full(dve, ("brow", n))
                        psq, freeq = full(dve, ("qk", n))
                        dve.tensor_tensor(gd(d, "a"), psq[:, :], gd(d, "dt"), ALU.mult).then_inc(freeq, 1)
                        psk, freek = full(dve, ("kk", n))
                        dve.tensor_tensor(gd(d, "lt"), psk[:, :], gd(d, "dt"), ALU.mult).then_inc(freek, 1)
                        drained(dve, ("kk", n))
                        dve.tensor_tensor(gd(d, "lt"), psb[:, :], gd(d, "lt"), ALU.mult).then_inc(freeb, 1)
                    for d, t in enumerate(tiles):
                        n = batch(l, p, d)
                        dve.wait_ge(sem("level_part"), level_count(l, p, d, 0))
                        dve.tensor_tensor(h4(gd(d, "xt")), fan(c("ident"), H), h4(gd(d, "m")), ALU.subtract).then_inc(sem("inv_start"), 1)
                    for v in range(1, LEVELS):
                        for d, t in enumerate(tiles):
                            n = batch(l, p, d)
                            if v == 1:
                                drained(dve, ("x0", n))
                                dve.wait_ge(sem("inv_start"), n + 1)
                            if v > 1:
                                drained(dve, ("xy", n, v - 1))
                                drained(dve, ("xty", n, v - 1))
                            if v < LEVELS - 1:
                                ps, free = full(dve, ("xy", n, v))
                                dve.tensor_tensor(gd(d, "x"), gd(d, "x"), ps[:, :], ALU.subtract).then_inc(free, 1)
                            ps, free = full(dve, ("xty", n, v))
                            dve.tensor_tensor(gd(d, "xt"), gd(d, "xt"), ps[:, :], ALU.subtract).then_inc(free, 1)
                    for d, t in enumerate(tiles):
                        n = batch(l, p, d)
                        at = t * 8 + d * 4
                        drained(dve, ("vtok", l, t))
                        ins = dve.tensor_tensor(h4(gd(d, "y")), h4(vtok[:, t, :]), wide(col(BETA + at, 4), P), ALU.mult)
                        if p == 0:
                            ins.then_inc(sem("gdn_rhs"), 1)
                            continue
                        link(ins)
                        ps, free = full(dve, ("ks", n))
                        dve.tensor_tensor(h4(gd(d, "m")), h4(ps[:, :]), wide(col(BEGC + at, 4), P), ALU.mult).then_inc(free, 1)
                        drained(dve, ("ks", n))
                        dve.tensor_tensor(gd(d, "y"), gd(d, "y"), gd(d, "m"), ALU.subtract).then_inc(sem("gdn_rhs"), 1)
                        ps, free = full(dve, ("qs", n))
                        dve.tensor_tensor(h4(gd(d, "dt")), h4(ps[:, :]), wide(col(EGC + at, 4), P), ALU.mult).then_inc(free, 1)
                        drained(dve, ("qs", n))
                    for d, t in enumerate(tiles):
                        n = batch(l, p, d)
                        at = t * 8 + d * 4
                        ps, free = full(dve, ("vnew", n))
                        if p:
                            dve.wait_ge(sem("gdn_rhs"), n + 1)
                        link(dve.tensor_copy(gd(d, "x"), ps[:, :]))
                        dve.tensor_tensor(h4(gd(d, "m")), h4(ps[:, :]), wide(col(ETAIL + at, 4), P), ALU.mult).then_inc(free, 1)
                    for d, t in enumerate(tiles):
                        n = batch(l, p, d)
                        at = t * 8 + d * 4
                        ps, free = full(dve, ("av", n))
                        if p == 0:
                            if t in seen:
                                dve.tensor_tensor(ov[:, t, :], ov[:, t, :], ps[:, :], ALU.add).then_inc(free, 1)
                            else:
                                dve.tensor_copy(ov[:, t, :], ps[:, :]).then_inc(free, 1)
                        else:
                            if t in seen:
                                link(dve.tensor_tensor(gd(d, "dt"), gd(d, "dt"), ov[:, t, :], ALU.add))
                            dve.tensor_tensor(ov[:, t, :], gd(d, "dt"), ps[:, :], ALU.add).then_inc(free, 1)
                        drained(dve, ("av", n))
                        seen.add(t)
                        if p == 2:
                            continue
                        if p == 0:
                            if l:
                                dve.wait_ge(sem("gla_out"), 64 * l)
                            ps, free = full(dve, ("ds", n))
                            dve.tensor_copy(st_out(d), ps[:, :]).then_inc(free, 1)
                        else:
                            s = s_gdn[:, d * W5:(d + 1) * W5]
                            link(dve.tensor_tensor(h4(s), h4(s), wide(col(ETOT + at, 4), P), ALU.mult))
                            ps, free = full(dve, ("ds", n))
                            dve.tensor_tensor(s, s, ps[:, :], ALU.add).then_inc(free, 1)
                finish(l, 0)

                for t in range(T):
                    ps, free = full(dve, ("glog", l, t))
                    dve.wait_ge(sem("gla_ln"), l * T + t + 1)
                    dve.scalar_tensor_tensor(out=u_gla[:, t * W5:(t + 1) * W5], in0=ps[:, :], scalar=0.0, in1=gl_ln,
                                             op0=ALU.min, op1=ALU.subtract).then_inc(free, 1)
                seen = set()
                for p, tiles in enumerate(PAIRS):
                    for name, src, key in (("q_in", 0, "gla_rel"), ("k_in", 256, "gla_rel"), ("q_dec", 0, "gla_sum"), ("k_tail", 256, "gla_tail")):
                        drained(dve, (key, l, p))
                        for d, t in enumerate(tiles):
                            w = gl(name)[:, d * 256:(d + 1) * 256]
                            ins = dve.tensor_tensor(w, w, gqkv[:, t, src:src + 256], ALU.mult)
                        ins.then_inc(sem("gla_decayed"), 1)
                    for d, t in enumerate(tiles):
                        ps, free = full(dve, ("gla_a", l, p, d))
                        if p == 0 and d == 0:
                            dve.wait_ge(sem("gla_zeroed"), l + 1)
                        dve.copy_predicated(h4(gla_at(d)), fan(c(f"sum{d}").bitcast(U32), H), h4(ps[:, :])).then_inc(free, 1)
                    for d, t in enumerate(tiles):
                        ps, free = full(dve, ("gla_av", l, p, d))
                        if t in seen:
                            dve.tensor_tensor(ov[:, t, :], ov[:, t, :], ps[:, :], ALU.add).then_inc(free, 1)
                        else:
                            if p == 0:
                                drained(dve, ("ot", l, 0, H - 1))
                            dve.tensor_copy(ov[:, t, :], ps[:, :]).then_inc(free, 1)
                        seen.add(t)
                        drained(dve, ("gla_av", l, p, d))
                    for step in range(2):
                        for d, t in enumerate(tiles):
                            ch = step if d == 0 else 1 - step
                            tok = slice(ch * HALF, (ch + 1) * HALF)
                            ps, free = full(dve, ("gla_inter", l, p, d, step))
                            dve.tensor_tensor(ov[tok, t, :], ov[tok, t, :], ps[tok, :], ALU.add).then_inc(free, 1)
                            drained(dve, ("gla_inter", l, p, d, step))
                            if p == 2 and step == 1:
                                continue
                            if step == 0:
                                drained(dve, ("gla_gt", l, p))
                            ps, free = full(dve, ("gla_ds", l, p, d, step))
                            s = gla_state(p, d)
                            for hp in range(2):
                                for hh in range(2):
                                    rr, cc = slice(hh * 64, hh * 64 + 64), slice(hp * 256 + hh * P, hp * 256 + hh * P + P)
                                    g0 = (d * 2 + hp) * 2 + ch
                                    ins = dve.scalar_tensor_tensor(out=s[rr, cc], in0=s[rr, cc], scalar=gla_gt(p)[rr, g0:g0 + 1],
                                                                   in1=ps[rr, cc], op0=ALU.mult, op1=ALU.add)
                            ins.then_inc(free, 1)
                            drained(dve, ("gla_ds", l, p, d, step))
                finish(l, 1)

                lp = par[:, l * 656 + 400:l * 656 + 656].rearrange("p (a s d) -> p a s d", a=2, s=2)
                link(dve.tensor_tensor(col(LPROD, 128).rearrange("p (a d) -> p a d", a=2), lp[:, :, 0, :], lp[:, :, 1, :], ALU.mult))
                dve.tensor_reduce(col(LAM, 2), col(LPROD, 128).rearrange("p (a d) -> p a d", a=2), AX.X, ALU.add).then_inc(sem("lam_parts"), 1)
                dve.wait_ge(sem("lam_exp"), l + 1)
                link(dve.tensor_tensor(col(LAM, 1), col(LAM, 1), col(LAM + 1, 1), ALU.subtract))
                link(dve.tensor_scalar(col(LAM, 1), col(LAM, 1), lam_init(l), None, ALU.add))
                tmp = u_att[:, 3072:3584]
                for t in (1, 2):
                    for name, v in (("dq", dqv), ("dk", dkv)):
                        drained(dve, (name, l, t))
                        rope = c("rope", (t - 1) * P, t * P)
                        s = v[:, t, :]
                        s5 = s.rearrange("p (g r j w) -> p g r j w", g=8, r=2, j=2)
                        tp5 = tmp.rearrange("p (g r j w) -> p g r j w", g=8, r=2, j=2)
                        sin = rope[:, 64:128].rearrange("p (r j w) -> p r j w", r=2, j=2)
                        for j in range(2):
                            for r in range(2):
                                link(dve.tensor_tensor(tp5[:, :, r, j, :],
                                                       s5[:, :, r, 1 - j, :],
                                                       fan(sin[:, r, j, :], 8), ALU.mult))
                        s8 = s.rearrange("p (g w) -> p g w", g=8)
                        link(dve.tensor_tensor(s8, s8, fan(rope[:, 0:64], 8), ALU.mult))
                        dve.tensor_tensor(s, s, tmp, ALU.add).then_inc(sem("roped"), 1)
                        dve.wait_ge(sem("roped"), (l * 2 + t - 1) * 2 + (1 if name == "dq" else 2))
                for t in range(T):
                    nk = P if t == 0 else KEYS
                    for hh in range(H + 1):
                        if hh < H:
                            n = (l * T + t) * H + hh
                            for s in range(2):
                                ps, _ = full(dve, ("sc", l, t, hh, s))
                                link(dve.tensor_reduce(col(NM + s, 1), ps[:, 0:nk], AX.X, ALU.max))
                                dve.tensor_scalar(col(NM + s, 1), col(NM + s, 1), -DH ** -0.5, None, ALU.mult).then_inc(sem("neg_max"), 1)
                        if hh < H:
                            drained(dve, ("sc", l, t, hh, 0))
                            drained(dve, ("sc", l, t, hh, 1))
                            link(dve.reciprocal(col(RP, 2), col(SUMP, 2)))
                            link(dve.tensor_tensor(col(RP + 1, 1), col(RP + 1, 1), col(LAM, 1), ALU.mult))
                            link(dve.tensor_scalar(dp(1)[:, 0:nk], dp(1)[:, 0:nk], col(RP + 1, 1), None, ALU.mult))
                            if n > 1:
                                m = n - 2
                                full(dve, ("wt", m // (T * H), m // H % T, m % H))
                            dve.scalar_tensor_tensor(out=dw(n % 2)[:, 0:nk], in0=dp(0)[:, 0:nk], scalar=col(RP, 1), in1=dp(1)[:, 0:nk],
                                                     op0=ALU.mult, op1=ALU.subtract).then_inc(sem("attn_weights"), 1)
                            dve.wait_ge(sem("attn_weights"), n + 1)
                        if hh:
                            h = hh - 1
                            ps, free = full(dve, ("att", l, t, h))
                            if t == 0 and h == 0:
                                drained(dve, ("ot", l, 1, H - 1))
                            dve.tensor_copy(ov[:, t, h * P:(h + 1) * P], ps[:, 0:P]).then_inc(free, 1)
                drained(dve, ("att", l, T - 1, H - 1))
                finish(l, 2)

                tmp = mtmp
                for s in range(3):
                    for t in range(T):
                        for half in range(2):
                            cut = slice(half * W5, (half + 1) * W5)
                            ps, free = full(dve, ("branch", l, s, t, half))
                            drained(dve, (("mergel", 2 * s + half), l, t))
                            if s == 0:
                                dve.tensor_tensor(mix[:, t, cut], mg[:, t, cut], ps[:, :], ALU.mult).then_inc(free, 1)
                                drained(dve, ("branch", l, s, t, half))
                            else:
                                dve.tensor_tensor(tmp, mg[:, t, cut], ps[:, :], ALU.mult).then_inc(free, 1)
                                drained(dve, ("branch", l, s, t, half))
                                ins = dve.tensor_tensor(mix[:, t, cut], mix[:, t, cut], tmp, ALU.add)
                                if s == 2 and t == T - 1 and half == 1:
                                    ins.then_inc(sem("mixed"), 1)
                                else:
                                    link(ins)
                for half in range(2):
                    for t in range(T):
                        cut = slice(half * W5, (half + 1) * W5)
                        ps, free = full(dve, (("outl", half), l, t))
                        dve.tensor_tensor(tmp, gatev[:, min(t, 1), cut], ps[:, :], ALU.mult).then_inc(free, 1)
                        drained(dve, (("outl", half), l, t))
                        link(dve.scalar_tensor_tensor(out=xv[:, t, cut], in0=xv[:, t, cut], scalar=ALPHA, in1=tmp, op0=ALU.mult, op1=ALU.add))
                layer_norm(l, 0)
                modulation_rows(l, 6)
                drained(dve, ("modc", l, 9))
                modulate(l, 1)

                sc, bi, cm, eq, rk, gs, gr = (RTR + at for at in (0, 48, 96, 288, 480, 528, 540))
                drained(dve, ("router", l))
                dve.wait_ge(sem("router_in"), 32)
                link(dve.tensor_tensor(col(bi, 48).rearrange("p (t e) -> p t e", t=T), col(sc, 48).rearrange("p (t e) -> p t e", t=T),
                                       fan(rbias[:, :], T), ALU.add))

                def ranks(src, n, dst):
                    v = col(src, 4 * n).rearrange("p (g f) -> p g f", g=n)
                    other = v.unsqueeze(2).broadcast_to([P, n, 4, 4])
                    own = v.unsqueeze(3).broadcast_to([P, n, 4, 4])
                    a4 = col(cm, 16 * n).rearrange("p (g e f) -> p g e f", g=n, e=4)
                    b4 = col(eq, 16 * n).rearrange("p (g e f) -> p g e f", g=n, e=4)
                    link(dve.tensor_tensor(a4, other, own, ALU.is_gt))
                    link(dve.tensor_tensor(b4, other, own, ALU.is_equal))
                    b3 = col(eq, 16 * n).rearrange("p (g w) -> p g w", g=n)
                    link(dve.tensor_tensor(b3, b3, fan(c("before"), n), ALU.mult))
                    link(dve.tensor_tensor(col(cm, 16 * n), col(cm, 16 * n), col(eq, 16 * n), ALU.add))
                    link(dve.tensor_reduce(col(dst, 4 * n), col(cm, 16 * n).rearrange("p (a f) -> p a f", f=4), AX.X, ALU.add))

                ranks(bi, T * NG, rk)
                link(dve.tensor_scalar(col(rk, 48), col(rk, 48), 1.5, None, ALU.is_lt))
                link(dve.tensor_tensor(col(bi, 48), col(bi, 48), col(rk, 48), ALU.mult))
                link(dve.tensor_reduce(col(gs, 12), col(bi, 48).rearrange("p (g f) -> p g f", f=4), AX.X, ALU.add))
                ranks(gs, T, gr)
                link(dve.tensor_scalar(col(gr, 12), col(gr, 12), 0.5, None, ALU.is_lt))
                link(dve.tensor_tensor(col(sc, 48), col(sc, 48), col(rk, 48), ALU.mult))
                link(dve.tensor_tensor(col(sc, 48).rearrange("p (g f) -> p g f", f=4), col(sc, 48).rearrange("p (g f) -> p g f", f=4),
                                       wide(col(gr, 12), 4), ALU.mult))
                link(dve.tensor_reduce(col(RS, T), col(sc, 48).rearrange("p (t e) -> p t e", t=T), AX.X, ALU.add))
                link(dve.reciprocal(col(RS, T), col(RS, T)))
                link(dve.tensor_tensor(col(sc, 48).rearrange("p (t e) -> p t e", t=T), col(sc, 48).rearrange("p (t e) -> p t e", t=T),
                                       wide(col(RS, T), E), ALU.mult))
                link(dve.memset(proj[:, T * D:2 * T * D], 0.0))
                gates3 = col(sc, 48).rearrange("p (t e) -> p t e", t=T)
                with dve.Fori(0, E) as e:
                    for m in range(4):
                        drained(dve, ("gatep", l, m), e)
                        ps, free = full(dve, ("upp", l, m), e)
                        dve.tensor_tensor(hact[:, m, :], ag[:, m, :], ps[:, 0:TOK], ALU.mult).then_inc(free, 1)
                    for t in range(T):
                        for half in range(2):
                            ycut = yacc[:, t, half * W5:(half + 1) * W5]
                            b, n = fills["downp", l, t, half]
                            dve.wait_ge(bank_free[b], e * 2 + (n - 2))
                            ps, free = full(dve, ("downp", l, t, half), e)
                            dve.scalar_tensor_tensor(out=ycut, in0=ps[:, :], scalar=gates3[:, t, bass.ds(e, 1)],
                                                     in1=ycut, op0=ALU.mult, op1=ALU.add).then_inc(free, 1)
                for t in range(T):
                    b, n = fills["downp", l, t, 1]
                    dve.wait_ge(bank_free[b], n + 2 * (E - 1))
                    link(dve.tensor_tensor(yacc[:, t, :], yacc[:, t, :], gatev[:, min(t, 1), :], ALU.mult))
                    link(dve.scalar_tensor_tensor(out=xv[:, t, :], in0=xv[:, t, :], scalar=ALPHA, in1=yacc[:, t, :], op0=ALU.mult, op1=ALU.add))
                layer_norm(l, 1)


_INS = ["x_prompt", "x_sample", "c", "state_gdn", "state_gla", "cache_k", "cache_v", "c_ctx", "w_mod", "b_mod", "w_in",
        "gdn_conv", "gdn_a_log", "gdn_dt_bias", "gdn_norm", "gla_w_gate", "gla_b_gate", "gla_norm", "diff_lambda",
        "diff_norm", "w_branch", "w_out", "ln_g", "ln_b", "router_w", "router_b", "exp_w_gate", "exp_w_up", "exp_w_down"]
_OUTS = [("y_prompt", (1, SEQ, D)), ("y_sample", (1, DEC, D)), ("new_gdn", (1, DEPTH, 2, H, P, P)),
         ("new_gla", (1, DEPTH, 2, H, GLA_DK, P)), ("new_k", (1, DEPTH, SEQ, H, P)), ("new_v", (1, DEPTH, SEQ, H, P))]


def kernel(**inputs):
    import numpy as _np
    import concourse.bacc as _bacc
    from concourse import mybir as _mybir
    from concourse.bass_utils import run_bass_kernel_spmd as _run

    nc = _bacc.Bacc("TRN2", target_bir_lowering=False, num_devices=1)
    arrays = {f"in_{n}": _np.ascontiguousarray(inputs[n]) for n in _INS}
    arrays["in_consts"] = constants()[0]
    dram = {n: nc.dram_tensor(n, v.shape, _mybir.dt.from_np(v.dtype), kind="ExternalInput").ap() for n, v in arrays.items()}
    outs = [nc.dram_tensor(n, shape, F32, kind="ExternalOutput").ap() for n, shape in _OUTS]
    program(nc, {n: dram[f"in_{n}"] for n in _INS}, dram["in_consts"], *outs)
    r = _run(nc, [arrays], core_ids=[0])
    return tuple(r.results[0][n] for n, _ in _OUTS)
```

```python
from contextlib import ExitStack

import concourse.bass as bass
import numpy as np
from concourse import mybir

F32 = mybir.dt.float32
U32 = mybir.dt.uint32
ALU = mybir.AluOpType
ACT = mybir.ActivationFunctionType
AX = mybir.AxisListType

P = 128
D = 1024
KC = D // P
DEPTH = 2
SEQ, DEC = 128, 256
T = (SEQ + DEC) // P
TOK = T * P
H = 4
W5 = 512
GLA_DK = 64
HALF = 64
RANK = 16
DH = 64
PAST = 128
KEYS = DEC + PAST
TAPS = 5
E = 16
NG = 4
ALPHA = (2 * DEPTH) ** 0.25
EPS = 1e-6
TAU = 16.0
DIR = 2
LEVELS = 7
CW = TOK + 2
COL = (0, SEQ + 2, SEQ + 2 + P)
IN_COL = dict(qkv=0, z=1536, ba=2048, gqk=2064, gv=2576, r=3088, lr=3600, dq=3632, dk=4144, dv=4656, merge=5168)
RING = 3
SLOTS = 64
MORE = TOK * 2 // SLOTS
JOBS = E + MORE + 2
PAIRS_MAX = (E + MORE) // 2
EP = E + 1
CHUNK_W = KC * W5
PAIRS = ((0, 0), (1, 2), (2, 1))


def lam_init(l):
    return 0.8 - 0.6 * float(np.exp(-0.3 * l))


def constants():
    k, i = np.arange(P)[:, None], np.arange(P)[None, :]
    same = (k // HALF) == (i // HALF)
    mats = dict(ident=k == i, tri0=k <= i, tri1=k >= i, ones=np.ones((P, P)))
    for n in range(LEVELS):
        b = 1 << n
        lower = (k // (2 * b) == i // (2 * b)) & (k // b % 2 == 0) & (i // b % 2 == 1)
        mats[f"level0_{n}"], mats[f"level1_{n}"] = lower, lower.T
    base = i // HALF * HALF
    for d in range(DIR):
        upto = lambda t: same & ((k <= t) if d == 0 else (k >= t))
        ref = base + (HALF // 2 if d == 0 else HALF // 2 - 1)
        mats[f"sum{d}"] = upto(i)
        mats[f"rel{d}"] = upto(i).astype(float) - upto(ref).astype(float)
        mats[f"tail{d}"] = same.astype(float) - upto(i).astype(float)
    cols = {n: np.asarray(m, np.float32) for n, m in mats.items()}
    cols["slots"] = np.broadcast_to(np.arange(TOK, dtype=np.float32)[None, :], (P, TOK))
    cols["unit"] = np.broadcast_to(np.arange(15)[None, :] == 7, (P, 15)).astype(np.float32)
    cols["mod_sum"] = (np.arange(P)[:, None] % 32 == np.arange(2)[None, :]).astype(np.float32)
    cols["chunks"] = (k // HALF == np.arange(2)[None, :]).astype(np.float32)
    e, f = np.arange(4)[:, None], np.arange(4)[None, :]
    cols["before"] = np.broadcast_to((f < e).astype(np.float32).reshape(1, 16), (P, 16))
    pos = np.arange(DEC)
    inv = np.float32(10000.0) ** (-np.arange(0, 32, 2, dtype=np.float32) / np.float32(32))
    rot = np.zeros((DEC, 2, 2, 2, 16), np.float32)
    for half, where in enumerate((pos // 64, pos % 64)):
        ang = where.astype(np.float32)[:, None] * inv[None, :]
        rot[:, 0, half] = np.cos(ang)[:, None, :]
        rot[:, 1, half, 0], rot[:, 1, half, 1] = -np.sin(ang), np.sin(ang)
    cols["rope"] = rot.reshape(2, P, 128).transpose(1, 0, 2).reshape(P, 256)
    at, where = 0, {}
    for n, m in cols.items():
        where[n] = (at, m.shape[1])
        at += m.shape[1]
    return np.ascontiguousarray(np.concatenate(list(cols.values()), axis=1), np.float32), where


def program(nc, a, consts, y_prompt, y_sample, new_gdn, new_gla, new_k, new_v):
    order, place, dense_end = [], {}, []
    _, cwhere = constants()

    with ExitStack() as ctx:
        def sb(name, width, parts=P):
            return ctx.enter_context(nc.sbuf_tensor(name, [parts, width], F32))

        sems = {}

        def sem(name):
            if name not in sems:
                sems[name] = ctx.enter_context(nc.semaphore(name))
            return sems[name]

        cst = sb("cst", sum(w for _, w in cwhere.values()))
        x = sb("x", T * D)
        xt = sb("xt", KC * TOK)
        ring = sb("ring", RING * CHUNK_W)
        gate = sb("gate", 2 * D)
        modt = sb("modt", DEPTH * 96)
        bcol = sb("bcol", DEPTH * 48)
        crow = sb("crow", P, 16)
        scol = sb("scol", KC * 32)
        mrow = sb("mrow", W5)
        router = sb("router", KC * E)
        rbias = sb("rbias", E)
        wsmall = sb("wsmall", DEPTH * KC * 48)
        convrow = sb("convrow", DEPTH * P, 12 * TAPS)
        convc = sb("convc", 12 * TAPS)
        par = sb("par", DEPTH * 656)
        wgate = sb("wgate", DEPTH * W5, 33)
        lrt = sb("lrt", TOK, 33)
        small = sb("small", 1060 + 2 + 2 * T)
        s_gdn = sb("s_gdn", DIR * W5)
        s_gla = sb("s_gla", 2 * DIR * W5)
        qkvp = sb("qkvp", 12 * 390)
        otok = sb("otok", T * W5)
        shared = sb("shared", 13312)
        late = shared[:, 0:4608]
        proj = shared[:, 4608:10752]
        tail = shared[:, 10752:13312]
        lnp, mtmp = tail[:, 0:2 * D], tail[:, 2 * D:]
        ckv = tail[:, 0:2 * W5]
        u_gdn = shared[:, 6144:13312]
        u_gla = shared[:, 0:6144]
        u_att = proj

        banks = [ctx.enter_context(nc.psum_tensor(f"bank{b}", [P, W5], F32)) for b in range(8)]
        bank_full = [sem(f"bank{b}_full") for b in range(8)]
        bank_free = [sem(f"bank{b}_free") for b in range(8)]
        slot_in = [sem(f"slot{s}_in") for s in range(RING)]

        def c(name, a0=None, a1=None):
            at, w = cwhere[name]
            return cst[:, at + (a0 or 0):at + (w if a1 is None else a1)]

        def fan(ap, n):
            return ap.unsqueeze(1).broadcast_to([ap.shape[0], n, ap.shape[-1]])

        def wide(ap, w):
            return ap.unsqueeze(2).broadcast_to([ap.shape[0], ap.shape[1], w])

        xv = x[:, :].rearrange("p (t d) -> p t d", t=T)
        xtv = xt[:, :].rearrange("p (k t) -> p k t", k=KC)
        gatev = gate[:, :].rearrange("p (c d) -> p c d", c=2)
        modv = modt[:, :].rearrange("p (l j c) -> p l j c", l=DEPTH, c=2)
        mod_bank = banks[7]
        qk = qkvp[:, :].rearrange("p (m w) -> p m w", m=12)
        ot = qkvp[:, 0:12 * TOK].rearrange("p (m t) -> p m t", m=12)
        zv = proj[:, 0:T * W5].rearrange("p (t w) -> p t w", t=T)
        rv = proj[:, T * W5:2 * T * W5].rearrange("p (t w) -> p t w", t=T)
        gqkv = proj[:, 2 * T * W5:3 * T * W5].rearrange("p (t w) -> p t w", t=T)
        gvv = proj[:, 3 * T * W5:].rearrange("p (t w) -> p t w", t=T)
        mix = proj[:, 0:T * D].rearrange("p (t d) -> p t d", t=T)
        yacc = proj[:, T * D:].rearrange("p (t d) -> p t d", t=T)
        ktok = late[:, 0:T * W5].rearrange("p (t w) -> p t w", t=T)
        vtok = late[:, T * W5:2 * T * W5].rearrange("p (t w) -> p t w", t=T)
        dqv = late[:, 0:T * W5].rearrange("p (t w) -> p t w", t=T)
        dkv = late[:, T * W5:2 * T * W5].rearrange("p (t w) -> p t w", t=T)
        dvv = late[:, 2 * T * W5:].rearrange("p (t w) -> p t w", t=T)
        mg = late[:, 0:T * D].rearrange("p (t d) -> p t d", t=T)
        ov = otok[:, :].rearrange("p (t w) -> p t w", t=T)
        ring_in = [ring[:, s * CHUNK_W:(s + 1) * CHUNK_W].rearrange("p (k n) -> p k n", k=KC) for s in range(RING)]
        ring_dn = [ring[:, s * CHUNK_W:(s + 1) * CHUNK_W].rearrange("p (m n) -> p m n", m=4) for s in range(RING)]
        smv = wsmall[:, :].rearrange("p (l k n) -> p l k n", l=DEPTH, k=KC)
        rtv = router[:, :].rearrange("p (k e) -> p k e", k=KC)
        htok = proj[:, 0:T * D].rearrange("p (t d) -> p t d", t=T)
        hot = qkvp[:, 0:384].rearrange("p (t u s) -> p t u s", t=T, u=2)
        hotg = qkvp[:, 384:768].rearrange("p (t u s) -> p t u s", t=T, u=2)
        xg, ag, hact, ht = late[:, 0:1024], late[:, 1024:1536], late[:, 1536:2048], late[:, 2048:2560]
        oe, hott = late[:, 2560:3584], late[:, 3584:3968]
        jobs = ctx.enter_context(nc.sbuf_tensor("jobs", [1, 3 * JOBS + 2], mybir.dt.int32))

        def col(at, n):
            return small[:, at:at + n]

        BETA, GG, GC, TOTC, EGC, ETOT, ETAIL, BEGC = (24 * n for n in range(8))
        AB, EXPA, LAM, LPROD, SS, RS, NM, SUMP, RP, ST, MV, RTR, GSEL = 192, 216, 224, 228, 360, 376, 392, 396, 400, 404, 428, 440, 1062

        filled = [0] * 8
        fills = {}
        turn = [0]
        chunk_end = {}

        def take(pe, key):
            b = turn[0] % 7
            turn[0] += 1
            if filled[b]:
                pe.wait_ge(bank_free[b], filled[b])
            filled[b] += 1
            fills[key] = (b, filled[b], 0)
            return banks[b], bank_full[b]

        def full(eng, key, e=None):
            b, n, turn_ = fills[key]
            eng.wait_ge(bank_full[b], n if e is None else e * turn_ + n)
            return banks[b], bank_free[b]

        def drained(eng, key, e=None, back=0):
            b, n, turn_ = fills[key]
            eng.wait_ge(bank_free[b], n - back * turn_ if e is None else e * turn_ + (n - back * turn_))

        def arrived(eng, key, e=None):
            if key not in place:
                place[key] = len(order)
                order.append(key)
            n = place[key]
            first = 16 * (n // RING + 1)
            eng.wait_ge(slot_in[n % RING], first if e is None else e * 32 + first)
            return n % RING


        GD = dict(dt=0, a=1, lt=2, m=3, x=4, xt=5, y=6)

        def gd(d, name, h=None):
            at = (d * len(GD) + GD[name]) * W5
            return u_gdn[:, at:at + W5] if h is None else u_gdn[:, at + h * P:at + (h + 1) * P]

        def square(m):
            return u_gdn[:, m % 2 * 388:m % 2 * 388 + CW]

        def conv_out(m):
            return u_gdn[:, 776 + m % 2 * 388:776 + m % 2 * 388 + CW]

        def st_out(d):
            return s_gla[:, d * W5:(d + 1) * W5]

        def glog(t, d):
            return u_gla[:, t * W5 + d * 256:t * W5 + (d + 1) * 256]

        GL = dict(q_in=3, k_in=4, q_dec=5, k_tail=6)

        def gl(name):
            return u_gla[:, GL[name] * W5:(GL[name] + 1) * W5]

        gl_qz, gl_k, gl_dec = u_gla[:, 3584:4608], u_gla[:, 4608:5120], u_gla[:, 5120:5632]
        gl_ln = u_gla[:, 5632:6144]

        def gla_at(d):
            return tail[:, d * W5:(d + 1) * W5]

        def gla_state(p, d):
            at = (min(p, 1) * DIR + d) * W5
            return s_gla[:, at:at + W5]

        def gla_gt(p):
            return col(1030 + 8 * p, 8)

        dk_all = u_att[:, 1024:3072].rearrange("p (h k) -> p h k", h=H)

        def dq_z(s, h):
            return u_att[:, s * W5 + h * P:s * W5 + (h + 1) * P]

        def dp(s):
            return u_att[:, 3584 + s * KEYS:3584 + (s + 1) * KEYS]

        def dw(i):
            return u_att[:, 4352 + i * KEYS:4352 + (i + 1) * KEYS]

        def dwt(i):
            return u_att[:, 5120 + i * KEYS:5120 + (i + 1) * KEYS]

        EXPERT_BANKS = dict(out=(0, 1), gate=(2,), up=(3,), gather=(4, 5), turned=(6,), back=(7, 0, 1, 2, 3, 4),
                            choice=(5,))

        def made(eng, name, n, k=0):
            b = EXPERT_BANKS[name]
            eng.wait_ge(sem(f"expert_{name}_full"), n * len(b) + (k + 1))
            return banks[b[k]], sem(f"expert_{name}_free")

        def used(eng, name, n, k=0):
            ahead = len(EXPERT_BANKS["back"]) if name == "back" else 0
            eng.wait_ge(sem(f"expert_{name}_free"), n * len(EXPERT_BANKS[name]) + (k + 1 + ahead))

        def added(eng, n, k):
            eng.wait_ge(sem("expert_back_free"), n * len(EXPERT_BANKS["back"]) + (k + 1))

        W_AT, X_AT, S_AT, TURNS_AT, BEFORE_AT = 0, JOBS, 2 * JOBS, 3 * JOBS, 3 * JOBS + 1

        def listed(eng, l):
            eng.wait_ge(sem("jobs_listed"), l + 1)
            turns = eng.value_load(jobs[0:1, TURNS_AT:TURNS_AT + 1], min_val=E // 2 - 1, max_val=PAIRS_MAX - 1)
            if l == 0:
                return turns, 0
            return turns, eng.value_load(jobs[0:1, BEFORE_AT:BEFORE_AT + 1], min_val=E // 2, max_val=PAIRS_MAX)

        def level_count(l, p, d, v):
            return ((l * 3 + p) * LEVELS + v) * DIR + d + 1

        def silu(act, l, m):
            act.wait_ge(sem("conv_done"), l * 12 + m + 1)
            act.activation(qk[:, m, 0:CW], conv_out(m), ACT.Silu).then_inc(sem("silu_done"), 1)

        def gate_in(act, name, l, v):
            for t in range(T):
                ps, free = full(act, (name, l, t))
                act.activation(v[:, t, :], ps[:, :], ACT.Silu).then_inc(free, 1)

        chosen = col(RTR + 480, 48)

        def branch_root(act, l, br):
            act.wait_ge(sem("branch_var"), l * 3 + br + 1)
            act.activation(col(SS, 12), col(SS, 12), ACT.Sqrt).then_inc(sem("branch_std"), 1)

        def branch_ot(act, l, br):
            for h in range(H):
                ps, free = full(act, ("ot", l, br, h))
                act.activation(ot[:, br * 4 + h, :], ps[:, 0:TOK], ACT.Copy).then_inc(free, 1)

        block = ctx.enter_context(nc.Block())

        def batch(l, p, d):
            return (l * 3 + p) * 2 + d

        @block.tensor
        def _(pe):
            pe.sem_inc(sem("expert_back_free"), len(EXPERT_BANKS["back"]))
            pe.wait_ge(sem("consts_in"), 16)
            pe.wait_ge(sem("cond_in"), 32)
            ps, ready = take(pe, "cond")
            pe.transpose(ps[:, 0:16], crow[0:16, :], c("ident")[0:16, 0:16]).then_inc(ready, 1)
            drained(pe, "cond")
            scv = scol[:, :].rearrange("p (k c) -> p k c", k=KC)

            def tokens_product(key, l, w_of, width=W5, scale_key=None):
                for t in range(T):
                    ps, ready = take(pe, (key, l, t))
                    for k in range(KC):
                        mm = pe.matmul(ps[:, 0:width], xtv[:, k, t * P:(t + 1) * P], w_of(k),
                                       start=(k == 0), stop=(k == KC - 1))
                    mm.then_inc(ready, 1)

            def transpose_x(l, which):
                for k in range(KC):
                    ps, ready = take(pe, ("xt", l, which, k))
                    for t in range(T):
                        if k == 0:
                            n = (l * 2 + which) * T
                            if n:
                                pe.wait_ge(sem("x_ready"), n - T + t + 1)
                            elif t == 0:
                                pe.wait_ge(sem("x_in"), 32)
                        mm = pe.transpose(ps[:, t * P:(t + 1) * P], xv[:, t, k * P:(k + 1) * P], c("ident"))
                    mm.then_inc(ready, 1)
                drained(pe, ("xt", l, which, KC - 1))

            def finish_branch(l, br):
                pe.wait_ge(sem("branch_normed"), l * 3 + br + 1)
                for h in range(H):
                    ps, ready = take(pe, ("ot", l, br, h))
                    for t in range(T):
                        mm = pe.transpose(ps[:, t * P:(t + 1) * P], ov[:, t, h * P:(h + 1) * P], c("ident"))
                    mm.then_inc(ready, 1)

            def mod_rows(l, j):
                slot = arrived(pe, ("mod", l, j))
                ps, ready = take(pe, ("modrow", l, j))
                for k in range(KC):
                    part = k % 4 * 32
                    mm = pe.matmul(ps[part:part + 32, :], scv[:, k, :], ring_in[slot][:, k, :], start=(k < 4), stop=(k >= 4))
                mm.then_inc(ready, 1)
                chunk_end["mod", l, j] = ("modrow", l, j)

            def mod_columns(l, j):
                drained(pe, ("modrow", l, j))
                if j % 6 == 0 and l * 2 + j // 6:
                    pe.wait_ge(sem("mod_out"), l * 2 + j // 6)
                for b in range(4):
                    at = (l * 48 + j * 4 + b) * 2
                    mm = pe.matmul(mod_bank[:, at:at + 2], mrow[:, b * P:(b + 1) * P], c("mod_sum"), start=True, stop=True)
                if j % 6 == 5:
                    mm.then_inc(sem("mod_done"), 1)

            def gate_rows(l, which):
                pe.wait_ge(sem("mod_out"), l * 2 + which + 1)
                for half in range(2):
                    for cond in range(2):
                        ps, ready = take(pe, ("modg", l, which, half, cond))
                        for b in range(4):
                            i = 16 + 24 * which + half * 4 + b
                            mm = pe.matmul(ps[:, b * P:(b + 1) * P], modv[:, l, i, cond:cond + 1].broadcast_to([P, P]), c("ident"),
                                           start=True, stop=True)
                        mm.then_inc(ready, 1)
            ps, ready = take(pe, "mod_bias")
            pe.wait_ge(sem("mod_bias_in"), 16)
            pe.transpose(ps[:, 0:96], otok[0:96, 0:P], c("ident")[0:96, 0:96]).then_inc(ready, 1)
            for l in range(DEPTH):
                if l == 0:
                    for j in range(6):
                        mod_rows(0, j)
                        mod_columns(0, j)
                pe.wait_ge(sem(f"params{l}_in"), 16 * 7)
                ps, ready = take(pe, ("taps", l))
                pe.transpose(ps[:, 0:60], convrow[:, l * P:(l + 1) * P], c("ident")[0:60, 0:60]).then_inc(ready, 1)
                transpose_x(l, 0)

                for m in range(12):
                    ps, ready = take(pe, ("qkv", l, m))
                    slot = arrived(pe, ("qkv", l, m // 4))
                    for k in range(KC):
                        mm = pe.matmul(ps[:, 0:TOK], ring_in[slot][:, k, m % 4 * P:(m % 4 + 1) * P],
                                       xtv[:, k, :], start=(k == 0), stop=(k == KC - 1))
                    mm.then_inc(ready, 1)
                    chunk_end["qkv", l, m // 4] = ("qkv", l, m)
                ps, ready = take(pe, ("ba", l))
                for t in range(T):
                    for k in range(KC):
                        mm = pe.matmul(ps[:, t * 16:(t + 1) * 16], xtv[:, k, t * P:(t + 1) * P],
                                       smv[:, l, k, 0:16], start=(k == 0), stop=(k == KC - 1))
                mm.then_inc(ready, 1)
                ps, ready = take(pe, ("lr", l))
                for k in range(KC):
                    mm = pe.matmul(ps[0:32, 0:TOK], smv[:, l, k, 16:48], xtv[:, k, :],
                                   start=(k == 0), stop=(k == KC - 1))
                mm.then_inc(ready, 1)
                ps, ready = take(pe, ("ss", l))
                for m in range(8):
                    pe.wait_ge(sem("squares"), l * 8 + m + 1)
                    pe.matmul(ps[0:8, 0:CW], c("unit", 7 - m, 15 - m), square(m), start=(m == 0), stop=(m == 7))\
                        .then_inc(ready if m == 7 else sem("squares_summed"), 1)
                slot = arrived(pe, ("z", l, 0))
                tokens_product("z", l, lambda k: ring_in[slot][:, k, :])
                chunk_end["z", l, 0] = ("z", l, T - 1)

                for m in range(8):
                    ps, ready = take(pe, ("norm", l, m))
                    if m == 0:
                        pe.wait_ge(sem("norms_inverse"), l + 1)
                    pe.matmul(ps[:, 0:CW], c("ident")[0:8, m:m + 1].broadcast_to([8, P]), u_gdn[0:8, 1552:1552 + CW],
                              start=True, stop=True).then_inc(ready, 1)
                ps, ready = take(pe, ("gc", l))
                pe.wait_ge(sem("log_decay"), l + 1)
                for t in range(T):
                    for d in range(DIR):
                        at = t * 8 + d * 4
                        pe.matmul(ps[:, at:at + 4], c(f"tri{d}"), col(GG + at, 4), start=True, stop=True)
                pe.matmul(ps[:, 32:56], c("ones"), col(GG, 24), start=True, stop=True).then_inc(ready, 1)
                gate_rows(l, 0)
                mod_rows(l, 6)
                drained(pe, ("norm", l, 7))
                for t in range(T):
                    for n, first in (("k", 4), ("v", 8)):
                        ps, ready = take(pe, (n + "tok", l, t))
                        for h in range(H):
                            mm = pe.transpose(ps[:, h * P:(h + 1) * P], qk[:, first + h, COL[t]:COL[t] + P],
                                              c("ident"))
                        mm.then_inc(ready, 1)

                def heads(ps, lhs, rhs, ready):
                    for h in range(H):
                        mm = pe.matmul(ps[:, h * P:(h + 1) * P], lhs(h), rhs(h), start=True, stop=True)
                    mm.then_inc(ready, 1)

                for p, tiles in enumerate(PAIRS):
                    for d, t in enumerate(tiles):
                        n = batch(l, p, d)
                        k_t = lambda h, t=t: qk[:, 4 + h, COL[t]:COL[t] + P]
                        q_t = lambda h, t=t: qk[:, h, COL[t]:COL[t] + P]
                        ps, ready = take(pe, ("gcrow", n))
                        pe.wait_ge(sem("gdn_rows"), n + 1)
                        pe.matmul(ps[:, :], c("ones"), gd(d, "y"), start=True, stop=True).then_inc(ready, 1)
                        ps, ready = take(pe, ("brow", n))
                        pe.matmul(ps[:, :], c("ones"), gd(d, "m"), start=True, stop=True).then_inc(ready, 1)
                        ps, ready = take(pe, ("qk", n))
                        heads(ps, k_t, q_t, ready)
                        ps, ready = take(pe, ("kk", n))
                        heads(ps, k_t, k_t, ready)
                    mod_columns(l, 6 + p)
                    mod_rows(l, 7 + p)
                    for d, t in enumerate(tiles):
                        n = batch(l, p, d)
                        ps, ready = take(pe, ("x0", n))
                        pe.wait_ge(sem("inv_start"), n + 1)
                        for h in range(H):
                            mm = pe.transpose(ps[:, h * P:(h + 1) * P], gd(d, "xt", h), c("ident"))
                        mm.then_inc(ready, 1)
                    for v in range(1, LEVELS):
                        for d, t in enumerate(tiles):
                            n = batch(l, p, d)
                            ps, ready = take(pe, ("y", n, v))
                            pe.wait_ge(sem("level_part"), level_count(l, p, d, v))
                            if v == 1:
                                drained(pe, ("x0", n))
                            else:
                                drained(pe, ("xty", n, v - 1))
                            heads(ps, lambda h: gd(d, "m", h), lambda h: gd(d, "x", h), ready)
                        for d, t in enumerate(tiles):
                            n = batch(l, p, d)
                            if v < LEVELS - 1:
                                ps, ready = take(pe, ("xy", n, v))
                                drained(pe, ("y", n, v))
                                heads(ps, lambda h: gd(d, "xt", h), lambda h: gd(d, "y", h), ready)
                            ps, ready = take(pe, ("xty", n, v))
                            if v == LEVELS - 1:
                                drained(pe, ("y", n, v))
                            heads(ps, lambda h: gd(d, "y", h), lambda h: gd(d, "xt", h), ready)
                    for d, t in enumerate(tiles):
                        n = batch(l, p, d)
                        if p:
                            state = lambda h, d=d: s_gdn[:, d * W5 + h * P:d * W5 + (h + 1) * P]
                            ps, ready = take(pe, ("ks", n))
                            if p == 1:
                                pe.wait_ge(sem("gdn_state_in"), 32 * (l + 1))
                            else:
                                drained(pe, ("ds", batch(l, 1, d)))
                            heads(ps, lambda h: qk[:, 4 + h, COL[t]:COL[t] + P], state, ready)
                            ps, ready = take(pe, ("qs", n))
                            heads(ps, lambda h: qk[:, h, COL[t]:COL[t] + P], state, ready)
                    for d, t in enumerate(tiles):
                        n = batch(l, p, d)
                        ps, ready = take(pe, ("vnew", n))
                        pe.wait_ge(sem("gdn_rhs"), n + 1)
                        drained(pe, ("xty", n, LEVELS - 1))
                        heads(ps, lambda h: gd(d, "xt", h), lambda h: gd(d, "y", h), ready)
                    for d, t in enumerate(tiles):
                        n = batch(l, p, d)
                        ps, ready = take(pe, ("av", n))
                        drained(pe, ("vnew", n))
                        heads(ps, lambda h: gd(d, "a", h), lambda h: gd(d, "x", h), ready)
                        if p < 2:
                            ps, ready = take(pe, ("ds", n))
                            heads(ps, lambda h: ktok[:, t, h * P:(h + 1) * P], lambda h: gd(d, "m", h), ready)
                mod_columns(l, 9)
                mod_rows(l, 10)
                slot = arrived(pe, ("gqk", l, 0))
                tokens_product("gqk", l, lambda k: ring_in[slot][:, k, :])
                chunk_end["gqk", l, 0] = ("gqk", l, T - 1)
                finish_branch(l, 0)

                slot = arrived(pe, ("gv", l, 0))
                tokens_product("gv", l, lambda k: ring_in[slot][:, k, :])
                chunk_end["gv", l, 0] = ("gv", l, T - 1)
                for t in range(T):
                    ps, ready = take(pe, ("glog", l, t))
                    if t == 0:
                        drained(pe, ("lr", l))
                        pe.wait_ge(sem("fixed_set"), 1)
                    pe.matmul(ps[:, :], lrt[0:33, t * P:(t + 1) * P], wgate[0:33, l * W5:(l + 1) * W5],
                              start=True, stop=True).then_inc(ready, 1)
                slot = arrived(pe, ("r", l, 0))
                tokens_product("r", l, lambda k: ring_in[slot][:, k, :])
                chunk_end["r", l, 0] = ("r", l, T - 1)
                for p, tiles in enumerate(PAIRS):
                    for name in ("rel", "sum", "tail"):
                        ps, ready = take(pe, ("gla_" + name, l, p))
                        if name == "rel" and p == 0:
                            drained(pe, ("glog", l, T - 1))
                        for d, t in enumerate(tiles):
                            mm = pe.matmul(ps[:, d * 256:(d + 1) * 256], c(f"{name}{d}"), glog(t, d),
                                           start=True, stop=True)
                        mm.then_inc(ready, 1)
                    ps, ready = take(pe, ("gla_gt", l, p))
                    for d, t in enumerate(tiles):
                        for hp in range(2):
                            at = (d * 2 + hp) * 2
                            mm = pe.matmul(ps[:, at:at + 2], glog(t, d)[:, hp * P:(hp + 1) * P], c("chunks"),
                                           start=True, stop=True)
                    mm.then_inc(ready, 1)
                    for i, name in enumerate(("q_in", "k_in", "q_dec")):
                        ps, ready = take(pe, (name, l, p))
                        pe.wait_ge(sem("gla_decayed"), (l * 3 + p) * 4 + i + 1)
                        for d in range(DIR):
                            for hp in range(2):
                                at = (d * 2 + hp) * P
                                mm = pe.transpose(ps[:, at:at + P], gl(name)[:, at:at + P], c("ident"))
                        mm.then_inc(ready, 1)
                    for d, t in enumerate(tiles):
                        ps, ready = take(pe, ("gla_a", l, p, d))
                        if d == 0:
                            drained(pe, ("q_in", l, p))
                            drained(pe, ("k_in", l, p))
                        for h in range(H):
                            hp, par_ = h // 2, h % 2
                            mm = pe.matmul(ps[:, h * P:(h + 1) * P], gl_k[:, (d * 2 + hp) * P:(d * 2 + hp + 1) * P], gl_qz[:, par_ * W5 + (d * 2 + hp) * P:par_ * W5 + (d * 2 + hp + 1) * P],
                                           start=True, stop=True)
                        mm.then_inc(ready, 1)
                    for d, t in enumerate(tiles):
                        ps, ready = take(pe, ("gla_av", l, p, d))
                        drained(pe, ("gla_a", l, p, d))
                        for h in range(H):
                            mm = pe.matmul(ps[:, h * P:(h + 1) * P], gla_at(d)[:, h * P:(h + 1) * P],
                                           gvv[:, t, h * P:(h + 1) * P], start=True, stop=True)
                        mm.then_inc(ready, 1)
                    for step in range(2):
                        for d, t in enumerate(tiles):
                            ch = step if d == 0 else 1 - step
                            tok = slice(ch * HALF, (ch + 1) * HALF)
                            ps, ready = take(pe, ("gla_inter", l, p, d, step))
                            if step == 0 and d == 0:
                                drained(pe, ("q_dec", l, p))
                            if step == 1:
                                drained(pe, ("gla_ds", l, p, d, 0))
                            elif p == 1 and d == 0:
                                pe.wait_ge(sem("gla_state_in"), 64 * (l + 1))
                            elif p == 2:
                                drained(pe, ("gla_ds", l, 1, d, 1))
                            elif d == 0:
                                pe.wait_ge(sem("gla_zeroed"), l + 1)
                            for hp in range(2):
                                at = (d * 2 + hp) * P
                                mm = pe.matmul(ps[tok, hp * 256:(hp + 1) * 256], gl_dec[:, at + ch * HALF:at + (ch + 1) * HALF],
                                               gla_state(p, d)[:, hp * 256:(hp + 1) * 256], start=True, stop=True)
                            mm.then_inc(ready, 1)
                            if p == 2 and step == 1:
                                continue
                            ps, ready = take(pe, ("gla_ds", l, p, d, step))
                            if step == 0 and d == 0:
                                pe.wait_ge(sem("gla_decayed"), (l * 3 + p) * 4 + 4)
                            for hp in range(2):
                                at = (d * 2 + hp) * P
                                mm = pe.matmul(ps[:, hp * 256:(hp + 1) * 256], gl("k_tail")[tok, at:at + P],
                                               gvv[tok, t, hp * 256:(hp + 1) * 256], start=True, stop=True)
                            mm.then_inc(ready, 1)
                mod_columns(l, 10)
                mod_rows(l, 11)
                slot = arrived(pe, ("dq", l, 0))
                tokens_product("dq", l, lambda k: ring_in[slot][:, k, :])
                chunk_end["dq", l, 0] = ("dq", l, T - 1)
                finish_branch(l, 1)

                for name in ("dk", "dv"):
                    slot = arrived(pe, (name, l, 0))
                    tokens_product(name, l, lambda k: ring_in[slot][:, k, :])
                    chunk_end[name, l, 0] = (name, l, T - 1)
                mod_columns(l, 11)
                if l + 1 < DEPTH:
                    mod_rows(l + 1, 0)
                for t in range(T + 1):
                    ps, ready = take(pe, ("kt", l, t))
                    if t == T:
                        pe.wait_ge(sem("cache_in"), 32 * (l + 1))
                    elif t:
                        pe.wait_ge(sem("roped"), (l * 2 + t - 1) * 2 + 2)
                    else:
                        drained(pe, ("dk", l, 0))
                    for h in range(H):
                        src = ckv[:, h * P:(h + 1) * P] if t == T else dkv[:, t, h * P:(h + 1) * P]
                        mm = pe.transpose(ps[:, h * P:(h + 1) * P], src, c("ident"))
                    mm.then_inc(ready, 1)
                for t in range(T):
                    ps, ready = take(pe, ("qt", l, t))
                    if t == 0:
                        drained(pe, ("dq", l, 0))
                    for h in range(H):
                        mm = pe.transpose(ps[:, h * P:(h + 1) * P], dqv[:, t, h * P:(h + 1) * P], c("ident"))
                    mm.then_inc(ready, 1)
                    lo, hi = (0, P) if t == 0 else (P, P + KEYS)
                    tiles_k = [0] if t == 0 else [1, 2, 3]
                    for hh in range(H + 1):
                        if hh < H:
                            for s in range(2):
                                ps, ready = take(pe, ("sc", l, t, hh, s))
                                if hh == 0 and s == 0:
                                    drained(pe, ("qt", l, t))
                                    drained(pe, ("kt", l, T))
                                pe.matmul(ps[:, 0:hi - lo], dq_z(s, hh), dk_all[:, hh, :][:, lo:hi],
                                          start=True, stop=True).then_inc(ready, 1)
                        if l + 1 < DEPTH and hh == 1:
                            mod_columns(l + 1, t)
                            mod_rows(l + 1, t + 1)
                        if hh == 0:
                            continue
                        h = hh - 1
                        n = (l * T + t) * H + h
                        ps, ready = take(pe, ("wt", l, t, h))
                        pe.wait_ge(sem("attn_weights"), n + 1)
                        for i in range(len(tiles_k)):
                            mm = pe.transpose(ps[:, i * P:(i + 1) * P], dw(n % 2)[:, i * P:(i + 1) * P], c("ident"))
                        mm.then_inc(ready, 1)
                        ps, ready = take(pe, ("att", l, t, h))
                        drained(pe, ("wt", l, t, h))
                        for i, kt in enumerate(tiles_k):
                            val = ckv[:, W5 + h * P:W5 + (h + 1) * P] if kt == 3 else dvv[:, kt, h * P:(h + 1) * P]
                            mm = pe.matmul(ps[:, 0:P], dwt(n % 2)[:, i * P:(i + 1) * P], val,
                                           start=(i == 0), stop=(i == len(tiles_k) - 1))
                        mm.then_inc(ready, 1)
                if l + 1 < DEPTH:
                    mod_columns(l + 1, 3)
                    mod_rows(l + 1, 4)

                for s in range(3):
                    for half in range(2):
                        slot = arrived(pe, ("merge", l, 2 * s + half))
                        tokens_product(("mergel", 2 * s + half), l, lambda k: ring_in[slot][:, k, :])
                        chunk_end["merge", l, 2 * s + half] = (("mergel", 2 * s + half), l, T - 1)
                        if s == half == 0:
                            finish_branch(l, 2)
                            if l + 1 < DEPTH:
                                mod_columns(l + 1, 4)
                                mod_rows(l + 1, 5)
                    if s == 0 and l + 1 < DEPTH:
                        mod_columns(l + 1, 5)
                    slot = arrived(pe, ("branch", l, s))
                    drained(pe, ("ot", l, s, H - 1))
                    for t in range(T):
                        for half in range(2):
                            ps, ready = take(pe, ("branch", l, s, t, half))
                            for h in range(H):
                                mm = pe.matmul(ps[:, :], ot[:, s * 4 + h, t * P:(t + 1) * P],
                                               ring_dn[slot][:, h, half * W5:(half + 1) * W5],
                                               start=(h == 0), stop=(h == H - 1))
                            mm.then_inc(ready, 1)
                    chunk_end["branch", l, s] = ("branch", l, s, T - 1, 1)
                for k in range(KC):
                    ps, ready = take(pe, ("mixt", l, k))
                    if k == 0:
                        drained(pe, ("branch", l, 2, T - 1, 1))
                        pe.wait_ge(sem("mixed"), l + 1)
                    for t in range(T):
                        mm = pe.transpose(ps[:, t * P:(t + 1) * P], mix[:, t, k * P:(k + 1) * P], c("ident"))
                    mm.then_inc(ready, 1)
                drained(pe, ("mixt", l, KC - 1))
                for half in range(2):
                    slot = arrived(pe, ("out", l, half))
                    tokens_product(("outl", half), l, lambda k: ring_in[slot][:, k, :])
                    chunk_end["out", l, half] = (("outl", half), l, T - 1)

                gate_rows(l, 1)

                transpose_x(l, 1)
                ps, ready = take(pe, ("router", l))
                pe.wait_ge(sem("router_in"), 32)
                for t in range(T):
                    for k in range(KC):
                        mm = pe.matmul(ps[:, t * E:(t + 1) * E], xtv[:, k, t * P:(t + 1) * P], rtv[:, k, :],
                                       start=(k == 0), stop=(k == KC - 1))
                mm.then_inc(ready, 1)

                for t in range(T):
                    for half in range(2):
                        ps, ready = take(pe, ("htok", l, t, half))
                        for k in range(4):
                            mm = pe.transpose(ps[:, k * P:(k + 1) * P], xtv[:, half * 4 + k, t * P:(t + 1) * P], c("ident"))
                        mm.then_inc(ready, 1)
                drained(pe, ("htok", l, T - 1, 1))
                ps, ready = take(pe, ("places", l))
                pe.wait_ge(sem("chosen"), l + 1)
                for t in range(T):
                    for t2 in range(t + 1):
                        pe.matmul(ps[:, t * E:(t + 1) * E], c("tri0" if t2 == t else "ones"),
                                  chosen[:, t2 * E:(t2 + 1) * E], start=(t2 == 0), stop=(t2 == t))
                for t in range(T):
                    mm = pe.matmul(ps[:, T * E:(T + 1) * E], c("ones"), chosen[:, t * E:(t + 1) * E],
                                   start=(t == 0), stop=(t == T - 1))
                mm.then_inc(ready, 1)

                dense_end.append(len(order))
                first_slot = dense_end[l] % RING
                for b in range(7):
                    pe.wait_ge(bank_free[b], filled[b])
                pe.wait_ge(sem("mod_out"), min(l * 2 + 3, DEPTH * 2))
                turns, before = listed(pe, l)

                def chunk(q, j):
                    pe.wait_ge(sem(f"expert_chunk{j % RING}_in"), q * 64 + 32 * (j // RING + 1))
                    slot = (first_slot + j) % RING
                    return ring[:, slot * CHUNK_W:(slot + 1) * CHUNK_W].rearrange("p (u k n) -> p u k n", u=2, k=4)

                def gather(q):
                    pe.wait_ge(sem("hot"), q + (l + 1))
                    for half, b in enumerate(EXPERT_BANKS["gather"]):
                        for k in range(4):
                            for t in range(T):
                                at = (half * 4 + k) * P
                                mm = pe.matmul(banks[b][:, k * P:(k + 1) * P], htok[:, t, at:at + P],
                                               hot[:, t, :, :].rearrange("p u s -> p (u s)"), start=(t == 0), stop=(t == T - 1))
                        mm.then_inc(sem("expert_gather_full"), 1)

                def hidden(q, name, first_chunk):
                    ps = banks[EXPERT_BANKS[name][0]]
                    for part in range(2):
                        w = chunk(q, first_chunk + part)
                        for k in range(4):
                            for u in range(2):
                                at = (part * 4 + k) * P + u * SLOTS
                                mm = pe.matmul(ps[u * SLOTS:(u + 1) * SLOTS, :], xg[:, at:at + SLOTS], w[:, u, k, :],
                                               start=(part == k == 0), stop=(part == 1 and k == 3))
                        mm.then_inc(sem("expert_chunk_used") if part == 0 else sem(f"expert_{name}_full"), 1)

                def turned(q):
                    used(pe, "up", q)
                    ps = banks[EXPERT_BANKS["turned"][0]]
                    for m in range(4):
                        mm = pe.transpose(ps[:, m * P:(m + 1) * P], hact[:, m * P:(m + 1) * P], c("ident"))
                    mm.then_inc(sem("expert_turned_full"), 1)

                def choice(q):
                    pe.wait_ge(sem("hot_gated"), q + 1)
                    ps = banks[EXPERT_BANKS["choice"][0]]
                    for t in range(T):
                        mm = pe.transpose(ps[:, t * P:(t + 1) * P], hotg[:, t, :, :].rearrange("p u s -> p (u s)"), c("ident"))
                    mm.then_inc(sem("expert_choice_full"), 1)

                def output(q):
                    used(pe, "turned", q)
                    for half in range(2):
                        w = chunk(q, 4 + half)
                        for m in range(4):
                            for u in range(2):
                                at = m * P + u * SLOTS
                                mm = pe.matmul(banks[EXPERT_BANKS["out"][half]][u * SLOTS:(u + 1) * SLOTS, :], ht[:, at:at + SLOTS],
                                               w[:, u, m, :], start=(m == 0), stop=(m == 3))
                        mm.then_inc(sem("expert_out_full"), 1)

                def back(q, bank_wait):
                    used(pe, "choice", q)
                    used(pe, "out", q, 1)
                    for k in range(2 * T):
                        bank_wait(k)
                        pe.matmul(banks[EXPERT_BANKS["back"][k]][:, :], hott[:, k // 2 * P:(k // 2 + 1) * P],
                                  oe[:, k % 2 * W5:(k % 2 + 1) * W5], start=True, stop=True)\
                            .then_inc(sem("expert_back_full"), 1)

                gather(before)
                used(pe, "gather", before + l, 1)
                hidden(before, "gate", 0)
                hidden(before, "up", 2)
                gather(before + 1)
                turned(before)
                used(pe, "gather", before + (l + 1), 1)
                choice(before)
                with pe.Fori(0, turns) as i:
                    n = i + before
                    added(pe, n, 2)
                    output(n)
                    used(pe, "gather", n + (l + 1), 1)
                    added(pe, n, 3)
                    hidden(n + 1, "gate", 0)
                    added(pe, n, 4)
                    hidden(n + 1, "up", 2)
                    added(pe, n, 5)
                    used(pe, "choice", n)
                    gather(n + 2)
                    turned(n + 1)

                    def bank_wait(k):
                        if k == 0:
                            added(pe, n, 0)
                        elif k == 3:
                            used(pe, "gate", n + 1)
                        elif k == 4:
                            used(pe, "up", n + 1)
                        elif k == 5:
                            used(pe, "gather", n + (l + 2), 0)
                    back(n, bank_wait)
                    used(pe, "gather", n + (l + 2), 1)
                    choice(n + 1)
                last = turns + before
                added(pe, last, 2)
                output(last)
                back(last, lambda k: added(pe, last, k))
                used(pe, "back", last, 2 * T - 1)
                pe.sem_inc(sem("experts_done"), 1)

        @block.sync
        def _(sp):
            sp.dma_start(cst[:, :], consts).then_inc(sem("consts_in"), 16)
            sp.dma_start(crow[0:8, :], a["c_ctx"].rearrange("(k p) -> k p", p=P)).then_inc(sem("cond_in"), 16)
            sp.dma_start(crow[8:16, :], a["c"].rearrange("b (k p) -> (b k) p", p=P)).then_inc(sem("cond_in"), 16)
            sp.dma_start(xv[:, 0, :], a["x_prompt"][0]).then_inc(sem("x_in"), 16)
            sp.dma_start(xv[:, 1:3, :], a["x_sample"][0].rearrange("(t p) d -> p t d", p=P)).then_inc(sem("x_in"), 16)

            sp.dma_start(otok[0:96, 0:P], a["b_mod"].rearrange("l (j p) -> (l j) p", p=P)).then_inc(sem("mod_bias_in"), 16)

            rows = lambda w: w.rearrange("(k p) n -> p k n", p=P)
            source = {
                "mod": lambda l, j: rows(a["w_mod"][l])[:, :, j * W5:(j + 1) * W5],
                "qkv": lambda l, j: rows(a["w_in"][l])[:, :, j * W5:(j + 1) * W5],
                "merge": lambda l, j: rows(a["w_in"][l])[:, :, IN_COL["merge"] + j * W5:IN_COL["merge"] + (j + 1) * W5],
                "out": lambda l, j: rows(a["w_out"][l])[:, :, j * W5:(j + 1) * W5],
                "branch": lambda l, s: a["w_branch"][l, s].rearrange("(m p) n -> p m n", p=P),
            }
            for name in ("gqk", "gv", "z", "r", "dq", "dk", "dv"):
                source[name] = lambda l, j, name=name: rows(a["w_in"][l])[:, :, IN_COL[name]:IN_COL[name] + W5]

            def load(key):
                name, l, j = key
                slot = place[key] % RING
                sp.dma_start((ring_dn if name == "branch" else ring_in)[slot], source[name](l, j)).then_inc(slot_in[slot], 16)

            def load_pair(l, j, experts):
                slot = (dense_end[l] + j) % RING
                for u, e in enumerate(experts):
                    part = j % 2
                    if j < 4:
                        src = rows(a["exp_w_gate" if j < 2 else "exp_w_up"][l, e])[:, part * 4:(part + 1) * 4, :]
                    else:
                        src = rows(a["exp_w_down"][l, e])[:, :, part * W5:(part + 1) * W5]
                    at = slot * CHUNK_W + u * CHUNK_W // 2
                    sp.dma_start(ring[:, at:at + CHUNK_W // 2].rearrange("p (k n) -> p k n", k=4), src)\
                        .then_inc(sem(f"expert_chunk{j % RING}_in"), 16)

            def pair_used(j, q):
                if j == 0:
                    sp.wait_ge(sem("expert_up_full"), q + 1)
                elif j in (1, 2):
                    sp.wait_ge(sem("expert_out_full"), q * 2 + j)
                elif j == 4:
                    sp.wait_ge(sem("expert_gate_full"), q + 1)
                else:
                    sp.wait_ge(sem("expert_chunk_used"), q * 2 + (1 if j == 3 else 2))

            def reusable(n):
                full(sp, chunk_end[order[n]])

            for l in range(DEPTH):
                first = dense_end[l - 1] if l else 0
                for n in range(first, dense_end[l]):
                    if l and n < first + RING:
                        pair_used(n - first, last)
                    elif n >= RING:
                        reusable(n - RING)
                    load(order[n])
                for j in range(RING):
                    reusable(dense_end[l] - RING + j)
                    load_pair(l, j, (0, 1))
                turns, before = listed(sp, l)
                for j in range(RING, 6):
                    pair_used(j, before)
                    load_pair(l, j, (0, 1))
                with sp.Fori(0, turns) as i:
                    n = i + before
                    experts = [sp.value_load(jobs[0:1, bass.ds(i * 2 + (W_AT + 2 + u), 1)], min_val=0, max_val=E - 1)
                               for u in range(2)]
                    for j in range(6):
                        pair_used(j, n if j < RING else n + 1)
                        load_pair(l, j, experts)
                last = turns + before
            sp.wait_ge(sem("experts_done"), DEPTH)

        @block.gpsimd
        def _(pool):
            steps = [0]

            def link(ins):
                steps[0] += 1
                ins.then_inc(sem("pool_steps"), 1)
                pool.wait_ge(sem("pool_steps"), steps[0])

            for l in range(DEPTH):
                pin = sem(f"params{l}_in")
                pool.dma_start(smv[:, l, :, 0:16], a["w_in"][l, :, IN_COL["ba"]:IN_COL["ba"] + 16].rearrange("(k p) n -> p k n", p=P)).then_inc(pin, 16)
                pool.dma_start(smv[:, l, :, 16:48], a["w_in"][l, :, IN_COL["lr"]:IN_COL["lr"] + 32].rearrange("(k p) n -> p k n", p=P)).then_inc(pin, 16)
                pool.dma_start(convrow[:, l * P:(l + 1) * P], a["gdn_conv"][l].rearrange("k (c p) -> (k c) p", p=P)).then_inc(pin, 16)
                at = l * 656
                for name, w in (("gdn_a_log", 8), ("gdn_dt_bias", 8)):
                    pool.dma_start(par[:, at:at + w], a[name][l].rearrange("d h -> (d h)").partition_broadcast(P)).then_inc(pin, 16)
                    at += w
                at = l * 656 + 16 + 384
                pool.dma_start(par[:, at:at + 256], a["diff_lambda"][l].rearrange("s d -> (s d)").partition_broadcast(P)).then_inc(pin, 16)
                pool.dma_start(wgate[32:33, l * W5:(l + 1) * W5], a["gla_b_gate"][l].rearrange("(o d) k -> o (d k)", o=1)).then_inc(pin, 16)
                at = l * 656 + 16
                for name in ("gdn_norm", "gla_norm", "diff_norm"):
                    pool.dma_start(par[:, at:at + 128], a[name][l].partition_broadcast(P)).then_inc(sem("norms_in"), 16)
                    at += 128
            pool.dma_start(rtv, a["router_w"].rearrange("(k p) e -> p k e", p=P)).then_inc(sem("router_in"), 16)
            pool.dma_start(rbias[:, :], a["router_b"].partition_broadcast(P)).then_inc(sem("router_in"), 16)
            link(pool.memset(wgate[0:32, :], 0.0))
            for l in range(DEPTH):
                for d in range(DIR):
                    pool.dma_start(wgate[d * RANK:(d + 1) * RANK, l * W5 + d * 256:l * W5 + (d + 1) * 256],
                                   a["gla_w_gate"][l, d]).then_inc(sem("gate_w_in"), 16)
            link(pool.memset(lrt[32:33, :], 1.0))
            link(pool.memset(s_gla[:, :], 0.0))
            pool.wait_ge(sem("gate_w_in"), 64)
            link(pool.memset(small[:, 1000:1001], 0.0))
            pool.memset(small[:, 1001:1002], 0.0).then_inc(sem("fixed_set"), 1)
            for l in range(DEPTH):
                if l:
                    pool.wait_ge(sem("experts_done"), l)
                for at in (0, 130, 388):
                    ins = pool.memset(qk[:, :, at:at + 2], 0.0)
                    if at == 388:
                        ins.then_inc(sem("pads"), 1)
                def ln_params(which):
                    if which:
                        pool.wait_ge(sem("x_ready"), (l * 2 + which) * T)
                    else:
                        pool.wait_ge(sem("branch_normed"), l * 3 + 3)
                    for i, name in enumerate(("ln_g", "ln_b")):
                        pool.dma_start(lnp[:, i * D:(i + 1) * D], a[name][l, which].partition_broadcast(P)).then_inc(sem("ln_in"), 16)
                for m in range(8):
                    pool.wait_ge(sem("silu_done"), l * 12 + m + 1)
                    if m > 1:
                        pool.wait_ge(sem("squares_summed"), l * 7 + m - 1)
                    pool.tensor_tensor(square(m), qk[:, m, 0:CW], qk[:, m, 0:CW], ALU.mult)\
                        .then_inc(sem("squares"), 1)
                def scale_gate(i):
                    name, v, at = (("z", zv, 16), ("r", rv, 144))[i]
                    if i == 0 and l == 0:
                        pool.wait_ge(sem("norms_in"), 16 * 3 * DEPTH)
                    drained(pool, (name, l, T - 1))
                    vv = v.rearrange("p t (h w) -> p (t h) w", h=H)
                    pool.tensor_tensor(vv, vv, fan(par[:, l * 656 + at:l * 656 + at + P], T * H), ALU.mult)\
                        .then_inc(sem("gates_scaled"), 1)
                scale_gate(0)
                if l:
                    for d in range(DIR):
                        full(pool, ("qs", batch(l - 1, 2, d)))
                for d in range(DIR):
                    pool.dma_start(s_gdn[:, d * W5:(d + 1) * W5].rearrange("p (h e) -> p h e", h=H),
                                   a["state_gdn"][0, l, d].rearrange("h d e -> d h e")).then_inc(sem("gdn_state_in"), 16)
                for p, tiles in enumerate(PAIRS):
                    for d, t in enumerate(tiles):
                        n = batch(l, p, d)
                        if p == 0 and d == 0:
                            pool.wait_ge(sem("log_decay"), l + 1)
                            drained(pool, ("norm", l, 7))
                        if p:
                            m = batch(l, p - 1, d)
                            full(pool, ("av", m))
                            full(pool, ("ds", m))
                            full(pool, ("vnew", m))
                        pool.tensor_tensor(gd(d, "y").rearrange("p (h i) -> p h i", h=H), fan(c(f"tri{d}"), H),
                                           wide(col(GG + t * 8 + d * 4, 4), P), ALU.mult)
                        pool.tensor_tensor(gd(d, "m").rearrange("p (h i) -> p h i", h=H), fan(c("ident"), H),
                                           wide(col(BETA + t * 8 + d * 4, 4), P), ALU.mult).then_inc(sem("gdn_rows"), 1)
                    for v in range(LEVELS):
                        for d, t in enumerate(tiles):
                            n = batch(l, p, d)
                            if v == 0:
                                drained(pool, ("brow", n))
                            elif v > 1:
                                full(pool, ("y", n, v - 1))
                            else:
                                pool.wait_ge(sem("inv_start"), n + 1)
                            pool.tensor_tensor(gd(d, "m").rearrange("p (h i) -> p h i", h=H),
                                               gd(d, "lt").rearrange("p (h i) -> p h i", h=H),
                                               fan(c(f"level{d}_{v}"), H), ALU.mult).then_inc(sem("level_part"), 1)
                for d in range(DIR):
                    drained(pool, ("ds", batch(l, 0, d)))
                    pool.dma_start(new_gdn[0, l, d].rearrange("h d e -> d h e"),
                                   st_out(d).rearrange("p (h e) -> p h e", h=H)).then_inc(sem("outputs"), 16)
                for d in range(DIR):
                    for hh in range(2):
                        if l:
                            full(pool, ("gla_inter", l - 1, 2, d, 1))
                        rows_ = slice(hh * 64, hh * 64 + 64)
                        pool.dma_start(gla_state(1, d)[rows_, :].rearrange("p (a b e) -> p a b e", a=2, b=2)[:, :, hh, :],
                                       a["state_gla"][0, l, d].rearrange("(a b) k e -> b k a e", b=2)[hh])\
                            .then_inc(sem("gla_state_in"), 16)
                pool.wait_ge(sem("outputs"), 32 * (l + 1))
                pool.wait_ge(sem("branch_normed"), l * 3 + 1)
                link(pool.memset(gla_at(0), 0.0))
                link(pool.memset(gla_at(1), 0.0))
                link(pool.memset(gl_qz, 0.0))
                pool.memset(s_gla[:, 0:2 * W5], 0.0).then_inc(sem("gla_zeroed"), 1)
                scale_gate(1)
                for d in range(DIR):
                    drained(pool, ("gla_ds", l, 0, d, 1))
                    for hh in range(2):
                        rows_ = slice(hh * 64, hh * 64 + 64)
                        pool.dma_start(new_gla[0, l, d].rearrange("(a b) k e -> b k a e", b=2)[hh],
                                       gla_state(0, d)[rows_, :].rearrange("p (a b e) -> p a b e", a=2, b=2)[:, :, hh, :])\
                            .then_inc(sem("gla_out"), 16)
                pool.wait_ge(sem("branch_normed"), l * 3 + 2)
                pool.memset(u_att[:, 0:2 * W5], 0.0).then_inc(sem("dq_zeroed"), 1)
                pool.dma_start(ckv[:, 0:W5], a["cache_k"][0, l].rearrange("s h d -> s (h d)")).then_inc(sem("cache_in"), 16)
                pool.dma_start(ckv[:, W5:], a["cache_v"][0, l].rearrange("s h d -> s (h d)")).then_inc(sem("cache_in"), 16)
                for name, v, dst in (("dk", dkv, new_k), ("dv", dvv, new_v)):
                    drained(pool, (name, l, 0))
                    pool.dma_start(dst[0, l].rearrange("s h d -> s (h d)"), v[:, 0, :]).then_inc(sem("kv_out"), 16)
                ln_params(0)
                ln_params(1)
            pool.wait_ge(sem("x_ready"), DEPTH * 2 * T)
            pool.dma_start(y_prompt[0], xv[:, 0, :]).then_inc(sem("outputs"), 16)
            pool.dma_start(y_sample[0].rearrange("(t p) d -> p t d", p=P), xv[:, 1:3, :]).then_inc(sem("outputs"), 16)
            pool.wait_ge(sem("outputs"), 16 * (2 * DEPTH + 2))
            pool.wait_ge(sem("kv_out"), 32 * DEPTH)
            pool.wait_ge(sem("gla_out"), 64 * DEPTH)

        @block.scalar
        def _(act):
            steps = [0]

            def link(ins):
                steps[0] += 1
                ins.then_inc(sem("act_steps"), 1)
                act.wait_ge(sem("act_steps"), steps[0])

            def root(at, n, name, k):
                act.wait_ge(sem(name + "_var"), k)
                act.activation(col(at, n), col(at, n), ACT.Sqrt).then_inc(sem(name + "_std"), 1)

            def gates_out(l, which):
                if which:
                    drained(act, (("outl", 1), l, T - 1))
                elif l:
                    act.wait_ge(sem("x_ready"), l * 2 * T)
                for half in range(2):
                    for cond in range(2):
                        ps, free = full(act, ("modg", l, which, half, cond))
                        act.activation(gatev[:, cond, half * W5:(half + 1) * W5], ps[:, :], ACT.Copy).then_inc(free, 1)

            ps, free = full(act, "cond")
            act.wait_ge(sem("condition_padded"), 1)
            act.activation(scol[:, :].rearrange("p (k c) -> p k c", k=KC)[:, :, 0:2], ps[:, 0:16].rearrange("p (c k) -> p k c", c=2),
                           ACT.Silu).then_inc(free, 1)

            def mod_rows_in(l, j):
                ps, free = full(act, ("modrow", l, j))
                act.activation(mrow[:, :], ps[:, :], ACT.Copy).then_inc(free, 1)

            for l in range(DEPTH):
                if l == 0:
                    for j in range(6):
                        mod_rows_in(0, j)
                for m in range(12):
                    ps, free = full(act, ("qkv", l, m))
                    if m == 0:
                        if l:
                            act.wait_ge(sem("mixed"), l)
                        act.wait_ge(sem("pads"), l + 1)
                    act.activation(qk[:, m, 2:2 + SEQ], ps[:, 0:SEQ], ACT.Copy)
                    act.activation(qk[:, m, 4 + SEQ:4 + TOK], ps[:, SEQ:TOK], ACT.Copy).then_inc(free, 1)
                    if m > 1:
                        silu(act, l, m - 2)
                silu(act, l, 10)
                silu(act, l, 11)
                ps, free = full(act, ("ba", l))
                bav = ps[:, 0:48].rearrange("p (t c) -> p t c", t=T)
                act.activation(col(BETA, 24).rearrange("p (t c) -> p t c", t=T), bav[:, :, 0:8], ACT.Sigmoid)
                act.activation(col(AB, 24).rearrange("p (t c) -> p t c", t=T), bav[:, :, 8:16], ACT.Copy).then_inc(free, 1)
                ps, free = full(act, ("lr", l))
                act.activation(lrt[0:32, :], ps[0:32, 0:TOK], ACT.Copy).then_inc(free, 1)
                act.wait_ge(sem("decay_in"), l + 1)
                link(act.activation(col(GC, 24), col(AB, 24), ACT.Abs))
                link(act.activation(col(GC, 24), col(GC, 24), ACT.Exp, scale=-1.0))
                link(act.activation(col(GC, 24), col(GC, 24), ACT.Ln, bias=1.0))
                act.activation(col(EXPA, 8), par[:, l * 656:l * 656 + 8], ACT.Exp).then_inc(sem("softplus_part"), 1)
                ps, free = full(act, ("ss", l))
                act.wait_ge(sem("eps_set"), 1)
                act.activation(u_gdn[0:8, 1552:1552 + CW], ps[0:8, 0:CW], ACT.Sqrt, bias=small[0:8, 1010:1011]).then_inc(free, 1)
                gate_in(act, "z", l, zv)
                act.wait_ge(sem("decay_sums"), l + 1)
                act.activation(col(EGC, 24), col(GC, 24), ACT.Exp)
                act.activation(col(ETOT, 24), col(TOTC, 24), ACT.Exp)
                act.activation(col(ETAIL, 24), col(ETAIL, 24), ACT.Exp).then_inc(sem("decays"), 1)
                gates_out(l, 0)
                mod_rows_in(l, 6)
                for t in range(T):
                    for n, v in (("k", ktok), ("v", vtok)):
                        ps, free = full(act, (n + "tok", l, t))
                        act.activation(v[:, t, :], ps[:, :], ACT.Copy).then_inc(free, 1)
                for p, tiles in enumerate(PAIRS):
                    for d in range(DIR):
                        n = batch(l, p, d)
                        drained(act, ("gcrow", n))
                        act.activation(gd(d, "dt"), gd(d, "dt"), ACT.Exp).then_inc(sem("dt_exp"), 1)
                    mod_rows_in(l, 7 + p)
                    for d in range(DIR):
                        ps, free = full(act, ("x0", batch(l, p, d)))
                        act.activation(gd(d, "x"), ps[:, :], ACT.Copy).then_inc(free, 1)
                    for v in range(1, LEVELS):
                        for d in range(DIR):
                            ps, free = full(act, ("y", batch(l, p, d), v))
                            act.activation(gd(d, "y"), ps[:, :], ACT.Copy).then_inc(free, 1)
                mod_rows_in(l, 10)
                branch_root(act, l, 0)
                branch_ot(act, l, 0)
                for t in range(T):
                    ps, free = full(act, ("gqk", l, t))
                    act.activation(gqkv[:, t, 0:256], ps[:, 0:256], ACT.Copy, scale=GLA_DK ** -0.5)
                    act.activation(gqkv[:, t, 256:512], ps[:, 256:512], ACT.Copy).then_inc(free, 1)
                for t in range(T):
                    ps, free = full(act, ("gv", l, t))
                    act.activation(gvv[:, t, :], ps[:, :], ACT.Copy).then_inc(free, 1)
                for t in range(T):
                    ps, _ = full(act, ("glog", l, t))
                    if t:
                        drained(act, ("glog", l, t - 1))
                    else:
                        act.wait_ge(sem("branch_normed"), l * 3 + 1)
                    link(act.activation(gl_ln, ps[:, :], ACT.Abs))
                    link(act.activation(gl_ln, gl_ln, ACT.Exp, scale=-1.0))
                    act.activation(gl_ln, gl_ln, ACT.Ln, bias=1.0).then_inc(sem("gla_ln"), 1)
                gate_in(act, "r", l, rv)
                for p in range(3):
                    if p:
                        full(act, ("q_dec", l, p - 1))
                        full(act, ("gla_ds", l, p - 1, 1, 1))
                    ps, free = full(act, ("gla_rel", l, p))
                    act.activation(gl("q_in"), ps[:, :], ACT.Exp, scale=1.0 / TAU)
                    act.activation(gl("k_in"), ps[:, :], ACT.Exp, scale=-1.0 / TAU).then_inc(free, 1)
                    ps, free = full(act, ("gla_sum", l, p))
                    act.activation(gl("q_dec"), ps[:, :], ACT.Exp, scale=1.0 / TAU).then_inc(free, 1)
                    ps, free = full(act, ("gla_tail", l, p))
                    act.activation(gl("k_tail"), ps[:, :], ACT.Exp, scale=1.0 / TAU).then_inc(free, 1)
                    ps, free = full(act, ("gla_gt", l, p))
                    act.activation(gla_gt(p), ps[:, 0:8], ACT.Exp, scale=1.0 / TAU).then_inc(free, 1)
                    ps, free = full(act, ("q_in", l, p))
                    if p == 0:
                        act.wait_ge(sem("gla_zeroed"), l + 1)
                    for hh in range(2):
                        ins = act.activation(gl_qz[hh * 64:hh * 64 + 64, hh * W5:(hh + 1) * W5], ps[hh * 64:hh * 64 + 64, :], ACT.Copy)
                    ins.then_inc(free, 1)
                    ps, free = full(act, ("k_in", l, p))
                    act.activation(gl_k, ps[:, :], ACT.Copy).then_inc(free, 1)
                    ps, free = full(act, ("q_dec", l, p))
                    act.activation(gl_dec, ps[:, :], ACT.Copy).then_inc(free, 1)
                mod_rows_in(l, 11)
                branch_root(act, l, 1)
                branch_ot(act, l, 1)
                for name, v in (("dq", dqv), ("dk", dkv), ("dv", dvv)):
                    for t in range(T):
                        ps, free = full(act, (name, l, t))
                        act.activation(v[:, t, :], ps[:, :], ACT.Copy).then_inc(free, 1)
                if l + 1 < DEPTH:
                    mod_rows_in(l + 1, 0)
                act.wait_ge(sem("lam_parts"), l + 1)
                act.activation(col(LAM, 2), col(LAM, 2), ACT.Exp).then_inc(sem("lam_exp"), 1)
                for t in range(T + 1):
                    ps, free = full(act, ("kt", l, t))
                    act.activation(dk_all[:, :, t * P:(t + 1) * P], ps[:, :].rearrange("p (h i) -> p h i", h=H), ACT.Copy).then_inc(free, 1)
                for t in range(T):
                    ps, free = full(act, ("qt", l, t))
                    if t == 0:
                        act.wait_ge(sem("dq_zeroed"), l + 1)
                    else:
                        full(act, ("sc", l, t - 1, H - 1, 1))
                    for s in range(2):
                        ins = act.activation(u_att[s * 64:s * 64 + 64, s * W5:(s + 1) * W5], ps[s * 64:s * 64 + 64, :], ACT.Copy)
                    ins.then_inc(free, 1)
                    nk = P if t == 0 else KEYS
                    for hh in range(H + 1):
                        if hh < H:
                            n = (l * T + t) * H + hh
                            for s in range(2):
                                ps, free = full(act, ("sc", l, t, hh, s))
                                act.wait_ge(sem("neg_max"), 2 * n + s + 1)
                                act.activation(dp(s)[:, 0:nk], ps[:, 0:nk], ACT.Exp, bias=col(NM + s, 1), scale=DH ** -0.5,
                                               accum_out=col(SUMP + s, 1)).then_inc(free, 1)
                        if l + 1 < DEPTH and hh == 1:
                            mod_rows_in(l + 1, t + 1)
                        if hh:
                            n = (l * T + t) * H + hh - 1
                            ps, free = full(act, ("wt", l, t, hh - 1))
                            if n > 1:
                                m = n - 2
                                full(act, ("att", m // (T * H), m // H % T, m % H))
                            act.activation(dwt(n % 2)[:, 0:nk], ps[:, 0:nk], ACT.Copy).then_inc(free, 1)
                if l + 1 < DEPTH:
                    mod_rows_in(l + 1, 4)
                branch_root(act, l, 2)
                branch_ot(act, l, 2)
                for s in range(3):
                    for half in range(2):
                        for t in range(T):
                            ps, free = full(act, (("mergel", 2 * s + half), l, t))
                            if s == half == t == 0:
                                act.wait_ge(sem("kv_out"), 32 * (l + 1))
                            if s and half == 0 and t == 0:
                                drained(act, ("branch", l, s - 1, T - 1, 1))
                            act.activation(mg[:, t, half * W5:(half + 1) * W5], ps[:, :], ACT.Sigmoid).then_inc(free, 1)
                        if s == half == 0 and l + 1 < DEPTH:
                            mod_rows_in(l + 1, 5)
                for k in range(KC):
                    ps, free = full(act, ("mixt", l, k))
                    act.activation(xtv[:, k, :], ps[:, 0:TOK], ACT.Copy).then_inc(free, 1)
                gates_out(l, 1)
                root(RS, T, "ln", l * 2 + 1)
                ps, free = full(act, ("router", l))
                act.activation(col(RTR, 48), ps[:, 0:48], ACT.Sigmoid).then_inc(free, 1)
                for t in range(T):
                    for half in range(2):
                        ps, free = full(act, ("htok", l, t, half))
                        act.activation(htok[:, t, half * W5:(half + 1) * W5], ps[:, :], ACT.Copy).then_inc(free, 1)
                turns, before = listed(act, l)

                def tokens_in(q):
                    for half in range(2):
                        ps, free = made(act, "gather", q + l, half)
                        act.activation(xg[:, half * W5:(half + 1) * W5], ps[:, :], ACT.Copy).then_inc(free, 1)

                def gate_silu(q):
                    ps, free = made(act, "gate", q)
                    act.activation(ag, ps[:, :], ACT.Silu).then_inc(free, 1)

                def turned_in(q):
                    ps, free = made(act, "turned", q)
                    act.activation(ht, ps[:, :], ACT.Copy).then_inc(free, 1)

                def choice_in(q):
                    ps, free = made(act, "choice", q)
                    act.activation(hott, ps[:, 0:TOK], ACT.Copy).then_inc(free, 1)

                def output_in(q):
                    for half in range(2):
                        ps, free = made(act, "out", q, half)
                        act.activation(oe[:, half * W5:(half + 1) * W5], ps[:, :], ACT.Copy).then_inc(free, 1)

                tokens_in(before)
                gate_silu(before)
                tokens_in(before + 1)
                turned_in(before)
                choice_in(before)
                with act.Fori(0, turns) as i:
                    n = i + before
                    output_in(n)
                    gate_silu(n + 1)
                    tokens_in(n + 2)
                    turned_in(n + 1)
                    choice_in(n + 1)
                output_in(turns + before)
                root(RS, T, "ln", l * 2 + 2)

        @block.vector
        def _(dve):
            steps = [0]

            def link(ins):
                steps[0] += 1
                ins.then_inc(sem("dve_steps"), 1)
                dve.wait_ge(sem("dve_steps"), steps[0])

            def layer_norm(l, which):
                n = l * 2 + which
                for t in range(T):
                    for half in range(2):
                        ins = dve.bn_stats(col(ST + half * 6, 6), xv[:, t, half * W5:(half + 1) * W5])
                        link(ins)
                    link(dve.bn_aggr(col(MV + 2 * t, 2), col(ST, 12)))
                    ins = dve.tensor_scalar(col(RS + t, 1), col(MV + 2 * t + 1, 1), EPS, None, ALU.add)
                    if t < T - 1:
                        link(ins)
                ins.then_inc(sem("ln_var"), 1)
                dve.wait_ge(sem("ln_std"), n + 1)
                link(dve.reciprocal(col(RS, T), col(RS, T)))
                dve.wait_ge(sem("ln_in"), 32 * (n + 1))
                for t in range(T):
                    link(dve.tensor_scalar(xv[:, t, :], xv[:, t, :], col(MV + 2 * t, 1), col(RS + t, 1), ALU.subtract, ALU.mult))
                for t in range(T):
                    link(dve.tensor_tensor(xv[:, t, :], xv[:, t, :], lnp[:, 0:D], ALU.mult))
                for t in range(T):
                    dve.tensor_tensor(xv[:, t, :], xv[:, t, :], lnp[:, D:2 * D], ALU.add).then_inc(sem("x_ready"), 1)

            def modulate(l, which):
                shift, scale = (0, 8) if which == 0 else (24, 32)
                dve.wait_ge(sem("mod_out"), l * 2 + which + 1)
                for k in range(KC):
                    ps, free = full(dve, ("xt", l, which, k))
                    dve.tensor_scalar(xtv[:, k, 0:SEQ], ps[:, 0:SEQ], modv[:, l, scale + k, 0:1], modv[:, l, shift + k, 0:1],
                                      ALU.mult, ALU.add)
                    dve.tensor_scalar(xtv[:, k, SEQ:], ps[:, SEQ:TOK], modv[:, l, scale + k, 1:2], modv[:, l, shift + k, 1:2],
                                      ALU.mult, ALU.add).then_inc(free, 1)

            def finish(l, br):
                o12 = otok[:, :].rearrange("p (n w) -> p n w", w=P)
                sq = (u_gdn, u_gla, u_att)[br][:, 0:T * W5]
                link(dve.tensor_tensor(sq, otok[:, :], otok[:, :], ALU.mult))
                link(dve.tensor_reduce(col(SS, 12), sq.rearrange("p (n w) -> p n w", w=P), AX.X, ALU.add))
                dve.tensor_scalar(col(SS, 12), col(SS, 12), 1.0 / P, EPS, ALU.mult, ALU.add).then_inc(sem("branch_var"), 1)
                dve.wait_ge(sem("branch_std"), l * 3 + br + 1)
                link(dve.reciprocal(col(SS, 12), col(SS, 12)))
                if br == 2:
                    link(dve.tensor_scalar(col(SS, 12), col(SS, 12), 1.0 - lam_init(l), None, ALU.mult))
                link(dve.tensor_tensor(o12, o12, wide(col(SS, 12), P), ALU.mult))
                if br < 2:
                    dve.wait_ge(sem("gates_scaled"), l * 2 + br + 1)
                    dve.tensor_tensor(ov, ov, (zv, rv)[br], ALU.mult).then_inc(sem("branch_normed"), 1)
                else:
                    dve.tensor_tensor(o12, o12, fan(par[:, l * 656 + 272:l * 656 + 400], 12), ALU.mult).then_inc(sem("branch_normed"), 1)

            def mod_out(l, which):
                dve.wait_ge(sem("mod_done"), l * 2 + which + 1)
                at = l * 48 + which * 24
                dve.tensor_tensor(modt[:, 2 * at:2 * at + 48].rearrange("p (i c) -> p i c", c=2),
                                  mod_bank[:, 2 * at:2 * at + 48].rearrange("p (i c) -> p i c", c=2),
                                  wide(bcol[:, at:at + 24], 2), ALU.add).then_inc(sem("mod_out"), 1)

            dve.memset(scol[:, :], 0.0).then_inc(sem("condition_padded"), 1)
            ps, free = full(dve, "mod_bias")
            dve.tensor_copy(bcol[:, :], ps[:, 0:96]).then_inc(free, 1)
            drained(dve, "mod_bias")
            for at in (8, 32, 56, 80):
                link(dve.tensor_scalar(bcol[:, at:at + 8], bcol[:, at:at + 8], 1.0, None, ALU.add))
            dve.memset(col(1010, 1), EPS).then_inc(sem("eps_set"), 1)
            for l in range(DEPTH):
                if l == 0:
                    mod_out(0, 0)
                ps, free = full(dve, ("taps", l))
                dve.tensor_copy(convc[:, :], ps[:, 0:60]).then_inc(free, 1)
                drained(dve, ("taps", l))
                modulate(l, 0)
                for m in range(12):
                    tmp = conv_out(m)
                    drained(dve, ("qkv", l, m))
                    if m > 1:
                        dve.wait_ge(sem("silu_done"), l * 12 + m - 1)
                    link(dve.tensor_scalar(tmp, qk[:, m, 0:CW], convc[:, m:m + 1], None, ALU.mult))
                    for k in range(1, TAPS):
                        ins = dve.scalar_tensor_tensor(out=tmp, in0=qk[:, m, k:k + CW], scalar=convc[:, 12 * k + m:12 * k + m + 1],
                                                       in1=tmp, op0=ALU.mult, op1=ALU.add)
                        if k < TAPS - 1:
                            link(ins)
                    ins.then_inc(sem("conv_done"), 1)
                drained(dve, ("ba", l))
                ab3 = col(AB, 24).rearrange("p (t c) -> p t c", t=T)
                dve.tensor_tensor(ab3, ab3, fan(par[:, l * 656 + 8:l * 656 + 16], T), ALU.add).then_inc(sem("decay_in"), 1)
                dve.wait_ge(sem("softplus_part"), l + 1)
                link(dve.scalar_tensor_tensor(out=col(GG, 24), in0=col(AB, 24), scalar=0.0, in1=col(GC, 24), op0=ALU.max, op1=ALU.add))
                link(dve.tensor_scalar(col(EXPA, 8), col(EXPA, 8), -1.0, None, ALU.mult))
                gg3 = col(GG, 24).rearrange("p (t c) -> p t c", t=T)
                dve.tensor_tensor(gg3, gg3, fan(col(EXPA, 8), T), ALU.mult).then_inc(sem("log_decay"), 1)
                drained(dve, ("ss", l))
                dve.reciprocal(u_gdn[0:8, 1552:1552 + CW], u_gdn[0:8, 1552:1552 + CW]).then_inc(sem("norms_inverse"), 1)
                for m in range(8):
                    ps, free = full(dve, ("norm", l, m))
                    dve.scalar_tensor_tensor(out=qk[:, m, 0:CW], in0=qk[:, m, 0:CW], scalar=P ** -0.5 if m < 4 else 1.0,
                                             in1=ps[:, 0:CW], op0=ALU.mult, op1=ALU.mult).then_inc(free, 1)
                ps, free = full(dve, ("gc", l))
                dve.wait_ge(sem("log_decay"), l + 1)
                dve.tensor_copy(col(GC, 24), ps[:, 0:24])
                dve.tensor_copy(col(TOTC, 24), ps[:, 32:56]).then_inc(free, 1)
                drained(dve, ("gc", l))
                dve.tensor_tensor(col(ETAIL, 24), col(TOTC, 24), col(GC, 24), ALU.subtract).then_inc(sem("decay_sums"), 1)
                dve.wait_ge(sem("decays"), l + 1)
                link(dve.tensor_tensor(col(BEGC, 24), col(BETA, 24), col(EGC, 24), ALU.mult))

                def h4(ap):
                    return ap.rearrange("p (h i) -> p h i", h=H)

                seen = set()
                for p, tiles in enumerate(PAIRS):
                    for d, t in enumerate(tiles):
                        n = batch(l, p, d)
                        at = t * 8 + d * 4
                        ps, free = full(dve, ("gcrow", n))
                        for h in range(H):
                            ins = dve.tensor_scalar(gd(d, "dt", h), ps[:, h * P:(h + 1) * P], col(GC + at + h, 1), 0.0,
                                                    ALU.subtract, ALU.min)
                        ins.then_inc(free, 1)
                        dve.wait_ge(sem("dt_exp"), n + 1)
                        link(dve.tensor_tensor(h4(gd(d, "dt")), h4(gd(d, "dt")), fan(c(f"tri{d}"), H), ALU.mult))
                        psb, freeb = full(dve, ("brow", n))
                        psq, freeq = full(dve, ("qk", n))
                        dve.tensor_tensor(gd(d, "a"), psq[:, :], gd(d, "dt"), ALU.mult).then_inc(freeq, 1)
                        psk, freek = full(dve, ("kk", n))
                        dve.tensor_tensor(gd(d, "lt"), psk[:, :], gd(d, "dt"), ALU.mult).then_inc(freek, 1)
                        drained(dve, ("kk", n))
                        dve.tensor_tensor(gd(d, "lt"), psb[:, :], gd(d, "lt"), ALU.mult).then_inc(freeb, 1)
                    for d, t in enumerate(tiles):
                        n = batch(l, p, d)
                        dve.wait_ge(sem("level_part"), level_count(l, p, d, 0))
                        dve.tensor_tensor(h4(gd(d, "xt")), fan(c("ident"), H), h4(gd(d, "m")), ALU.subtract).then_inc(sem("inv_start"), 1)
                    for v in range(1, LEVELS):
                        for d, t in enumerate(tiles):
                            n = batch(l, p, d)
                            if v == 1:
                                drained(dve, ("x0", n))
                                dve.wait_ge(sem("inv_start"), n + 1)
                            if v > 1:
                                drained(dve, ("xy", n, v - 1))
                                drained(dve, ("xty", n, v - 1))
                            if v < LEVELS - 1:
                                ps, free = full(dve, ("xy", n, v))
                                dve.tensor_tensor(gd(d, "x"), gd(d, "x"), ps[:, :], ALU.subtract).then_inc(free, 1)
                            ps, free = full(dve, ("xty", n, v))
                            dve.tensor_tensor(gd(d, "xt"), gd(d, "xt"), ps[:, :], ALU.subtract).then_inc(free, 1)
                    for d, t in enumerate(tiles):
                        n = batch(l, p, d)
                        at = t * 8 + d * 4
                        drained(dve, ("vtok", l, t))
                        ins = dve.tensor_tensor(h4(gd(d, "y")), h4(vtok[:, t, :]), wide(col(BETA + at, 4), P), ALU.mult)
                        if p == 0:
                            ins.then_inc(sem("gdn_rhs"), 1)
                            continue
                        link(ins)
                        ps, free = full(dve, ("ks", n))
                        dve.tensor_tensor(h4(gd(d, "m")), h4(ps[:, :]), wide(col(BEGC + at, 4), P), ALU.mult).then_inc(free, 1)
                        drained(dve, ("ks", n))
                        dve.tensor_tensor(gd(d, "y"), gd(d, "y"), gd(d, "m"), ALU.subtract).then_inc(sem("gdn_rhs"), 1)
                        ps, free = full(dve, ("qs", n))
                        dve.tensor_tensor(h4(gd(d, "dt")), h4(ps[:, :]), wide(col(EGC + at, 4), P), ALU.mult).then_inc(free, 1)
                        drained(dve, ("qs", n))
                    for d, t in enumerate(tiles):
                        n = batch(l, p, d)
                        at = t * 8 + d * 4
                        ps, free = full(dve, ("vnew", n))
                        if p:
                            dve.wait_ge(sem("gdn_rhs"), n + 1)
                        link(dve.tensor_copy(gd(d, "x"), ps[:, :]))
                        dve.tensor_tensor(h4(gd(d, "m")), h4(ps[:, :]), wide(col(ETAIL + at, 4), P), ALU.mult).then_inc(free, 1)
                    for d, t in enumerate(tiles):
                        n = batch(l, p, d)
                        at = t * 8 + d * 4
                        ps, free = full(dve, ("av", n))
                        if p == 0:
                            if t in seen:
                                dve.tensor_tensor(ov[:, t, :], ov[:, t, :], ps[:, :], ALU.add).then_inc(free, 1)
                            else:
                                dve.tensor_copy(ov[:, t, :], ps[:, :]).then_inc(free, 1)
                        else:
                            if t in seen:
                                link(dve.tensor_tensor(gd(d, "dt"), gd(d, "dt"), ov[:, t, :], ALU.add))
                            dve.tensor_tensor(ov[:, t, :], gd(d, "dt"), ps[:, :], ALU.add).then_inc(free, 1)
                        drained(dve, ("av", n))
                        seen.add(t)
                        if p == 2:
                            continue
                        if p == 0:
                            if l:
                                dve.wait_ge(sem("gla_out"), 64 * l)
                            ps, free = full(dve, ("ds", n))
                            dve.tensor_copy(st_out(d), ps[:, :]).then_inc(free, 1)
                        else:
                            s = s_gdn[:, d * W5:(d + 1) * W5]
                            link(dve.tensor_tensor(h4(s), h4(s), wide(col(ETOT + at, 4), P), ALU.mult))
                            ps, free = full(dve, ("ds", n))
                            dve.tensor_tensor(s, s, ps[:, :], ALU.add).then_inc(free, 1)
                finish(l, 0)

                for t in range(T):
                    ps, free = full(dve, ("glog", l, t))
                    dve.wait_ge(sem("gla_ln"), l * T + t + 1)
                    dve.scalar_tensor_tensor(out=u_gla[:, t * W5:(t + 1) * W5], in0=ps[:, :], scalar=0.0, in1=gl_ln,
                                             op0=ALU.min, op1=ALU.subtract).then_inc(free, 1)
                seen = set()
                for p, tiles in enumerate(PAIRS):
                    for name, src, key in (("q_in", 0, "gla_rel"), ("k_in", 256, "gla_rel"), ("q_dec", 0, "gla_sum"), ("k_tail", 256, "gla_tail")):
                        drained(dve, (key, l, p))
                        for d, t in enumerate(tiles):
                            w = gl(name)[:, d * 256:(d + 1) * 256]
                            ins = dve.tensor_tensor(w, w, gqkv[:, t, src:src + 256], ALU.mult)
                        ins.then_inc(sem("gla_decayed"), 1)
                    for d, t in enumerate(tiles):
                        ps, free = full(dve, ("gla_a", l, p, d))
                        if p == 0 and d == 0:
                            dve.wait_ge(sem("gla_zeroed"), l + 1)
                        dve.copy_predicated(h4(gla_at(d)), fan(c(f"sum{d}").bitcast(U32), H), h4(ps[:, :])).then_inc(free, 1)
                    for d, t in enumerate(tiles):
                        ps, free = full(dve, ("gla_av", l, p, d))
                        if t in seen:
                            dve.tensor_tensor(ov[:, t, :], ov[:, t, :], ps[:, :], ALU.add).then_inc(free, 1)
                        else:
                            if p == 0:
                                drained(dve, ("ot", l, 0, H - 1))
                            dve.tensor_copy(ov[:, t, :], ps[:, :]).then_inc(free, 1)
                        seen.add(t)
                        drained(dve, ("gla_av", l, p, d))
                    for step in range(2):
                        for d, t in enumerate(tiles):
                            ch = step if d == 0 else 1 - step
                            tok = slice(ch * HALF, (ch + 1) * HALF)
                            ps, free = full(dve, ("gla_inter", l, p, d, step))
                            dve.tensor_tensor(ov[tok, t, :], ov[tok, t, :], ps[tok, :], ALU.add).then_inc(free, 1)
                            drained(dve, ("gla_inter", l, p, d, step))
                            if p == 2 and step == 1:
                                continue
                            if step == 0:
                                drained(dve, ("gla_gt", l, p))
                            ps, free = full(dve, ("gla_ds", l, p, d, step))
                            s = gla_state(p, d)
                            for hp in range(2):
                                for hh in range(2):
                                    rr, cc = slice(hh * 64, hh * 64 + 64), slice(hp * 256 + hh * P, hp * 256 + hh * P + P)
                                    g0 = (d * 2 + hp) * 2 + ch
                                    ins = dve.scalar_tensor_tensor(out=s[rr, cc], in0=s[rr, cc], scalar=gla_gt(p)[rr, g0:g0 + 1],
                                                                   in1=ps[rr, cc], op0=ALU.mult, op1=ALU.add)
                            ins.then_inc(free, 1)
                            drained(dve, ("gla_ds", l, p, d, step))
                finish(l, 1)

                mod_out(l, 1)
                lp = par[:, l * 656 + 400:l * 656 + 656].rearrange("p (a s d) -> p a s d", a=2, s=2)
                link(dve.tensor_tensor(col(LPROD, 128).rearrange("p (a d) -> p a d", a=2), lp[:, :, 0, :], lp[:, :, 1, :], ALU.mult))
                dve.tensor_reduce(col(LAM, 2), col(LPROD, 128).rearrange("p (a d) -> p a d", a=2), AX.X, ALU.add).then_inc(sem("lam_parts"), 1)
                dve.wait_ge(sem("lam_exp"), l + 1)
                link(dve.tensor_tensor(col(LAM, 1), col(LAM, 1), col(LAM + 1, 1), ALU.subtract))
                link(dve.tensor_scalar(col(LAM, 1), col(LAM, 1), lam_init(l), None, ALU.add))
                tmp = u_att[:, 3072:3584]
                for t in (1, 2):
                    for name, v in (("dq", dqv), ("dk", dkv)):
                        drained(dve, (name, l, t))
                        rope = c("rope", (t - 1) * P, t * P)
                        s = v[:, t, :]
                        s5 = s.rearrange("p (g r j w) -> p g r j w", g=8, r=2, j=2)
                        tp5 = tmp.rearrange("p (g r j w) -> p g r j w", g=8, r=2, j=2)
                        sin = rope[:, 64:128].rearrange("p (r j w) -> p r j w", r=2, j=2)
                        for j in range(2):
                            for r in range(2):
                                link(dve.tensor_tensor(tp5[:, :, r, j, :],
                                                       s5[:, :, r, 1 - j, :],
                                                       fan(sin[:, r, j, :], 8), ALU.mult))
                        s8 = s.rearrange("p (g w) -> p g w", g=8)
                        link(dve.tensor_tensor(s8, s8, fan(rope[:, 0:64], 8), ALU.mult))
                        dve.tensor_tensor(s, s, tmp, ALU.add).then_inc(sem("roped"), 1)
                        dve.wait_ge(sem("roped"), (l * 2 + t - 1) * 2 + (1 if name == "dq" else 2))
                for t in range(T):
                    nk = P if t == 0 else KEYS
                    for hh in range(H + 1):
                        if hh < H:
                            n = (l * T + t) * H + hh
                            for s in range(2):
                                ps, _ = full(dve, ("sc", l, t, hh, s))
                                link(dve.tensor_reduce(col(NM + s, 1), ps[:, 0:nk], AX.X, ALU.max))
                                dve.tensor_scalar(col(NM + s, 1), col(NM + s, 1), -DH ** -0.5, None, ALU.mult).then_inc(sem("neg_max"), 1)
                        if hh < H:
                            drained(dve, ("sc", l, t, hh, 0))
                            drained(dve, ("sc", l, t, hh, 1))
                            link(dve.reciprocal(col(RP, 2), col(SUMP, 2)))
                            link(dve.tensor_tensor(col(RP + 1, 1), col(RP + 1, 1), col(LAM, 1), ALU.mult))
                            link(dve.tensor_scalar(dp(1)[:, 0:nk], dp(1)[:, 0:nk], col(RP + 1, 1), None, ALU.mult))
                            if n > 1:
                                m = n - 2
                                full(dve, ("wt", m // (T * H), m // H % T, m % H))
                            dve.scalar_tensor_tensor(out=dw(n % 2)[:, 0:nk], in0=dp(0)[:, 0:nk], scalar=col(RP, 1), in1=dp(1)[:, 0:nk],
                                                     op0=ALU.mult, op1=ALU.subtract).then_inc(sem("attn_weights"), 1)
                            dve.wait_ge(sem("attn_weights"), n + 1)
                        if hh:
                            h = hh - 1
                            ps, free = full(dve, ("att", l, t, h))
                            if t == 0 and h == 0:
                                drained(dve, ("ot", l, 1, H - 1))
                            dve.tensor_copy(ov[:, t, h * P:(h + 1) * P], ps[:, 0:P]).then_inc(free, 1)
                drained(dve, ("att", l, T - 1, H - 1))
                finish(l, 2)

                tmp = mtmp
                for s in range(3):
                    for t in range(T):
                        for half in range(2):
                            cut = slice(half * W5, (half + 1) * W5)
                            ps, free = full(dve, ("branch", l, s, t, half))
                            drained(dve, (("mergel", 2 * s + half), l, t))
                            if s == 0:
                                dve.tensor_tensor(mix[:, t, cut], mg[:, t, cut], ps[:, :], ALU.mult).then_inc(free, 1)
                                drained(dve, ("branch", l, s, t, half))
                            else:
                                dve.tensor_tensor(tmp, mg[:, t, cut], ps[:, :], ALU.mult).then_inc(free, 1)
                                drained(dve, ("branch", l, s, t, half))
                                ins = dve.tensor_tensor(mix[:, t, cut], mix[:, t, cut], tmp, ALU.add)
                                if s == 2 and t == T - 1 and half == 1:
                                    ins.then_inc(sem("mixed"), 1)
                                else:
                                    link(ins)
                if l + 1 < DEPTH:
                    mod_out(l + 1, 0)
                drained(dve, ("modg", l, 0, 1, 1))
                for half in range(2):
                    for t in range(T):
                        cut = slice(half * W5, (half + 1) * W5)
                        ps, free = full(dve, (("outl", half), l, t))
                        dve.tensor_tensor(tmp, gatev[:, min(t, 1), cut], ps[:, :], ALU.mult).then_inc(free, 1)
                        drained(dve, (("outl", half), l, t))
                        link(dve.scalar_tensor_tensor(out=xv[:, t, cut], in0=xv[:, t, cut], scalar=ALPHA, in1=tmp, op0=ALU.mult, op1=ALU.add))
                layer_norm(l, 0)
                modulate(l, 1)

                sc, bi, cm, eq, rk, gs, gr = (RTR + at for at in (0, 48, 96, 288, 480, 528, 540))
                drained(dve, ("router", l))
                dve.wait_ge(sem("router_in"), 32)
                link(dve.tensor_tensor(col(bi, 48).rearrange("p (t e) -> p t e", t=T), col(sc, 48).rearrange("p (t e) -> p t e", t=T),
                                       fan(rbias[:, :], T), ALU.add))

                def ranks(src, n, dst):
                    v = col(src, 4 * n).rearrange("p (g f) -> p g f", g=n)
                    other = v.unsqueeze(2).broadcast_to([P, n, 4, 4])
                    own = v.unsqueeze(3).broadcast_to([P, n, 4, 4])
                    a4 = col(cm, 16 * n).rearrange("p (g e f) -> p g e f", g=n, e=4)
                    b4 = col(eq, 16 * n).rearrange("p (g e f) -> p g e f", g=n, e=4)
                    link(dve.tensor_tensor(a4, other, own, ALU.is_gt))
                    link(dve.tensor_tensor(b4, other, own, ALU.is_equal))
                    b3 = col(eq, 16 * n).rearrange("p (g w) -> p g w", g=n)
                    link(dve.tensor_tensor(b3, b3, fan(c("before"), n), ALU.mult))
                    link(dve.tensor_tensor(col(cm, 16 * n), col(cm, 16 * n), col(eq, 16 * n), ALU.add))
                    link(dve.tensor_reduce(col(dst, 4 * n), col(cm, 16 * n).rearrange("p (a f) -> p a f", f=4), AX.X, ALU.add))

                ranks(bi, T * NG, rk)
                link(dve.tensor_scalar(col(rk, 48), col(rk, 48), 1.5, None, ALU.is_lt))
                link(dve.tensor_tensor(col(bi, 48), col(bi, 48), col(rk, 48), ALU.mult))
                link(dve.tensor_reduce(col(gs, 12), col(bi, 48).rearrange("p (g f) -> p g f", f=4), AX.X, ALU.add))
                ranks(gs, T, gr)
                link(dve.tensor_scalar(col(gr, 12), col(gr, 12), 0.5, None, ALU.is_lt))
                link(dve.tensor_tensor(col(sc, 48), col(sc, 48), col(rk, 48), ALU.mult))
                link(dve.tensor_tensor(col(sc, 48).rearrange("p (g f) -> p g f", f=4), col(sc, 48).rearrange("p (g f) -> p g f", f=4),
                                       wide(col(gr, 12), 4), ALU.mult))
                link(dve.tensor_reduce(col(RS, T), col(sc, 48).rearrange("p (t e) -> p t e", t=T), AX.X, ALU.add))
                link(dve.reciprocal(col(RS, T), col(RS, T)))
                gates = col(cm, T * EP).rearrange("p (t e) -> p t e", t=T)
                places = col(cm + T * EP, T * EP).rearrange("p (t e) -> p t e", t=T)
                link(dve.memset(col(cm, T * EP), 0.0))
                link(dve.memset(col(cm + T * EP, T * EP), -1.0))
                link(dve.tensor_tensor(gates[:, :, 0:E], col(sc, 48).rearrange("p (t e) -> p t e", t=T), wide(col(RS, T), E), ALU.mult))
                dve.tensor_scalar(chosen, col(sc, 48), 0.0, None, ALU.is_gt).then_inc(sem("chosen"), 1)
                dve.memset(proj[:, T * D:2 * T * D], 0.0)
                ps, free = full(dve, ("places", l))
                dve.wait_ge(sem("chosen"), l + 1)
                link(dve.scalar_tensor_tensor(out=col(bi, 48), in0=ps[:, 0:48], scalar=1.0, in1=chosen, op0=ALU.mult, op1=ALU.mult))
                link(dve.tensor_scalar(places[:, :, 0:E], col(bi, 48).rearrange("p (t e) -> p t e", t=T), -1.0, None, ALU.add))
                num, mor, inc = (small[0:1, RTR + at:RTR + at + E] for at in (0, 16, 32))
                dve.tensor_copy(num, ps[0:1, 48:64]).then_inc(free, 1)
                drained(dve, ("places", l))
                link(dve.tensor_scalar(mor, num, float(SLOTS), None, ALU.is_gt))
                for s in range(2, TOK // SLOTS):
                    link(dve.scalar_tensor_tensor(out=mor, in0=num, scalar=float(SLOTS * s), in1=mor, op0=ALU.is_gt, op1=ALU.add))
                link(dve.tensor_tensor_scan(inc, c("ones")[0:1, 0:E], mor, 0.0, ALU.mult, ALU.add))
                nj = JOBS - E
                ja = otok[0:1, 2 * W5:2 * W5 + nj * E].rearrange("p (j e) -> p j e", j=nj)
                je, jc = (otok[0:1, 2 * W5 + at:2 * W5 + at + nj] for at in (nj * E, nj * (E + 1)))
                idx = c("slots")[0:1, 0:nj]
                link(dve.tensor_tensor(ja, fan(inc, nj), wide(idx, E), ALU.is_le))
                link(dve.tensor_reduce(je, ja, AX.X, ALU.add))
                link(dve.tensor_tensor(ja, ja, fan(mor, nj), ALU.mult))
                link(dve.tensor_reduce(jc, ja, AX.X, ALU.add))
                link(dve.tensor_tensor(jc, idx, jc, ALU.subtract))
                link(dve.tensor_scalar(jc, jc, 1.0, float(SLOTS), ALU.add, ALU.mult))
                link(dve.tensor_scalar(jc, jc, float(TOK - SLOTS), 0.0, ALU.min, ALU.max))
                pairs, total = otok[0:1, 2 * W5 + nj * (E + 2):2 * W5 + nj * (E + 3)], small[0:1, 1060:1061]
                link(dve.tensor_scalar(pairs, idx, 2.0, None, ALU.mult))
                link(dve.tensor_tensor(pairs, pairs, inc[:, E - 1:E].broadcast_to([1, nj]), ALU.is_lt))
                link(dve.tensor_reduce(num[:, 0:1], pairs, AX.X, ALU.add))
                if l:
                    dve.wait_ge(sem("experts_done"), l)
                    link(dve.tensor_copy(jobs[0:1, BEFORE_AT:BEFORE_AT + 1], total))
                for at in (W_AT, X_AT):
                    link(dve.tensor_copy(jobs[0:1, at:at + E], c("slots")[0:1, 0:E]))
                link(dve.tensor_scalar(jobs[0:1, S_AT:S_AT + E], c("slots")[0:1, 0:E], 0.0, None, ALU.mult))
                link(dve.tensor_copy(jobs[0:1, X_AT + E:X_AT + JOBS], je))
                link(dve.tensor_scalar(je, je, float(E - 1), None, ALU.min))
                link(dve.tensor_copy(jobs[0:1, W_AT + E:W_AT + JOBS], je))
                link(dve.tensor_copy(jobs[0:1, S_AT + E:S_AT + JOBS], jc))
                link(dve.tensor_scalar(total, num[:, 0:1], float(E // 2), None, ALU.add))
                dve.tensor_scalar(jobs[0:1, TURNS_AT:TURNS_AT + 1], num[:, 0:1], float(E // 2 - 1), None, ALU.add)\
                    .then_inc(sem("jobs_listed"), 1)
                turns, before = listed(dve, l)
                gsel = col(GSEL, 2 * T).rearrange("p (t u) -> p t u", t=T)

                def pick(q, experts, firsts):
                    for u in range(2):
                        e = bass.ds(experts[u], 1)
                        dve.tensor_copy(gsel[:, :, u:u + 1], gates[:, :, e])
                        ins = dve.tensor_tensor(hot[:, :, u, :], fan(c("slots")[:, bass.ds(firsts[u], SLOTS)], T),
                                                places[:, :, e].broadcast_to([P, T, SLOTS]), ALU.is_equal)
                    ins.then_inc(sem("hot"), 1)

                def weigh(q):
                    dve.wait_ge(sem("hot"), q + (l + 1))
                    for u in range(2):
                        ins = dve.tensor_tensor(hotg[:, :, u, :], hot[:, :, u, :], wide(gsel[:, :, u], SLOTS), ALU.mult)
                    ins.then_inc(sem("hot_gated"), 1)

                def multiply(q):
                    used(dve, "gate", q)
                    ps, free = made(dve, "up", q)
                    dve.tensor_tensor(hact, ag, ps[:, :], ALU.mult).then_inc(free, 1)

                def add(q):
                    for k in range(2 * T):
                        ycut = yacc[:, k // 2, k % 2 * W5:(k % 2 + 1) * W5]
                        added(dve, q, k)
                        ps, free = made(dve, "back", q, k)
                        dve.tensor_tensor(ycut, ycut, ps[:, :], ALU.add).then_inc(free, 1)

                pick(before, (0, 1), (0, 0))
                weigh(before)
                made(dve, "gather", before + l, 1)
                dve.wait_ge(sem("hot_gated"), before + 1)
                pick(before + 1, (2, 3), (0, 0))
                multiply(before)
                with dve.Fori(0, turns) as i:
                    n = i + before
                    made(dve, "choice", n)
                    weigh(n + 1)
                    made(dve, "gather", n + (l + 1), 1)
                    experts, firsts = ([dve.value_load(jobs[0:1, bass.ds(i * 2 + (at + 4 + u), 1)], min_val=0, max_val=top)
                                        for u in range(2)] for at, top in ((X_AT, E), (S_AT, TOK - SLOTS)))
                    dve.wait_ge(sem("hot_gated"), n + 2)
                    pick(n + 2, experts, firsts)
                    multiply(n + 1)
                    add(n)
                last = turns + before
                add(last)
                used(dve, "back", last, 2 * T - 1)
                drained(dve, ("modg", l, 1, 1, 1))
                for t in range(T):
                    link(dve.tensor_tensor(yacc[:, t, :], yacc[:, t, :], gatev[:, min(t, 1), :], ALU.mult))
                    link(dve.scalar_tensor_tensor(out=xv[:, t, :], in0=xv[:, t, :], scalar=ALPHA, in1=yacc[:, t, :], op0=ALU.mult, op1=ALU.add))
                layer_norm(l, 1)


_INS = ["x_prompt", "x_sample", "c", "state_gdn", "state_gla", "cache_k", "cache_v", "c_ctx", "w_mod", "b_mod", "w_in",
        "gdn_conv", "gdn_a_log", "gdn_dt_bias", "gdn_norm", "gla_w_gate", "gla_b_gate", "gla_norm", "diff_lambda",
        "diff_norm", "w_branch", "w_out", "ln_g", "ln_b", "router_w", "router_b", "exp_w_gate", "exp_w_up", "exp_w_down"]
_OUTS = [("y_prompt", (1, SEQ, D)), ("y_sample", (1, DEC, D)), ("new_gdn", (1, DEPTH, 2, H, P, P)),
         ("new_gla", (1, DEPTH, 2, H, GLA_DK, P)), ("new_k", (1, DEPTH, SEQ, H, P)), ("new_v", (1, DEPTH, SEQ, H, P))]


def kernel(**inputs):
    import numpy as _np
    import concourse.bacc as _bacc
    from concourse import mybir as _mybir
    from concourse.bass_utils import run_bass_kernel_spmd as _run

    nc = _bacc.Bacc("TRN2", target_bir_lowering=False, num_devices=1)
    arrays = {f"in_{n}": _np.ascontiguousarray(inputs[n]) for n in _INS}
    arrays["in_consts"] = constants()[0]
    dram = {n: nc.dram_tensor(n, v.shape, _mybir.dt.from_np(v.dtype), kind="ExternalInput").ap() for n, v in arrays.items()}
    outs = [nc.dram_tensor(n, shape, F32, kind="ExternalOutput").ap() for n, shape in _OUTS]
    program(nc, {n: dram[f"in_{n}"] for n in _INS}, dram["in_consts"], *outs)
    r = _run(nc, [arrays], core_ids=[0])
    return tuple(r.results[0][n] for n, _ in _OUTS)
```

```python
from contextlib import ExitStack

import concourse.bass as bass
import numpy as np
from concourse import mybir

F32 = mybir.dt.float32
U32 = mybir.dt.uint32
ALU = mybir.AluOpType
ACT = mybir.ActivationFunctionType
AX = mybir.AxisListType

P = 128
D = 1024
KC = D // P
DEPTH = 2
SEQ, DEC = 128, 256
T = (SEQ + DEC) // P
TOK = T * P
H = 4
W5 = 512
GLA_DK = 64
HALF = 64
RANK = 16
DH = 64
PAST = 128
KEYS = DEC + PAST
TAPS = 5
E = 16
NG = 4
ALPHA = (2 * DEPTH) ** 0.25
EPS = 1e-6
TAU = 16.0
DIR = 2
LEVELS = 7
CW = TOK + 2
COL = (0, SEQ + 2, SEQ + 2 + P)
IN_COL = dict(qkv=0, z=1536, ba=2048, gqk=2064, gv=2576, r=3088, lr=3600, dq=3632, dk=4144, dv=4656, merge=5168)
RING = 3
SLOTS = 64
MORE = TOK * 2 // SLOTS
JOBS = E + MORE + 2
PAIRS_MAX = (E + MORE) // 2
EP = E + 1
CHUNK_W = KC * W5
PAIRS = ((0, 0), (1, 2), (2, 1))


def lam_init(l):
    return 0.8 - 0.6 * float(np.exp(-0.3 * l))


def constants():
    k, i = np.arange(P)[:, None], np.arange(P)[None, :]
    same = (k // HALF) == (i // HALF)
    mats = dict(ident=k == i, tri0=k <= i, tri1=k >= i, ones=np.ones((P, P)))
    for n in range(LEVELS):
        b = 1 << n
        lower = (k // (2 * b) == i // (2 * b)) & (k // b % 2 == 0) & (i // b % 2 == 1)
        mats[f"level0_{n}"], mats[f"level1_{n}"] = lower, lower.T
    base = i // HALF * HALF
    for d in range(DIR):
        upto = lambda t: same & ((k <= t) if d == 0 else (k >= t))
        ref = base + (HALF // 2 if d == 0 else HALF // 2 - 1)
        mats[f"sum{d}"] = upto(i)
        mats[f"rel{d}"] = upto(i).astype(float) - upto(ref).astype(float)
        mats[f"tail{d}"] = same.astype(float) - upto(i).astype(float)
    cols = dict(ident=np.asarray(mats.pop("ident"), np.float32),
                fold=(k % 32 == np.arange(32)[None, :]).astype(np.float32))
    cols.update({n: np.asarray(m, np.float32) for n, m in mats.items()})
    cols["slots"] = np.broadcast_to(np.arange(TOK, dtype=np.float32)[None, :], (P, TOK))
    cols["unit"] = np.broadcast_to(np.arange(15)[None, :] == 7, (P, 15)).astype(np.float32)
    cols["chunks"] = (k // HALF == np.arange(2)[None, :]).astype(np.float32)
    e, f = np.arange(4)[:, None], np.arange(4)[None, :]
    cols["before"] = np.broadcast_to((f < e).astype(np.float32).reshape(1, 16), (P, 16))
    pos = np.arange(DEC)
    inv = np.float32(10000.0) ** (-np.arange(0, 32, 2, dtype=np.float32) / np.float32(32))
    rot = np.zeros((DEC, 2, 2, 2, 16), np.float32)
    for half, where in enumerate((pos // 64, pos % 64)):
        ang = where.astype(np.float32)[:, None] * inv[None, :]
        rot[:, 0, half] = np.cos(ang)[:, None, :]
        rot[:, 1, half, 0], rot[:, 1, half, 1] = -np.sin(ang), np.sin(ang)
    cols["rope"] = rot.reshape(2, P, 128).transpose(1, 0, 2).reshape(P, 256)
    at, where = 0, {}
    for n, m in cols.items():
        where[n] = (at, m.shape[1])
        at += m.shape[1]
    return np.ascontiguousarray(np.concatenate(list(cols.values()), axis=1), np.float32), where


def program(nc, a, consts, y_prompt, y_sample, new_gdn, new_gla, new_k, new_v):
    order, place, dense_end = [], {}, []
    _, cwhere = constants()

    with ExitStack() as ctx:
        def sb(name, width, parts=P):
            return ctx.enter_context(nc.sbuf_tensor(name, [parts, width], F32))

        sems = {}

        def sem(name):
            if name not in sems:
                sems[name] = ctx.enter_context(nc.semaphore(name))
            return sems[name]

        cst = sb("cst", sum(w for _, w in cwhere.values()))
        x = sb("x", T * D)
        xt = sb("xt", KC * TOK)
        ring = sb("ring", RING * CHUNK_W)
        gate = sb("gate", 2 * D)
        modt = sb("modt", DEPTH * 96)
        bcol = sb("bcol", DEPTH * 48)
        crow = sb("crow", P, 16)
        scol = sb("scol", KC * 32)
        mrow = sb("mrow", W5)
        router = sb("router", KC * E)
        rbias = sb("rbias", E)
        wsmall = sb("wsmall", DEPTH * KC * 48)
        convrow = sb("convrow", DEPTH * P, 12 * TAPS)
        convc = sb("convc", 12 * TAPS)
        par = sb("par", DEPTH * 656)
        wgate = sb("wgate", DEPTH * W5, 33)
        lrt = sb("lrt", TOK, 33)
        small = sb("small", 1060 + 2 + 3 * T)
        s_gdn = sb("s_gdn", DIR * W5)
        s_gla = sb("s_gla", 2 * DIR * W5)
        qkvp = sb("qkvp", 12 * 390)
        otok = sb("otok", T * W5)
        shared = sb("shared", 13312)
        late = shared[:, 0:4608]
        proj = shared[:, 4608:10752]
        tail = shared[:, 10752:13312]
        lnp, mtmp = tail[:, 0:2 * D], tail[:, 2 * D:]
        ckv = tail[:, 0:2 * W5]
        u_gdn = shared[:, 6144:13312]
        u_gla = shared[:, 0:6144]
        u_att = proj

        banks = [ctx.enter_context(nc.psum_tensor(f"bank{b}", [P, W5], F32)) for b in range(8)]
        bank_full = [sem(f"bank{b}_full") for b in range(8)]
        bank_free = [sem(f"bank{b}_free") for b in range(8)]
        slot_in = [sem(f"slot{s}_in") for s in range(RING)]

        def c(name, a0=None, a1=None):
            at, w = cwhere[name]
            return cst[:, at + (a0 or 0):at + (w if a1 is None else a1)]

        def fan(ap, n):
            return ap.unsqueeze(1).broadcast_to([ap.shape[0], n, ap.shape[-1]])

        def wide(ap, w):
            return ap.unsqueeze(2).broadcast_to([ap.shape[0], ap.shape[1], w])

        xv = x[:, :].rearrange("p (t d) -> p t d", t=T)
        xtv = xt[:, :].rearrange("p (k t) -> p k t", k=KC)
        gatev = gate[:, :].rearrange("p (c d) -> p c d", c=2)
        modv = modt[:, :].rearrange("p (l j c) -> p l j c", l=DEPTH, c=2)
        mod_bank = banks[7]
        qk = qkvp[:, :].rearrange("p (m w) -> p m w", m=12)
        ot = qkvp[:, 0:12 * TOK].rearrange("p (m t) -> p m t", m=12)
        zv = proj[:, 0:T * W5].rearrange("p (t w) -> p t w", t=T)
        rv = proj[:, T * W5:2 * T * W5].rearrange("p (t w) -> p t w", t=T)
        gqkv = proj[:, 2 * T * W5:3 * T * W5].rearrange("p (t w) -> p t w", t=T)
        gvv = proj[:, 3 * T * W5:].rearrange("p (t w) -> p t w", t=T)
        mix = proj[:, 0:T * D].rearrange("p (t d) -> p t d", t=T)
        yacc = proj[:, T * D:].rearrange("p (t d) -> p t d", t=T)
        ktok = late[:, 0:T * W5].rearrange("p (t w) -> p t w", t=T)
        vtok = late[:, T * W5:2 * T * W5].rearrange("p (t w) -> p t w", t=T)
        dqv = late[:, 0:T * W5].rearrange("p (t w) -> p t w", t=T)
        dkv = late[:, T * W5:2 * T * W5].rearrange("p (t w) -> p t w", t=T)
        dvv = late[:, 2 * T * W5:].rearrange("p (t w) -> p t w", t=T)
        mg = late[:, 0:T * D].rearrange("p (t d) -> p t d", t=T)
        ov = otok[:, :].rearrange("p (t w) -> p t w", t=T)
        ring_in = [ring[:, s * CHUNK_W:(s + 1) * CHUNK_W].rearrange("p (k n) -> p k n", k=KC) for s in range(RING)]
        ring_dn = [ring[:, s * CHUNK_W:(s + 1) * CHUNK_W].rearrange("p (m n) -> p m n", m=4) for s in range(RING)]
        smv = wsmall[:, :].rearrange("p (l k n) -> p l k n", l=DEPTH, k=KC)
        rtv = router[:, :].rearrange("p (k e) -> p k e", k=KC)
        htok = proj[:, 0:T * D].rearrange("p (t d) -> p t d", t=T)
        hot = qkvp[:, 0:384].rearrange("p (t u s) -> p t u s", t=T, u=2)
        hotg = qkvp[:, 384:768].rearrange("p (t u s) -> p t u s", t=T, u=2)
        xg, ag, hact, ht = late[:, 0:1024], late[:, 1024:1536], late[:, 1536:2048], late[:, 2048:2560]
        oe, hott = late[:, 2560:3584], late[:, 3584:3968]
        jobs = ctx.enter_context(nc.sbuf_tensor("jobs", [1, 3 * JOBS + 1 + DEPTH], mybir.dt.int32))

        def col(at, n):
            return small[:, at:at + n]

        BETA, GG, GC, TOTC, EGC, ETOT, ETAIL, BEGC = (24 * n for n in range(8))
        AB, EXPA, LAM, LPROD, SS, RS, NM, SUMP, RP, ST, MV, RTR, GSEL, NMR = 192, 216, 224, 228, 360, 376, 392, 396, 400, 228, 428, 440, 1062, 1068

        filled = [0] * 8
        fills = {}
        turn = [0]
        chunk_end = {}

        def take(pe, key):
            b = turn[0] % 7
            turn[0] += 1
            if filled[b]:
                pe.wait_ge(bank_free[b], filled[b])
            filled[b] += 1
            fills[key] = (b, filled[b])
            return banks[b], bank_full[b]

        def full(eng, key):
            b, n = fills[key]
            eng.wait_ge(bank_full[b], n)
            return banks[b], bank_free[b]

        def drained(eng, key):
            b, n = fills[key]
            eng.wait_ge(bank_free[b], n)

        def arrived(eng, key):
            if key not in place:
                place[key] = len(order)
                order.append(key)
            n = place[key]
            eng.wait_ge(slot_in[n % RING], 16 * (n // RING + 1))
            return n % RING


        GD = dict(dt=0, a=1, lt=2, m=3, x=4, xt=5, y=6)

        def gd(d, name, h=None):
            at = (d * len(GD) + GD[name]) * W5
            return u_gdn[:, at:at + W5] if h is None else u_gdn[:, at + h * P:at + (h + 1) * P]

        def square(m):
            return u_gdn[:, m % 2 * 388:m % 2 * 388 + CW]

        def conv_out(m):
            return u_gdn[:, 776 + m % 2 * 388:776 + m % 2 * 388 + CW]

        def st_out(d):
            return s_gla[:, d * W5:(d + 1) * W5]

        def glog(t, d):
            return u_gla[:, t * W5 + d * 256:t * W5 + (d + 1) * 256]

        GL = dict(q_in=3, k_in=4, q_dec=5, k_tail=6)

        def gl(name):
            return u_gla[:, GL[name] * W5:(GL[name] + 1) * W5]

        gl_qz, gl_k, gl_dec = u_gla[:, 3584:4608], u_gla[:, 4608:5120], u_gla[:, 5120:5632]
        gl_ln = u_gla[:, 5632:6144]

        def gla_at(d):
            return tail[:, d * W5:(d + 1) * W5]

        def gla_state(p, d):
            at = (min(p, 1) * DIR + d) * W5
            return s_gla[:, at:at + W5]

        def gla_gt(p):
            return col(1030 + 8 * p, 8)

        dk_all = u_att[:, 1024:3072].rearrange("p (h k) -> p h k", h=H)

        def dq_z(s, h):
            return u_att[:, s * W5 + h * P:s * W5 + (h + 1) * P]

        def dp(n, s):
            at = 3072 + (n % 2 * 2 + s) * KEYS
            return u_att[:, at:at + KEYS]

        def dw(i):
            return u_att[:, 4608 + i * KEYS:4608 + (i + 1) * KEYS]

        def dwt(i):
            return u_att[:, 5376 + i * KEYS:5376 + (i + 1) * KEYS]

        EXPERT_BANKS = dict(out=(0, 1), gate=(2,), up=(3,), gather=(4, 5), turned=(6,), back=(7, 0, 1, 2, 3, 4),
                            choice=(5,))

        def made(eng, name, n, k=0):
            b = EXPERT_BANKS[name]
            eng.wait_ge(sem(f"expert_{name}_full"), n * len(b) + (k + 1))
            return banks[b[k]], sem(f"expert_{name}_free")

        def used(eng, name, n, k=0):
            ahead = len(EXPERT_BANKS["back"]) if name == "back" else 0
            eng.wait_ge(sem(f"expert_{name}_free"), n * len(EXPERT_BANKS[name]) + (k + 1 + ahead))

        def added(eng, n, k):
            eng.wait_ge(sem("expert_back_free"), n * len(EXPERT_BANKS["back"]) + (k + 1))

        W_AT, X_AT, S_AT, TURNS_AT, BEFORE_AT = 0, JOBS, 2 * JOBS, 3 * JOBS, 3 * JOBS + 1

        def before_layer(eng, l):
            if l == 0:
                return 0
            eng.wait_ge(sem("jobs_listed"), l)
            return eng.value_load(jobs[0:1, BEFORE_AT + l:BEFORE_AT + l + 1], min_val=E // 2, max_val=l * PAIRS_MAX)

        def turns_of(eng, l):
            eng.wait_ge(sem("jobs_listed"), l + 1)
            return eng.value_load(jobs[0:1, TURNS_AT:TURNS_AT + 1], min_val=E // 2 - 1, max_val=PAIRS_MAX - 1)

        def level_count(l, p, d, v):
            return ((l * 3 + p) * LEVELS + v) * DIR + d + 1

        def silu(act, l, m):
            act.wait_ge(sem("conv_done"), l * 12 + m + 1)
            act.activation(qk[:, m, 0:CW], conv_out(m), ACT.Silu).then_inc(sem("silu_done"), 1)

        def gate_in(act, name, l, v):
            for t in range(T):
                ps, free = full(act, (name, l, t))
                act.activation(v[:, t, :], ps[:, :], ACT.Silu).then_inc(free, 1)

        chosen = col(RTR + 480, 48)

        def branch_root(act, l, br):
            act.wait_ge(sem("branch_var"), l * 3 + br + 1)
            act.activation(col(SS, 12), col(SS, 12), ACT.Sqrt).then_inc(sem("branch_std"), 1)

        def branch_ot(act, l, br):
            for h in range(H):
                ps, free = full(act, ("ot", l, br, h))
                act.activation(ot[:, br * 4 + h, :], ps[:, 0:TOK], ACT.Copy).then_inc(free, 1)

        block = ctx.enter_context(nc.Block())

        def batch(l, p, d):
            return (l * 3 + p) * 2 + d

        @block.tensor
        def _(pe):
            pe.sem_inc(sem("expert_back_free"), len(EXPERT_BANKS["back"]))
            pe.wait_ge(sem("first_consts_in"), 16)
            pe.wait_ge(sem("cond_in"), 32)
            ps, ready = take(pe, "cond")
            pe.transpose(ps[:, 0:16], crow[0:16, :], c("ident")[0:16, 0:16]).then_inc(ready, 1)
            drained(pe, "cond")
            scv = scol[:, :].rearrange("p (k c) -> p k c", k=KC)

            def tokens_product(key, l, w_of, width=W5, scale_key=None):
                for t in range(T):
                    ps, ready = take(pe, (key, l, t))
                    for k in range(KC):
                        mm = pe.matmul(ps[:, 0:width], xtv[:, k, t * P:(t + 1) * P], w_of(k),
                                       start=(k == 0), stop=(k == KC - 1))
                    mm.then_inc(ready, 1)

            def transpose_x(l, which):
                for k in range(KC):
                    ps, ready = take(pe, ("xt", l, which, k))
                    for t in range(T):
                        if k == 0:
                            n = (l * 2 + which) * T
                            if n:
                                pe.wait_ge(sem("x_ready"), n - T + t + 1)
                            elif t == 0:
                                pe.wait_ge(sem("x_in"), 32)
                        mm = pe.transpose(ps[:, t * P:(t + 1) * P], xv[:, t, k * P:(k + 1) * P], c("ident"))
                    mm.then_inc(ready, 1)
                for k in (KC - 2, KC - 1):
                    drained(pe, ("xt", l, which, k))

            def finish_branch(l, br):
                pe.wait_ge(sem("branch_normed"), l * 3 + br + 1)
                for h in range(H):
                    ps, ready = take(pe, ("ot", l, br, h))
                    for t in range(T):
                        mm = pe.transpose(ps[:, t * P:(t + 1) * P], ov[:, t, h * P:(h + 1) * P], c("ident"))
                    mm.then_inc(ready, 1)

            def mod_rows(l, j):
                slot = arrived(pe, ("mod", l, j))
                ps, ready = take(pe, ("modrow", l, j))
                for k in range(KC):
                    part = k % 4 * 32
                    mm = pe.matmul(ps[part:part + 32, :], scv[:, k, :], ring_in[slot][:, k, :], start=(k < 4), stop=(k >= 4))
                mm.then_inc(ready, 1)
                chunk_end["mod", l, j] = ("modrow", l, j)

            def mod_columns(l, j):
                drained(pe, ("modrow", l, j))
                if j % 6 == 0 and l * 2 + j // 6:
                    pe.wait_ge(sem("mod_out"), l * 2 + j // 6)
                for b in range(4):
                    at = (l * 48 + j * 4 + b) * 2
                    mm = pe.matmul(mod_bank[:, at:at + 2], mrow[:, b * P:(b + 1) * P], c("fold", 0, 2), start=True, stop=True)
                if j % 6 == 5:
                    mm.then_inc(sem("mod_done"), 1)

            def narrow_rows(ps, cleared, w_of):
                if cleared:
                    pe.wait_ge(sem("narrow_cleared"), cleared)
                for k in range(KC):
                    w = w_of(k)
                    part = k % 4 * 32
                    mm = pe.matmul(ps[part:part + w.shape[-1], 0:TOK], w, xtv[:, k, :], start=(k < 4), stop=(k >= 4))
                return mm

            def fold_tokens(key, copied):
                ps, ready = take(pe, key)
                pe.wait_ge(sem("narrow_copied"), copied)
                for t in range(T):
                    mm = pe.matmul(ps[:, t * E:(t + 1) * E], otok[:, t * P:(t + 1) * P], c("fold", 0, E), start=True, stop=True)
                mm.then_inc(ready, 1)

            def gate_rows(l, which):
                pe.wait_ge(sem("mod_out"), l * 2 + which + 1)
                for half in range(2):
                    for cond in range(2):
                        ps, ready = take(pe, ("modg", l, which, half, cond))
                        for b in range(4):
                            i = 16 + 24 * which + half * 4 + b
                            mm = pe.matmul(ps[:, b * P:(b + 1) * P], modv[:, l, i, cond:cond + 1].broadcast_to([P, P]), c("ident"),
                                           start=True, stop=True)
                        mm.then_inc(ready, 1)
            ps, ready = take(pe, "mod_bias")
            pe.wait_ge(sem("mod_bias_in"), 16)
            pe.transpose(ps[:, 0:96], otok[0:96, 0:P], c("ident")[0:96, 0:96]).then_inc(ready, 1)
            for l in range(DEPTH):
                if l == 0:
                    for j in range(6):
                        mod_rows(0, j)
                        mod_columns(0, j)
                if l == 0:
                    pe.wait_ge(sem("consts_in"), 16)
                pe.wait_ge(sem(f"params{l}_in"), 16 * 7)
                ps, ready = take(pe, ("taps", l))
                pe.transpose(ps[:, 0:60], convrow[:, l * P:(l + 1) * P], c("ident")[0:60, 0:60]).then_inc(ready, 1)
                transpose_x(l, 0)

                for m in range(12):
                    ps, ready = take(pe, ("qkv", l, m))
                    slot = arrived(pe, ("qkv", l, m // 4))
                    for k in range(KC):
                        mm = pe.matmul(ps[:, 0:TOK], ring_in[slot][:, k, m % 4 * P:(m % 4 + 1) * P],
                                       xtv[:, k, :], start=(k == 0), stop=(k == KC - 1))
                    mm.then_inc(ready, 1)
                    chunk_end["qkv", l, m // 4] = ("qkv", l, m)
                narrow_rows(mod_bank, l * 2 + 1, lambda k: smv[:, l, k, 0:16]).then_inc(sem("narrow_rows"), 1)
                ps, ready = take(pe, ("lr_rows", l))
                narrow_rows(ps, None, lambda k: smv[:, l, k, 16:48]).then_inc(ready, 1)
                ps, ready = take(pe, ("ss", l))
                for m in range(8):
                    pe.wait_ge(sem("squares"), l * 8 + m + 1)
                    pe.matmul(ps[0:8, 0:CW], c("unit", 7 - m, 15 - m), square(m), start=(m == 0), stop=(m == 7))\
                        .then_inc(ready if m == 7 else sem("squares_summed"), 1)
                fold_tokens(("ba", l), l * 2 + 1)
                ps, ready = take(pe, ("lr", l))
                drained(pe, ("lr_rows", l))
                pe.matmul(ps[0:32, 0:TOK], c("fold"), otok[:, TOK:2 * TOK], start=True, stop=True).then_inc(ready, 1)
                slot = arrived(pe, ("z", l, 0))
                tokens_product("z", l, lambda k: ring_in[slot][:, k, :])
                chunk_end["z", l, 0] = ("z", l, T - 1)

                for m in range(8):
                    ps, ready = take(pe, ("norm", l, m))
                    if m == 0:
                        pe.wait_ge(sem("norms_inverse"), l + 1)
                    pe.matmul(ps[:, 0:CW], c("ident")[0:8, m:m + 1].broadcast_to([8, P]), u_gdn[0:8, 1552:1552 + CW],
                              start=True, stop=True).then_inc(ready, 1)
                ps, ready = take(pe, ("gc", l))
                pe.wait_ge(sem("log_decay"), l + 1)
                for t in range(T):
                    for d in range(DIR):
                        at = t * 8 + d * 4
                        pe.matmul(ps[:, at:at + 4], c(f"tri{d}"), col(GG + at, 4), start=True, stop=True)
                pe.matmul(ps[:, 32:56], c("ones"), col(GG, 24), start=True, stop=True).then_inc(ready, 1)
                gate_rows(l, 0)
                mod_rows(l, 6)
                drained(pe, ("norm", l, 7))
                for t in range(T):
                    for n, first in (("k", 4), ("v", 8)):
                        ps, ready = take(pe, (n + "tok", l, t))
                        for h in range(H):
                            mm = pe.transpose(ps[:, h * P:(h + 1) * P], qk[:, first + h, COL[t]:COL[t] + P],
                                              c("ident"))
                        mm.then_inc(ready, 1)

                def heads(ps, lhs, rhs, ready):
                    for h in range(H):
                        mm = pe.matmul(ps[:, h * P:(h + 1) * P], lhs(h), rhs(h), start=True, stop=True)
                    mm.then_inc(ready, 1)

                for p, tiles in enumerate(PAIRS):
                    for d, t in enumerate(tiles):
                        n = batch(l, p, d)
                        k_t = lambda h, t=t: qk[:, 4 + h, COL[t]:COL[t] + P]
                        q_t = lambda h, t=t: qk[:, h, COL[t]:COL[t] + P]
                        ps, ready = take(pe, ("gcrow", n))
                        pe.wait_ge(sem("gdn_rows"), n + 1)
                        pe.matmul(ps[:, :], c("ones"), gd(d, "y"), start=True, stop=True).then_inc(ready, 1)
                        ps, ready = take(pe, ("brow", n))
                        pe.matmul(ps[:, :], c("ones"), gd(d, "m"), start=True, stop=True).then_inc(ready, 1)
                        ps, ready = take(pe, ("qk", n))
                        heads(ps, k_t, q_t, ready)
                        ps, ready = take(pe, ("kk", n))
                        heads(ps, k_t, k_t, ready)
                    mod_columns(l, 6 + p)
                    mod_rows(l, 7 + p)
                    for d, t in enumerate(tiles):
                        n = batch(l, p, d)
                        ps, ready = take(pe, ("x0", n))
                        pe.wait_ge(sem("inv_start"), n + 1)
                        for h in range(H):
                            mm = pe.transpose(ps[:, h * P:(h + 1) * P], gd(d, "xt", h), c("ident"))
                        mm.then_inc(ready, 1)
                    for v in range(1, LEVELS):
                        for d, t in enumerate(tiles):
                            n = batch(l, p, d)
                            if v == 1:
                                drained(pe, ("x0", n))
                            else:
                                ps, ready = take(pe, ("xt_new", n, v))
                                drained(pe, ("xy", n, v - 1))
                                for h in range(H):
                                    mm = pe.transpose(ps[:, h * P:(h + 1) * P], gd(d, "x", h), c("ident"))
                                mm.then_inc(ready, 1)
                            ps, ready = take(pe, ("y", n, v))
                            pe.wait_ge(sem("level_part"), level_count(l, p, d, v))
                            heads(ps, lambda h: gd(d, "m", h), lambda h: gd(d, "x", h), ready)
                        for d, t in enumerate(tiles):
                            n = batch(l, p, d)
                            name = "xy" if v < LEVELS - 1 else "xty"
                            ps, ready = take(pe, (name, n, v))
                            drained(pe, ("y", n, v))
                            if v > 1:
                                drained(pe, ("xt_new", n, v))
                            if v < LEVELS - 1:
                                heads(ps, lambda h: gd(d, "xt", h), lambda h: gd(d, "y", h), ready)
                            else:
                                heads(ps, lambda h: gd(d, "y", h), lambda h: gd(d, "xt", h), ready)
                    for d, t in enumerate(tiles):
                        n = batch(l, p, d)
                        if p:
                            state = lambda h, d=d: s_gdn[:, d * W5 + h * P:d * W5 + (h + 1) * P]
                            ps, ready = take(pe, ("ks", n))
                            if p == 1:
                                pe.wait_ge(sem("gdn_state_in"), 32 * (l + 1))
                            else:
                                drained(pe, ("ds", batch(l, 1, d)))
                            heads(ps, lambda h: qk[:, 4 + h, COL[t]:COL[t] + P], state, ready)
                            ps, ready = take(pe, ("qs", n))
                            heads(ps, lambda h: qk[:, h, COL[t]:COL[t] + P], state, ready)
                    for d, t in enumerate(tiles):
                        n = batch(l, p, d)
                        ps, ready = take(pe, ("vnew", n))
                        pe.wait_ge(sem("gdn_rhs"), n + 1)
                        drained(pe, ("xty", n, LEVELS - 1))
                        heads(ps, lambda h: gd(d, "xt", h), lambda h: gd(d, "y", h), ready)
                    for d, t in enumerate(tiles):
                        n = batch(l, p, d)
                        ps, ready = take(pe, ("av", n))
                        drained(pe, ("vnew", n))
                        heads(ps, lambda h: gd(d, "a", h), lambda h: gd(d, "x", h), ready)
                        if p < 2:
                            ps, ready = take(pe, ("ds", n))
                            heads(ps, lambda h: ktok[:, t, h * P:(h + 1) * P], lambda h: gd(d, "m", h), ready)
                mod_columns(l, 9)
                mod_rows(l, 10)
                slot = arrived(pe, ("gqk", l, 0))
                tokens_product("gqk", l, lambda k: ring_in[slot][:, k, :])
                chunk_end["gqk", l, 0] = ("gqk", l, T - 1)
                finish_branch(l, 0)

                slot = arrived(pe, ("gv", l, 0))
                tokens_product("gv", l, lambda k: ring_in[slot][:, k, :])
                chunk_end["gv", l, 0] = ("gv", l, T - 1)
                for t in range(T):
                    ps, ready = take(pe, ("glog", l, t))
                    if t == 0:
                        drained(pe, ("lr", l))
                        pe.wait_ge(sem("fixed_set"), 1)
                    pe.matmul(ps[:, :], lrt[0:33, t * P:(t + 1) * P], wgate[0:33, l * W5:(l + 1) * W5],
                              start=True, stop=True).then_inc(ready, 1)
                slot = arrived(pe, ("r", l, 0))
                tokens_product("r", l, lambda k: ring_in[slot][:, k, :])
                chunk_end["r", l, 0] = ("r", l, T - 1)
                for p, tiles in enumerate(PAIRS):
                    for name in ("rel", "sum", "tail"):
                        ps, ready = take(pe, ("gla_" + name, l, p))
                        if name == "rel" and p == 0:
                            drained(pe, ("glog", l, T - 1))
                        for d, t in enumerate(tiles):
                            mm = pe.matmul(ps[:, d * 256:(d + 1) * 256], c(f"{name}{d}"), glog(t, d),
                                           start=True, stop=True)
                        mm.then_inc(ready, 1)
                    ps, ready = take(pe, ("gla_gt", l, p))
                    for d, t in enumerate(tiles):
                        for hp in range(2):
                            at = (d * 2 + hp) * 2
                            mm = pe.matmul(ps[:, at:at + 2], glog(t, d)[:, hp * P:(hp + 1) * P], c("chunks"),
                                           start=True, stop=True)
                    mm.then_inc(ready, 1)
                    for i, name in enumerate(("q_in", "k_in", "q_dec")):
                        ps, ready = take(pe, (name, l, p))
                        pe.wait_ge(sem("gla_decayed"), (l * 3 + p) * 4 + i + 1)
                        for d in range(DIR):
                            for hp in range(2):
                                at = (d * 2 + hp) * P
                                mm = pe.transpose(ps[:, at:at + P], gl(name)[:, at:at + P], c("ident"))
                        mm.then_inc(ready, 1)
                    for d, t in enumerate(tiles):
                        ps, ready = take(pe, ("gla_a", l, p, d))
                        if d == 0:
                            drained(pe, ("q_in", l, p))
                            drained(pe, ("k_in", l, p))
                        for h in range(H):
                            hp, par_ = h // 2, h % 2
                            mm = pe.matmul(ps[:, h * P:(h + 1) * P], gl_k[:, (d * 2 + hp) * P:(d * 2 + hp + 1) * P], gl_qz[:, par_ * W5 + (d * 2 + hp) * P:par_ * W5 + (d * 2 + hp + 1) * P],
                                           start=True, stop=True)
                        mm.then_inc(ready, 1)
                    for d, t in enumerate(tiles):
                        ps, ready = take(pe, ("gla_av", l, p, d))
                        drained(pe, ("gla_a", l, p, d))
                        for h in range(H):
                            mm = pe.matmul(ps[:, h * P:(h + 1) * P], gla_at(d)[:, h * P:(h + 1) * P],
                                           gvv[:, t, h * P:(h + 1) * P], start=True, stop=True)
                        mm.then_inc(ready, 1)
                    for step in range(2):
                        for d, t in enumerate(tiles):
                            ch = step if d == 0 else 1 - step
                            tok = slice(ch * HALF, (ch + 1) * HALF)
                            ps, ready = take(pe, ("gla_inter", l, p, d, step))
                            if step == 0 and d == 0:
                                drained(pe, ("q_dec", l, p))
                            if step == 1:
                                drained(pe, ("gla_ds", l, p, d, 0))
                            elif p == 1 and d == 0:
                                pe.wait_ge(sem("gla_state_in"), 64 * (l + 1))
                            elif p == 2:
                                drained(pe, ("gla_ds", l, 1, d, 1))
                            elif d == 0:
                                pe.wait_ge(sem("gla_zeroed"), l + 1)
                            for hp in range(2):
                                at = (d * 2 + hp) * P
                                mm = pe.matmul(ps[tok, hp * 256:(hp + 1) * 256], gl_dec[:, at + ch * HALF:at + (ch + 1) * HALF],
                                               gla_state(p, d)[:, hp * 256:(hp + 1) * 256], start=True, stop=True)
                            mm.then_inc(ready, 1)
                            if p == 2 and step == 1:
                                continue
                            ps, ready = take(pe, ("gla_ds", l, p, d, step))
                            if step == 0 and d == 0:
                                pe.wait_ge(sem("gla_decayed"), (l * 3 + p) * 4 + 4)
                            for hp in range(2):
                                at = (d * 2 + hp) * P
                                mm = pe.matmul(ps[:, hp * 256:(hp + 1) * 256], gl("k_tail")[tok, at:at + P],
                                               gvv[tok, t, hp * 256:(hp + 1) * 256], start=True, stop=True)
                            mm.then_inc(ready, 1)
                mod_columns(l, 10)
                mod_rows(l, 11)
                slot = arrived(pe, ("dq", l, 0))
                tokens_product("dq", l, lambda k: ring_in[slot][:, k, :])
                chunk_end["dq", l, 0] = ("dq", l, T - 1)
                finish_branch(l, 1)
                mod_columns(l, 11)

                for name in ("dk", "dv"):
                    slot = arrived(pe, (name, l, 0))
                    tokens_product(name, l, lambda k: ring_in[slot][:, k, :])
                    chunk_end[name, l, 0] = (name, l, T - 1)
                if l + 1 < DEPTH:
                    mod_rows(l + 1, 0)
                for t in range(T + 1):
                    ps, ready = take(pe, ("kt", l, t))
                    if t == T:
                        pe.wait_ge(sem("cache_in"), 32 * (l + 1))
                    elif t:
                        pe.wait_ge(sem("roped"), (l * 2 + t - 1) * 2 + 2)
                    else:
                        drained(pe, ("dk", l, 0))
                    for h in range(H):
                        src = ckv[:, h * P:(h + 1) * P] if t == T else dkv[:, t, h * P:(h + 1) * P]
                        mm = pe.transpose(ps[:, h * P:(h + 1) * P], src, c("ident"))
                    mm.then_inc(ready, 1)
                for m in range(T * H + 3):
                    if m < T * H:
                        t, h = divmod(m, H)
                        if h == 0:
                            ps, ready = take(pe, ("qt", l, t))
                            if t == 0:
                                drained(pe, ("dq", l, 0))
                            for hh in range(H):
                                mm = pe.transpose(ps[:, hh * P:(hh + 1) * P], dqv[:, t, hh * P:(hh + 1) * P], c("ident"))
                            mm.then_inc(ready, 1)
                        lo, hi = (0, P) if t == 0 else (P, P + KEYS)
                        for s in range(2):
                            ps, ready = take(pe, ("sc", l, m, s))
                            if h == 0 and s == 0:
                                drained(pe, ("qt", l, t))
                                drained(pe, ("kt", l, T))
                            pe.matmul(ps[:, 0:hi - lo], dq_z(s, h), dk_all[:, h, :][:, lo:hi],
                                      start=True, stop=True).then_inc(ready, 1)
                        if l + 1 < DEPTH and h == 1:
                            mod_columns(l + 1, t)
                            mod_rows(l + 1, t + 1)
                    if 2 <= m < T * H + 2:
                        n = l * T * H + m - 2
                        tiles_k = [0] if m - 2 < H else [1, 2, 3]
                        ps, ready = take(pe, ("wt", n))
                        pe.wait_ge(sem("attn_weights"), n + 1)
                        for i in range(len(tiles_k)):
                            mm = pe.transpose(ps[:, i * P:(i + 1) * P], dw(n % 2)[:, i * P:(i + 1) * P], c("ident"))
                        mm.then_inc(ready, 1)
                    if m >= 3:
                        t, h = divmod(m - 3, H)
                        n = l * T * H + m - 3
                        tiles_k = [0] if t == 0 else [1, 2, 3]
                        ps, ready = take(pe, ("att", n))
                        drained(pe, ("wt", n))
                        for i, kt in enumerate(tiles_k):
                            val = ckv[:, W5 + h * P:W5 + (h + 1) * P] if kt == 3 else dvv[:, kt, h * P:(h + 1) * P]
                            mm = pe.matmul(ps[:, 0:P], dwt(n % 2)[:, i * P:(i + 1) * P], val,
                                           start=(i == 0), stop=(i == len(tiles_k) - 1))
                        mm.then_inc(ready, 1)
                if l + 1 < DEPTH:
                    mod_columns(l + 1, 3)
                    mod_rows(l + 1, 4)

                for s in range(3):
                    for half in range(2):
                        slot = arrived(pe, ("merge", l, 2 * s + half))
                        tokens_product(("mergel", 2 * s + half), l, lambda k: ring_in[slot][:, k, :])
                        chunk_end["merge", l, 2 * s + half] = (("mergel", 2 * s + half), l, T - 1)
                        if s == half == 0:
                            finish_branch(l, 2)
                            if l + 1 < DEPTH:
                                mod_columns(l + 1, 4)
                                mod_rows(l + 1, 5)
                    if s == 0 and l + 1 < DEPTH:
                        mod_columns(l + 1, 5)
                    slot = arrived(pe, ("branch", l, s))
                    drained(pe, ("ot", l, s, H - 1))
                    for t in range(T):
                        for half in range(2):
                            ps, ready = take(pe, ("branch", l, s, t, half))
                            for h in range(H):
                                mm = pe.matmul(ps[:, :], ot[:, s * 4 + h, t * P:(t + 1) * P],
                                               ring_dn[slot][:, h, half * W5:(half + 1) * W5],
                                               start=(h == 0), stop=(h == H - 1))
                            mm.then_inc(ready, 1)
                    chunk_end["branch", l, s] = ("branch", l, s, T - 1, 1)
                for k in range(KC):
                    ps, ready = take(pe, ("mixt", l, k))
                    if k == 0:
                        drained(pe, ("branch", l, 2, T - 1, 1))
                        pe.wait_ge(sem("mixed"), l + 1)
                    for t in range(T):
                        mm = pe.transpose(ps[:, t * P:(t + 1) * P], mix[:, t, k * P:(k + 1) * P], c("ident"))
                    mm.then_inc(ready, 1)
                drained(pe, ("mixt", l, KC - 1))
                for half in range(2):
                    slot = arrived(pe, ("out", l, half))
                    tokens_product(("outl", half), l, lambda k: ring_in[slot][:, k, :])
                    chunk_end["out", l, half] = (("outl", half), l, T - 1)

                gate_rows(l, 1)

                transpose_x(l, 1)
                pe.wait_ge(sem("router_in"), 32)
                narrow_rows(mod_bank, l * 2 + 2, lambda k: rtv[:, k, :]).then_inc(sem("narrow_rows"), 1)
                for t in range(T):
                    for half in range(2):
                        ps, ready = take(pe, ("htok", l, t, half))
                        for k in range(4):
                            mm = pe.transpose(ps[:, k * P:(k + 1) * P], xtv[:, half * 4 + k, t * P:(t + 1) * P], c("ident"))
                        mm.then_inc(ready, 1)
                    if t == 0:
                        fold_tokens(("router", l), l * 2 + 2)
                drained(pe, ("htok", l, T - 1, 1))
                ps, ready = take(pe, ("places", l))
                pe.wait_ge(sem("chosen"), l + 1)
                for t in range(T):
                    for t2 in range(t + 1):
                        pe.matmul(ps[:, t * E:(t + 1) * E], c("tri0" if t2 == t else "ones"),
                                  chosen[:, t2 * E:(t2 + 1) * E], start=(t2 == 0), stop=(t2 == t))
                for t in range(T):
                    mm = pe.matmul(ps[:, T * E:(T + 1) * E], c("ones"), chosen[:, t * E:(t + 1) * E],
                                   start=(t == 0), stop=(t == T - 1))
                mm.then_inc(ready, 1)

                dense_end.append(len(order))
                first_slot = dense_end[l] % RING
                for b in range(7):
                    pe.wait_ge(bank_free[b], filled[b])
                pe.wait_ge(sem("mod_out"), min(l * 2 + 3, DEPTH * 2))
                before = before_layer(pe, l)

                def chunk(q, j):
                    pe.wait_ge(sem(f"expert_chunk{j % RING}_in"), q * 64 + 32 * (j // RING + 1))
                    slot = (first_slot + j) % RING
                    return ring[:, slot * CHUNK_W:(slot + 1) * CHUNK_W].rearrange("p (u k n) -> p u k n", u=2, k=4)

                def gather(q):
                    pe.wait_ge(sem("hot"), q + (l + 1))
                    for half, b in enumerate(EXPERT_BANKS["gather"]):
                        for k in range(4):
                            for t in range(T):
                                at = (half * 4 + k) * P
                                mm = pe.matmul(banks[b][:, k * P:(k + 1) * P], htok[:, t, at:at + P],
                                               hot[:, t, :, :].rearrange("p u s -> p (u s)"), start=(t == 0), stop=(t == T - 1))
                        mm.then_inc(sem("expert_gather_full"), 1)

                def hidden(q, name, first_chunk):
                    ps = banks[EXPERT_BANKS[name][0]]
                    for part in range(2):
                        w = chunk(q, first_chunk + part)
                        for k in range(4):
                            for u in range(2):
                                at = (part * 4 + k) * P + u * SLOTS
                                mm = pe.matmul(ps[u * SLOTS:(u + 1) * SLOTS, :], xg[:, at:at + SLOTS], w[:, u, k, :],
                                               start=(part == k == 0), stop=(part == 1 and k == 3))
                        mm.then_inc(sem("expert_chunk_used") if part == 0 else sem(f"expert_{name}_full"), 1)

                def turned(q):
                    used(pe, "up", q)
                    ps = banks[EXPERT_BANKS["turned"][0]]
                    for m in range(4):
                        mm = pe.transpose(ps[:, m * P:(m + 1) * P], hact[:, m * P:(m + 1) * P], c("ident"))
                    mm.then_inc(sem("expert_turned_full"), 1)

                def choice(q):
                    pe.wait_ge(sem("hot_gated"), q + 1)
                    ps = banks[EXPERT_BANKS["choice"][0]]
                    for t in range(T):
                        mm = pe.transpose(ps[:, t * P:(t + 1) * P], hotg[:, t, :, :].rearrange("p u s -> p (u s)"), c("ident"))
                    mm.then_inc(sem("expert_choice_full"), 1)

                def output(q):
                    used(pe, "turned", q)
                    for half in range(2):
                        w = chunk(q, 4 + half)
                        for m in range(4):
                            for u in range(2):
                                at = m * P + u * SLOTS
                                mm = pe.matmul(banks[EXPERT_BANKS["out"][half]][u * SLOTS:(u + 1) * SLOTS, :], ht[:, at:at + SLOTS],
                                               w[:, u, m, :], start=(m == 0), stop=(m == 3))
                        mm.then_inc(sem("expert_out_full"), 1)

                def back(q, bank_wait, parts=range(2 * T)):
                    used(pe, "choice", q)
                    used(pe, "out", q, 1)
                    for k in parts:
                        bank_wait(k)
                        pe.matmul(banks[EXPERT_BANKS["back"][k]][:, :], hott[:, k // 2 * P:(k // 2 + 1) * P],
                                  oe[:, k % 2 * W5:(k % 2 + 1) * W5], start=True, stop=True)\
                            .then_inc(sem("expert_back_full"), 1)

                gather(before)
                used(pe, "gather", before + l, 1)
                hidden(before, "gate", 0)
                hidden(before, "up", 2)
                gather(before + 1)
                turned(before)
                used(pe, "gather", before + (l + 1), 1)
                choice(before)
                turns = turns_of(pe, l)
                with pe.Fori(0, turns) as i:
                    n = i + before
                    added(pe, n, 2)
                    output(n)
                    used(pe, "gather", n + (l + 1), 1)
                    added(pe, n, 3)
                    hidden(n + 1, "gate", 0)
                    added(pe, n, 0)
                    back(n, lambda k: None, range(3))
                    added(pe, n, 4)
                    hidden(n + 1, "up", 2)
                    added(pe, n, 5)
                    used(pe, "choice", n)
                    gather(n + 2)
                    turned(n + 1)

                    def bank_wait(k):
                        if k == 3:
                            used(pe, "gate", n + 1)
                        elif k == 4:
                            used(pe, "up", n + 1)
                        elif k == 5:
                            used(pe, "gather", n + (l + 2), 0)
                    back(n, bank_wait, range(3, 2 * T))
                    used(pe, "gather", n + (l + 2), 1)
                    choice(n + 1)
                last = turns + before
                added(pe, last, 2)
                output(last)
                back(last, lambda k: added(pe, last, k))
                used(pe, "back", last, 2 * T - 1)
                pe.sem_inc(sem("experts_done"), 1)

        @block.sync
        def _(sp):
            sp.dma_start(cst[:, 0:P + 32], consts[:, 0:P + 32]).then_inc(sem("first_consts_in"), 16)
            sp.dma_start(crow[0:8, :], a["c_ctx"].rearrange("(k p) -> k p", p=P)).then_inc(sem("cond_in"), 16)
            sp.dma_start(crow[8:16, :], a["c"].rearrange("b (k p) -> (b k) p", p=P)).then_inc(sem("cond_in"), 16)
            sp.dma_start(otok[0:96, 0:P], a["b_mod"].rearrange("l (j p) -> (l j) p", p=P)).then_inc(sem("mod_bias_in"), 16)

            rows = lambda w: w.rearrange("(k p) n -> p k n", p=P)
            source = {
                "mod": lambda l, j: rows(a["w_mod"][l])[:, :, j * W5:(j + 1) * W5],
                "qkv": lambda l, j: rows(a["w_in"][l])[:, :, j * W5:(j + 1) * W5],
                "merge": lambda l, j: rows(a["w_in"][l])[:, :, IN_COL["merge"] + j * W5:IN_COL["merge"] + (j + 1) * W5],
                "out": lambda l, j: rows(a["w_out"][l])[:, :, j * W5:(j + 1) * W5],
                "branch": lambda l, s: a["w_branch"][l, s].rearrange("(m p) n -> p m n", p=P),
            }
            for name in ("gqk", "gv", "z", "r", "dq", "dk", "dv"):
                source[name] = lambda l, j, name=name: rows(a["w_in"][l])[:, :, IN_COL[name]:IN_COL[name] + W5]

            def load(key):
                name, l, j = key
                slot = place[key] % RING
                sp.dma_start((ring_dn if name == "branch" else ring_in)[slot], source[name](l, j)).then_inc(slot_in[slot], 16)

            def load_pair(l, j, experts):
                slot = (dense_end[l] + j) % RING
                for u, e in enumerate(experts):
                    part = j % 2
                    if j < 4:
                        src = rows(a["exp_w_gate" if j < 2 else "exp_w_up"][l, e])[:, part * 4:(part + 1) * 4, :]
                    else:
                        src = rows(a["exp_w_down"][l, e])[:, :, part * W5:(part + 1) * W5]
                    at = slot * CHUNK_W + u * CHUNK_W // 2
                    sp.dma_start(ring[:, at:at + CHUNK_W // 2].rearrange("p (k n) -> p k n", k=4), src)\
                        .then_inc(sem(f"expert_chunk{j % RING}_in"), 16)

            def pair_used(j, q):
                if j == 0:
                    sp.wait_ge(sem("expert_up_full"), q + 1)
                elif j in (1, 2):
                    sp.wait_ge(sem("expert_out_full"), q * 2 + j)
                elif j == 4:
                    sp.wait_ge(sem("expert_gate_full"), q + 1)
                else:
                    sp.wait_ge(sem("expert_chunk_used"), q * 2 + (1 if j == 3 else 2))

            def reusable(n):
                full(sp, chunk_end[order[n]])

            for l in range(DEPTH):
                first = dense_end[l - 1] if l else 0
                for n in range(first, dense_end[l]):
                    if l == 0 and n == RING:
                        sp.dma_start(cst[:, P + 32:], consts[:, P + 32:]).then_inc(sem("consts_in"), 16)
                        sp.dma_start(xv[:, 0, :], a["x_prompt"][0]).then_inc(sem("x_in"), 16)
                        sp.dma_start(xv[:, 1:3, :], a["x_sample"][0].rearrange("(t p) d -> p t d", p=P)).then_inc(sem("x_in"), 16)
                    if l and n < first + RING:
                        pair_used(n - first, last)
                    elif n >= RING:
                        reusable(n - RING)
                    load(order[n])
                for j in range(RING):
                    reusable(dense_end[l] - RING + j)
                    load_pair(l, j, (0, 1))
                before = before_layer(sp, l)
                for j in range(RING, 6):
                    pair_used(j, before)
                    load_pair(l, j, (0, 1))
                turns = turns_of(sp, l)
                with sp.Fori(0, turns) as i:
                    n = i + before
                    experts = [sp.value_load(jobs[0:1, bass.ds(i * 2 + (W_AT + 2 + u), 1)], min_val=0, max_val=E - 1)
                               for u in range(2)]
                    for j in range(6):
                        pair_used(j, n if j < RING else n + 1)
                        load_pair(l, j, experts)
                last = turns + before
            sp.wait_ge(sem("experts_done"), DEPTH)

        @block.gpsimd
        def _(pool):
            steps = [0]

            def link(ins):
                steps[0] += 1
                ins.then_inc(sem("pool_steps"), 1)
                pool.wait_ge(sem("pool_steps"), steps[0])

            for l in range(DEPTH):
                pin = sem(f"params{l}_in")
                pool.dma_start(smv[:, l, :, 0:16], a["w_in"][l, :, IN_COL["ba"]:IN_COL["ba"] + 16].rearrange("(k p) n -> p k n", p=P)).then_inc(pin, 16)
                pool.dma_start(smv[:, l, :, 16:48], a["w_in"][l, :, IN_COL["lr"]:IN_COL["lr"] + 32].rearrange("(k p) n -> p k n", p=P)).then_inc(pin, 16)
                pool.dma_start(convrow[:, l * P:(l + 1) * P], a["gdn_conv"][l].rearrange("k (c p) -> (k c) p", p=P)).then_inc(pin, 16)
                at = l * 656
                for name, w in (("gdn_a_log", 8), ("gdn_dt_bias", 8)):
                    pool.dma_start(par[:, at:at + w], a[name][l].rearrange("d h -> (d h)").partition_broadcast(P)).then_inc(pin, 16)
                    at += w
                at = l * 656 + 16 + 384
                pool.dma_start(par[:, at:at + 256], a["diff_lambda"][l].rearrange("s d -> (s d)").partition_broadcast(P)).then_inc(pin, 16)
                pool.dma_start(wgate[32:33, l * W5:(l + 1) * W5], a["gla_b_gate"][l].rearrange("(o d) k -> o (d k)", o=1)).then_inc(pin, 16)
                at = l * 656 + 16
                for name in ("gdn_norm", "gla_norm", "diff_norm"):
                    pool.dma_start(par[:, at:at + 128], a[name][l].partition_broadcast(P)).then_inc(sem("norms_in"), 16)
                    at += 128
            pool.dma_start(rtv, a["router_w"].rearrange("(k p) e -> p k e", p=P)).then_inc(sem("router_in"), 16)
            pool.dma_start(rbias[:, :], a["router_b"].partition_broadcast(P)).then_inc(sem("router_in"), 16)
            link(pool.memset(wgate[0:32, :], 0.0))
            for l in range(DEPTH):
                for d in range(DIR):
                    pool.dma_start(wgate[d * RANK:(d + 1) * RANK, l * W5 + d * 256:l * W5 + (d + 1) * 256],
                                   a["gla_w_gate"][l, d]).then_inc(sem("gate_w_in"), 16)
            link(pool.memset(lrt[32:33, :], 1.0))
            link(pool.memset(s_gla[:, :], 0.0))
            pool.wait_ge(sem("gate_w_in"), 64)
            link(pool.memset(small[:, 1000:1001], 0.0))
            pool.memset(small[:, 1001:1002], 0.0).then_inc(sem("fixed_set"), 1)
            for l in range(DEPTH):
                if l:
                    pool.wait_ge(sem("experts_done"), l)
                for at in (0, 130, 388):
                    ins = pool.memset(qk[:, :, at:at + 2], 0.0)
                    if at == 388:
                        ins.then_inc(sem("pads"), 1)
                def ln_params(which):
                    if which:
                        pool.wait_ge(sem("x_ready"), (l * 2 + which) * T)
                    else:
                        pool.wait_ge(sem("branch_normed"), l * 3 + 3)
                    for i, name in enumerate(("ln_g", "ln_b")):
                        pool.dma_start(lnp[:, i * D:(i + 1) * D], a[name][l, which].partition_broadcast(P)).then_inc(sem("ln_in"), 16)
                for m in range(8):
                    pool.wait_ge(sem("silu_done"), l * 12 + m + 1)
                    if m > 1:
                        pool.wait_ge(sem("squares_summed"), l * 7 + m - 1)
                    pool.tensor_tensor(square(m), qk[:, m, 0:CW], qk[:, m, 0:CW], ALU.mult)\
                        .then_inc(sem("squares"), 1)
                def scale_gate(i):
                    name, v, at = (("z", zv, 16), ("r", rv, 144))[i]
                    if i == 0 and l == 0:
                        pool.wait_ge(sem("norms_in"), 16 * 3 * DEPTH)
                    drained(pool, (name, l, T - 1))
                    vv = v.rearrange("p t (h w) -> p (t h) w", h=H)
                    pool.tensor_tensor(vv, vv, fan(par[:, l * 656 + at:l * 656 + at + P], T * H), ALU.mult)\
                        .then_inc(sem("gates_scaled"), 1)
                scale_gate(0)
                if l:
                    for d in range(DIR):
                        full(pool, ("qs", batch(l - 1, 2, d)))
                for d in range(DIR):
                    pool.dma_start(s_gdn[:, d * W5:(d + 1) * W5].rearrange("p (h e) -> p h e", h=H),
                                   a["state_gdn"][0, l, d].rearrange("h d e -> d h e")).then_inc(sem("gdn_state_in"), 16)
                for p, tiles in enumerate(PAIRS):
                    for d, t in enumerate(tiles):
                        n = batch(l, p, d)
                        if p == 0 and d == 0:
                            pool.wait_ge(sem("log_decay"), l + 1)
                            drained(pool, ("norm", l, 7))
                        if p:
                            m = batch(l, p - 1, d)
                            full(pool, ("av", m))
                            full(pool, ("ds", m))
                            full(pool, ("vnew", m))
                        pool.tensor_tensor(gd(d, "y").rearrange("p (h i) -> p h i", h=H), fan(c(f"tri{d}"), H),
                                           wide(col(GG + t * 8 + d * 4, 4), P), ALU.mult)
                        pool.tensor_tensor(gd(d, "m").rearrange("p (h i) -> p h i", h=H), fan(c("ident"), H),
                                           wide(col(BETA + t * 8 + d * 4, 4), P), ALU.mult).then_inc(sem("gdn_rows"), 1)
                    for v in range(LEVELS):
                        for d, t in enumerate(tiles):
                            n = batch(l, p, d)
                            if v == 0:
                                drained(pool, ("brow", n))
                            elif v > 1:
                                full(pool, ("y", n, v - 1))
                            else:
                                pool.wait_ge(sem("inv_start"), n + 1)
                            pool.tensor_tensor(gd(d, "m").rearrange("p (h i) -> p h i", h=H),
                                               gd(d, "lt").rearrange("p (h i) -> p h i", h=H),
                                               fan(c(f"level{d}_{v}"), H), ALU.mult).then_inc(sem("level_part"), 1)
                for d in range(DIR):
                    drained(pool, ("ds", batch(l, 0, d)))
                    pool.dma_start(new_gdn[0, l, d].rearrange("h d e -> d h e"),
                                   st_out(d).rearrange("p (h e) -> p h e", h=H)).then_inc(sem("outputs"), 16)
                for d in range(DIR):
                    for hh in range(2):
                        if l:
                            full(pool, ("gla_inter", l - 1, 2, d, 1))
                        rows_ = slice(hh * 64, hh * 64 + 64)
                        pool.dma_start(gla_state(1, d)[rows_, :].rearrange("p (a b e) -> p a b e", a=2, b=2)[:, :, hh, :],
                                       a["state_gla"][0, l, d].rearrange("(a b) k e -> b k a e", b=2)[hh])\
                            .then_inc(sem("gla_state_in"), 16)
                pool.wait_ge(sem("outputs"), 32 * (l + 1))
                pool.wait_ge(sem("branch_normed"), l * 3 + 1)
                link(pool.memset(gla_at(0), 0.0))
                link(pool.memset(gla_at(1), 0.0))
                link(pool.memset(gl_qz, 0.0))
                pool.memset(s_gla[:, 0:2 * W5], 0.0).then_inc(sem("gla_zeroed"), 1)
                scale_gate(1)
                for d in range(DIR):
                    drained(pool, ("gla_ds", l, 0, d, 1))
                    for hh in range(2):
                        rows_ = slice(hh * 64, hh * 64 + 64)
                        pool.dma_start(new_gla[0, l, d].rearrange("(a b) k e -> b k a e", b=2)[hh],
                                       gla_state(0, d)[rows_, :].rearrange("p (a b e) -> p a b e", a=2, b=2)[:, :, hh, :])\
                            .then_inc(sem("gla_out"), 16)
                pool.wait_ge(sem("branch_normed"), l * 3 + 2)
                pool.memset(u_att[:, 0:2 * W5], 0.0).then_inc(sem("dq_zeroed"), 1)
                pool.dma_start(ckv[:, 0:W5], a["cache_k"][0, l].rearrange("s h d -> s (h d)")).then_inc(sem("cache_in"), 16)
                pool.dma_start(ckv[:, W5:], a["cache_v"][0, l].rearrange("s h d -> s (h d)")).then_inc(sem("cache_in"), 16)
                for name, v, dst in (("dk", dkv, new_k), ("dv", dvv, new_v)):
                    drained(pool, (name, l, 0))
                    pool.dma_start(dst[0, l].rearrange("s h d -> s (h d)"), v[:, 0, :]).then_inc(sem("kv_out"), 16)
                ln_params(0)
                ln_params(1)
            pool.wait_ge(sem("x_ready"), DEPTH * 2 * T)
            pool.dma_start(y_prompt[0], xv[:, 0, :]).then_inc(sem("outputs"), 16)
            pool.dma_start(y_sample[0].rearrange("(t p) d -> p t d", p=P), xv[:, 1:3, :]).then_inc(sem("outputs"), 16)
            pool.wait_ge(sem("outputs"), 16 * (2 * DEPTH + 2))
            pool.wait_ge(sem("kv_out"), 32 * DEPTH)
            pool.wait_ge(sem("gla_out"), 64 * DEPTH)

        @block.scalar
        def _(act):
            steps = [0]

            def link(ins):
                steps[0] += 1
                ins.then_inc(sem("act_steps"), 1)
                act.wait_ge(sem("act_steps"), steps[0])

            def root(at, n, name, k):
                act.wait_ge(sem(name + "_var"), k)
                act.activation(col(at, n), col(at, n), ACT.Sqrt).then_inc(sem(name + "_std"), 1)

            def centre(l, which):
                n = l * 2 + which
                for t in range(T):
                    root(RS + t, 1, "ln", n * T + t + 1)
                    act.wait_ge(sem("ln_factors"), n * T + t + 1)
                    act.activation(xv[:, t, :], xv[:, t, :], ACT.Identity, bias=col(NMR + t, 1), scale=col(RS + t, 1))\
                        .then_inc(sem("ln_centred"), 1)

            def gates_out(l, which):
                if which:
                    drained(act, (("outl", 1), l, T - 1))
                elif l:
                    act.wait_ge(sem("x_ready"), l * 2 * T)
                for half in range(2):
                    for cond in range(2):
                        ps, free = full(act, ("modg", l, which, half, cond))
                        act.activation(gatev[:, cond, half * W5:(half + 1) * W5], ps[:, :], ACT.Copy).then_inc(free, 1)

            ps, free = full(act, "cond")
            act.wait_ge(sem("condition_padded"), 1)
            act.activation(scol[:, :].rearrange("p (k c) -> p k c", k=KC)[:, :, 0:2], ps[:, 0:16].rearrange("p (c k) -> p k c", c=2),
                           ACT.Silu).then_inc(free, 1)

            def narrow_in(n):
                act.wait_ge(sem("narrow_rows"), n)
                act.activation(otok[:, 0:TOK], mod_bank[:, 0:TOK], ACT.Copy).then_inc(sem("narrow_copied"), 1)

            def modulate(l, which):
                shift, scale = (0, 8) if which == 0 else (24, 32)
                act.wait_ge(sem("mod_out"), l * 2 + which + 1)
                for k in range(1, KC, 2):
                    ps, free = full(act, ("xt", l, which, k))
                    act.activation(xtv[:, k, 0:SEQ], ps[:, 0:SEQ], ACT.Identity, bias=modv[:, l, shift + k, 0:1],
                                   scale=modv[:, l, scale + k, 0:1])
                    act.activation(xtv[:, k, SEQ:], ps[:, SEQ:TOK], ACT.Identity, bias=modv[:, l, shift + k, 1:2],
                                   scale=modv[:, l, scale + k, 1:2]).then_inc(free, 1)

            def mod_rows_in(l, j):
                ps, free = full(act, ("modrow", l, j))
                act.activation(mrow[:, :], ps[:, :], ACT.Copy).then_inc(free, 1)

            for l in range(DEPTH):
                if l == 0:
                    for j in range(6):
                        mod_rows_in(0, j)
                modulate(l, 0)
                for m in range(12):
                    ps, free = full(act, ("qkv", l, m))
                    if m == 0:
                        if l:
                            act.wait_ge(sem("mixed"), l)
                        act.wait_ge(sem("pads"), l + 1)
                    act.activation(qk[:, m, 2:2 + SEQ], ps[:, 0:SEQ], ACT.Copy)
                    act.activation(qk[:, m, 4 + SEQ:4 + TOK], ps[:, SEQ:TOK], ACT.Copy).then_inc(free, 1)
                    if m > 1:
                        silu(act, l, m - 2)
                silu(act, l, 10)
                silu(act, l, 11)
                narrow_in(l * 2 + 1)
                ps, free = full(act, ("lr_rows", l))
                act.activation(otok[:, TOK:2 * TOK], ps[:, 0:TOK], ACT.Copy).then_inc(free, 1)
                ps, free = full(act, ("ba", l))
                bav = ps[:, 0:48].rearrange("p (t c) -> p t c", t=T)
                act.activation(col(BETA, 24).rearrange("p (t c) -> p t c", t=T), bav[:, :, 0:8], ACT.Sigmoid)
                act.activation(col(AB, 24).rearrange("p (t c) -> p t c", t=T), bav[:, :, 8:16], ACT.Copy).then_inc(free, 1)
                ps, free = full(act, ("lr", l))
                act.activation(lrt[0:32, :], ps[0:32, 0:TOK], ACT.Copy).then_inc(free, 1)
                act.wait_ge(sem("decay_in"), l + 1)
                link(act.activation(col(GC, 24), col(AB, 24), ACT.Abs))
                link(act.activation(col(GC, 24), col(GC, 24), ACT.Exp, scale=-1.0))
                link(act.activation(col(GC, 24), col(GC, 24), ACT.Ln, bias=1.0))
                act.activation(col(EXPA, 8), par[:, l * 656:l * 656 + 8], ACT.Exp).then_inc(sem("softplus_part"), 1)
                ps, free = full(act, ("ss", l))
                act.wait_ge(sem("eps_set"), 1)
                act.activation(u_gdn[0:8, 1552:1552 + CW], ps[0:8, 0:CW], ACT.Sqrt, bias=small[0:8, 1010:1011]).then_inc(free, 1)
                gate_in(act, "z", l, zv)
                act.wait_ge(sem("decay_sums"), l + 1)
                act.activation(col(EGC, 24), col(GC, 24), ACT.Exp)
                act.activation(col(ETOT, 24), col(TOTC, 24), ACT.Exp)
                act.activation(col(ETAIL, 24), col(ETAIL, 24), ACT.Exp).then_inc(sem("decays"), 1)
                gates_out(l, 0)
                mod_rows_in(l, 6)
                for t in range(T):
                    for n, v in (("k", ktok), ("v", vtok)):
                        ps, free = full(act, (n + "tok", l, t))
                        act.activation(v[:, t, :], ps[:, :], ACT.Copy).then_inc(free, 1)
                for p, tiles in enumerate(PAIRS):
                    for d in range(DIR):
                        n = batch(l, p, d)
                        drained(act, ("gcrow", n))
                        act.activation(gd(d, "dt"), gd(d, "dt"), ACT.Exp).then_inc(sem("dt_exp"), 1)
                    mod_rows_in(l, 7 + p)
                    for d in range(DIR):
                        ps, free = full(act, ("x0", batch(l, p, d)))
                        act.activation(gd(d, "x"), ps[:, :], ACT.Copy).then_inc(free, 1)
                    for v in range(1, LEVELS):
                        for d in range(DIR):
                            ps, free = full(act, ("y", batch(l, p, d), v))
                            act.activation(gd(d, "y"), ps[:, :], ACT.Copy).then_inc(free, 1)
                mod_rows_in(l, 10)
                branch_root(act, l, 0)
                branch_ot(act, l, 0)
                for t in range(T):
                    ps, free = full(act, ("gqk", l, t))
                    act.activation(gqkv[:, t, 0:256], ps[:, 0:256], ACT.Copy, scale=GLA_DK ** -0.5)
                    act.activation(gqkv[:, t, 256:512], ps[:, 256:512], ACT.Copy).then_inc(free, 1)
                for t in range(T):
                    ps, free = full(act, ("gv", l, t))
                    act.activation(gvv[:, t, :], ps[:, :], ACT.Copy).then_inc(free, 1)
                for t in range(T):
                    ps, _ = full(act, ("glog", l, t))
                    if t:
                        drained(act, ("glog", l, t - 1))
                    else:
                        act.wait_ge(sem("branch_normed"), l * 3 + 1)
                    link(act.activation(gl_ln, ps[:, :], ACT.Abs))
                    link(act.activation(gl_ln, gl_ln, ACT.Exp, scale=-1.0))
                    act.activation(gl_ln, gl_ln, ACT.Ln, bias=1.0).then_inc(sem("gla_ln"), 1)
                gate_in(act, "r", l, rv)
                for p in range(3):
                    if p:
                        full(act, ("q_dec", l, p - 1))
                        full(act, ("gla_ds", l, p - 1, 1, 1))
                    ps, free = full(act, ("gla_rel", l, p))
                    act.activation(gl("q_in"), ps[:, :], ACT.Exp, scale=1.0 / TAU)
                    act.activation(gl("k_in"), ps[:, :], ACT.Exp, scale=-1.0 / TAU).then_inc(free, 1)
                    ps, free = full(act, ("gla_sum", l, p))
                    act.activation(gl("q_dec"), ps[:, :], ACT.Exp, scale=1.0 / TAU).then_inc(free, 1)
                    ps, free = full(act, ("gla_tail", l, p))
                    act.activation(gl("k_tail"), ps[:, :], ACT.Exp, scale=1.0 / TAU).then_inc(free, 1)
                    ps, free = full(act, ("gla_gt", l, p))
                    act.activation(gla_gt(p), ps[:, 0:8], ACT.Exp, scale=1.0 / TAU).then_inc(free, 1)
                    ps, free = full(act, ("q_in", l, p))
                    if p == 0:
                        act.wait_ge(sem("gla_zeroed"), l + 1)
                    for hh in range(2):
                        ins = act.activation(gl_qz[hh * 64:hh * 64 + 64, hh * W5:(hh + 1) * W5], ps[hh * 64:hh * 64 + 64, :], ACT.Copy)
                    ins.then_inc(free, 1)
                    ps, free = full(act, ("k_in", l, p))
                    act.activation(gl_k, ps[:, :], ACT.Copy).then_inc(free, 1)
                    ps, free = full(act, ("q_dec", l, p))
                    act.activation(gl_dec, ps[:, :], ACT.Copy).then_inc(free, 1)
                mod_rows_in(l, 11)
                branch_root(act, l, 1)
                branch_ot(act, l, 1)
                for name, v in (("dq", dqv), ("dk", dkv), ("dv", dvv)):
                    for t in range(T):
                        ps, free = full(act, (name, l, t))
                        act.activation(v[:, t, :], ps[:, :], ACT.Copy).then_inc(free, 1)
                if l + 1 < DEPTH:
                    mod_rows_in(l + 1, 0)
                act.wait_ge(sem("lam_parts"), l + 1)
                act.activation(col(LAM, 2), col(LAM, 2), ACT.Exp).then_inc(sem("lam_exp"), 1)
                for t in range(T + 1):
                    ps, free = full(act, ("kt", l, t))
                    act.activation(dk_all[:, :, t * P:(t + 1) * P], ps[:, :].rearrange("p (h i) -> p h i", h=H), ACT.Copy).then_inc(free, 1)
                for m in range(T * H + 2):
                    if m < T * H:
                        t, h = divmod(m, H)
                        n = l * T * H + m
                        if h == 0:
                            ps, free = full(act, ("qt", l, t))
                            if t == 0:
                                act.wait_ge(sem("dq_zeroed"), l + 1)
                            else:
                                full(act, ("sc", l, m - 1, 1))
                            for s in range(2):
                                ins = act.activation(u_att[s * 64:s * 64 + 64, s * W5:(s + 1) * W5], ps[s * 64:s * 64 + 64, :], ACT.Copy)
                            ins.then_inc(free, 1)
                        nk = P if t == 0 else KEYS
                        if n > 1:
                            act.wait_ge(sem("attn_weights"), n - 1)
                        for s in range(2):
                            ps, free = full(act, ("sc", l, m, s))
                            act.wait_ge(sem("neg_max"), 2 * n + s + 1)
                            act.activation(dp(n, s)[:, 0:nk], ps[:, 0:nk], ACT.Exp, bias=col(NM + n % 2 * 2 + s, 1), scale=DH ** -0.5,
                                           accum_out=col(SUMP + n % 2 * 2 + s, 1)).then_inc(free, 1)
                        if l + 1 < DEPTH and h == 1:
                            mod_rows_in(l + 1, t + 1)
                    if m > 1:
                        n = l * T * H + m - 2
                        nk = P if m - 2 < H else KEYS
                        ps, free = full(act, ("wt", n))
                        if n > 1:
                            full(act, ("att", n - 2))
                        act.activation(dwt(n % 2)[:, 0:nk], ps[:, 0:nk], ACT.Copy).then_inc(free, 1)
                if l + 1 < DEPTH:
                    mod_rows_in(l + 1, 4)
                branch_root(act, l, 2)
                branch_ot(act, l, 2)
                for s in range(3):
                    for half in range(2):
                        for t in range(T):
                            ps, free = full(act, (("mergel", 2 * s + half), l, t))
                            if s == half == t == 0:
                                act.wait_ge(sem("kv_out"), 32 * (l + 1))
                            if s and half == 0 and t == 0:
                                drained(act, ("branch", l, s - 1, T - 1, 1))
                            act.activation(mg[:, t, half * W5:(half + 1) * W5], ps[:, :], ACT.Sigmoid).then_inc(free, 1)
                        if s == half == 0 and l + 1 < DEPTH:
                            mod_rows_in(l + 1, 5)
                for k in range(KC):
                    ps, free = full(act, ("mixt", l, k))
                    act.activation(xtv[:, k, :], ps[:, 0:TOK], ACT.Copy).then_inc(free, 1)
                centre(l, 0)
                gates_out(l, 1)
                modulate(l, 1)
                narrow_in(l * 2 + 2)
                for t in range(T):
                    for half in range(2):
                        ps, free = full(act, ("htok", l, t, half))
                        act.activation(htok[:, t, half * W5:(half + 1) * W5], ps[:, :], ACT.Copy).then_inc(free, 1)
                    if t == 0:
                        ps, free = full(act, ("router", l))
                        act.activation(col(RTR, 48), ps[:, 0:48], ACT.Sigmoid).then_inc(free, 1)
                before = before_layer(act, l)

                def tokens_in(q):
                    for half in range(2):
                        ps, free = made(act, "gather", q + l, half)
                        act.activation(xg[:, half * W5:(half + 1) * W5], ps[:, :], ACT.Copy).then_inc(free, 1)

                def gate_silu(q):
                    ps, free = made(act, "gate", q)
                    act.activation(ag, ps[:, :], ACT.Silu).then_inc(free, 1)

                def turned_in(q):
                    ps, free = made(act, "turned", q)
                    act.activation(ht, ps[:, :], ACT.Copy).then_inc(free, 1)

                def choice_in(q):
                    ps, free = made(act, "choice", q)
                    act.activation(hott, ps[:, 0:TOK], ACT.Copy).then_inc(free, 1)

                def output_in(q):
                    for half in range(2):
                        ps, free = made(act, "out", q, half)
                        act.activation(oe[:, half * W5:(half + 1) * W5], ps[:, :], ACT.Copy).then_inc(free, 1)

                tokens_in(before)
                gate_silu(before)
                tokens_in(before + 1)
                turned_in(before)
                choice_in(before)
                turns = turns_of(act, l)
                with act.Fori(0, turns) as i:
                    n = i + before
                    output_in(n)
                    gate_silu(n + 1)
                    tokens_in(n + 2)
                    turned_in(n + 1)
                    choice_in(n + 1)
                output_in(turns + before)
                centre(l, 1)

        @block.vector
        def _(dve):
            steps = [0]

            def link(ins):
                steps[0] += 1
                ins.then_inc(sem("dve_steps"), 1)
                dve.wait_ge(sem("dve_steps"), steps[0])

            def statistics(t, half):
                ins = dve.bn_stats(col(ST + t * 12 + half * 6, 6), xv[:, t, half * W5:(half + 1) * W5])
                link(ins)

            def variance(n, t):
                link(dve.bn_aggr(col(MV + 2 * t, 2), col(ST + t * 12, 12)))
                dve.tensor_scalar(col(RS + t, 1), col(MV + 2 * t + 1, 1), EPS, None, ALU.add).then_inc(sem("ln_var"), 1)

            def factors(n, t):
                dve.wait_ge(sem("ln_std"), n * T + t + 1)
                link(dve.reciprocal(col(RS + t, 1), col(RS + t, 1)))
                dve.scalar_tensor_tensor(out=col(NMR + t, 1), in0=col(MV + 2 * t, 1), scalar=-1.0, in1=col(RS + t, 1),
                                         op0=ALU.mult, op1=ALU.mult).then_inc(sem("ln_factors"), 1)

            def weight(n, t):
                if t == 0:
                    dve.wait_ge(sem("ln_in"), 32 * (n + 1))
                dve.wait_ge(sem("ln_centred"), n * T + t + 1)
                dve.tensor_tensor(xv[:, t, :], xv[:, t, :], lnp[:, 0:D], ALU.mult).then_inc(sem("ln_weighted"), 1)

            def bias(n, t):
                dve.wait_ge(sem("ln_weighted"), n * T + t + 1)
                dve.tensor_tensor(xv[:, t, :], xv[:, t, :], lnp[:, D:2 * D], ALU.add).then_inc(sem("x_ready"), 1)

            def modulate(l, which):
                shift, scale = (0, 8) if which == 0 else (24, 32)
                dve.wait_ge(sem("mod_out"), l * 2 + which + 1)
                for k in range(0, KC, 2):
                    ps, free = full(dve, ("xt", l, which, k))
                    dve.tensor_scalar(xtv[:, k, 0:SEQ], ps[:, 0:SEQ], modv[:, l, scale + k, 0:1], modv[:, l, shift + k, 0:1],
                                      ALU.mult, ALU.add)
                    dve.tensor_scalar(xtv[:, k, SEQ:], ps[:, SEQ:TOK], modv[:, l, scale + k, 1:2], modv[:, l, shift + k, 1:2],
                                      ALU.mult, ALU.add).then_inc(free, 1)

            def finish(l, br):
                o12 = otok[:, :].rearrange("p (n w) -> p n w", w=P)
                sq = (u_gdn, u_gla, u_att)[br][:, 0:T * W5]
                link(dve.tensor_tensor(sq, otok[:, :], otok[:, :], ALU.mult))
                link(dve.tensor_reduce(col(SS, 12), sq.rearrange("p (n w) -> p n w", w=P), AX.X, ALU.add))
                dve.tensor_scalar(col(SS, 12), col(SS, 12), 1.0 / P, EPS, ALU.mult, ALU.add).then_inc(sem("branch_var"), 1)
                dve.wait_ge(sem("branch_std"), l * 3 + br + 1)
                link(dve.reciprocal(col(SS, 12), col(SS, 12)))
                if br == 2:
                    link(dve.tensor_scalar(col(SS, 12), col(SS, 12), 1.0 - lam_init(l), None, ALU.mult))
                link(dve.tensor_tensor(o12, o12, wide(col(SS, 12), P), ALU.mult))
                if br < 2:
                    dve.wait_ge(sem("gates_scaled"), l * 2 + br + 1)
                    dve.tensor_tensor(ov, ov, (zv, rv)[br], ALU.mult).then_inc(sem("branch_normed"), 1)
                else:
                    dve.tensor_tensor(o12, o12, fan(par[:, l * 656 + 272:l * 656 + 400], 12), ALU.mult).then_inc(sem("branch_normed"), 1)

            def mod_out(l, which):
                dve.wait_ge(sem("mod_done"), l * 2 + which + 1)
                at = l * 48 + which * 24
                dve.tensor_tensor(modt[:, 2 * at:2 * at + 48].rearrange("p (i c) -> p i c", c=2),
                                  mod_bank[:, 2 * at:2 * at + 48].rearrange("p (i c) -> p i c", c=2),
                                  wide(bcol[:, at:at + 24], 2), ALU.add).then_inc(sem("mod_out"), 1)

            dve.memset(scol[:, :], 0.0).then_inc(sem("condition_padded"), 1)
            ps, free = full(dve, "mod_bias")
            dve.tensor_copy(bcol[:, :], ps[:, 0:96]).then_inc(free, 1)
            drained(dve, "mod_bias")
            for at in (8, 32, 56, 80):
                link(dve.tensor_scalar(bcol[:, at:at + 8], bcol[:, at:at + 8], 1.0, None, ALU.add))
            dve.memset(col(1010, 1), EPS).then_inc(sem("eps_set"), 1)
            for l in range(DEPTH):
                if l == 0:
                    mod_out(0, 0)
                    dve.wait_ge(sem("mod_out"), 1)
                dve.memset(mod_bank[:, 0:TOK], 0.0).then_inc(sem("narrow_cleared"), 1)
                ps, free = full(dve, ("taps", l))
                dve.tensor_copy(convc[:, :], ps[:, 0:60]).then_inc(free, 1)
                drained(dve, ("taps", l))
                modulate(l, 0)
                for m in range(12):
                    tmp = conv_out(m)
                    drained(dve, ("qkv", l, m))
                    if m > 1:
                        dve.wait_ge(sem("silu_done"), l * 12 + m - 1)
                    link(dve.tensor_scalar(tmp, qk[:, m, 0:CW], convc[:, m:m + 1], None, ALU.mult))
                    for k in range(1, TAPS):
                        ins = dve.scalar_tensor_tensor(out=tmp, in0=qk[:, m, k:k + CW], scalar=convc[:, 12 * k + m:12 * k + m + 1],
                                                       in1=tmp, op0=ALU.mult, op1=ALU.add)
                        if k < TAPS - 1:
                            link(ins)
                    ins.then_inc(sem("conv_done"), 1)
                drained(dve, ("ba", l))
                ab3 = col(AB, 24).rearrange("p (t c) -> p t c", t=T)
                dve.tensor_tensor(ab3, ab3, fan(par[:, l * 656 + 8:l * 656 + 16], T), ALU.add).then_inc(sem("decay_in"), 1)
                dve.wait_ge(sem("softplus_part"), l + 1)
                link(dve.scalar_tensor_tensor(out=col(GG, 24), in0=col(AB, 24), scalar=0.0, in1=col(GC, 24), op0=ALU.max, op1=ALU.add))
                link(dve.tensor_scalar(col(EXPA, 8), col(EXPA, 8), -1.0, None, ALU.mult))
                gg3 = col(GG, 24).rearrange("p (t c) -> p t c", t=T)
                dve.tensor_tensor(gg3, gg3, fan(col(EXPA, 8), T), ALU.mult).then_inc(sem("log_decay"), 1)
                drained(dve, ("ss", l))
                dve.reciprocal(u_gdn[0:8, 1552:1552 + CW], u_gdn[0:8, 1552:1552 + CW]).then_inc(sem("norms_inverse"), 1)
                for m in range(8):
                    ps, free = full(dve, ("norm", l, m))
                    dve.scalar_tensor_tensor(out=qk[:, m, 0:CW], in0=qk[:, m, 0:CW], scalar=P ** -0.5 if m < 4 else 1.0,
                                             in1=ps[:, 0:CW], op0=ALU.mult, op1=ALU.mult).then_inc(free, 1)
                ps, free = full(dve, ("gc", l))
                dve.wait_ge(sem("log_decay"), l + 1)
                dve.tensor_copy(col(GC, 24), ps[:, 0:24])
                dve.tensor_copy(col(TOTC, 24), ps[:, 32:56]).then_inc(free, 1)
                drained(dve, ("gc", l))
                dve.tensor_tensor(col(ETAIL, 24), col(TOTC, 24), col(GC, 24), ALU.subtract).then_inc(sem("decay_sums"), 1)
                dve.wait_ge(sem("decays"), l + 1)
                link(dve.tensor_tensor(col(BEGC, 24), col(BETA, 24), col(EGC, 24), ALU.mult))

                def h4(ap):
                    return ap.rearrange("p (h i) -> p h i", h=H)

                seen = set()
                for p, tiles in enumerate(PAIRS):
                    for d, t in enumerate(tiles):
                        n = batch(l, p, d)
                        at = t * 8 + d * 4
                        ps, free = full(dve, ("gcrow", n))
                        for h in range(H):
                            ins = dve.tensor_scalar(gd(d, "dt", h), ps[:, h * P:(h + 1) * P], col(GC + at + h, 1), 0.0,
                                                    ALU.subtract, ALU.min)
                        ins.then_inc(free, 1)
                        dve.wait_ge(sem("dt_exp"), n + 1)
                        link(dve.tensor_tensor(h4(gd(d, "dt")), h4(gd(d, "dt")), fan(c(f"tri{d}"), H), ALU.mult))
                        psb, freeb = full(dve, ("brow", n))
                        psq, freeq = full(dve, ("qk", n))
                        dve.tensor_tensor(gd(d, "a"), psq[:, :], gd(d, "dt"), ALU.mult).then_inc(freeq, 1)
                        psk, freek = full(dve, ("kk", n))
                        dve.tensor_tensor(gd(d, "lt"), psk[:, :], gd(d, "dt"), ALU.mult).then_inc(freek, 1)
                        drained(dve, ("kk", n))
                        dve.tensor_tensor(gd(d, "lt"), psb[:, :], gd(d, "lt"), ALU.mult).then_inc(freeb, 1)
                    for d, t in enumerate(tiles):
                        n = batch(l, p, d)
                        dve.wait_ge(sem("level_part"), level_count(l, p, d, 0))
                        dve.tensor_tensor(h4(gd(d, "xt")), fan(c("ident"), H), h4(gd(d, "m")), ALU.subtract).then_inc(sem("inv_start"), 1)
                    for v in range(1, LEVELS):
                        if v > 1:
                            for d in range(DIR):
                                ps, free = full(dve, ("xt_new", batch(l, p, d), v))
                                dve.tensor_copy(gd(d, "xt"), ps[:, :]).then_inc(free, 1)
                        for d, t in enumerate(tiles):
                            n = batch(l, p, d)
                            if v == 1:
                                drained(dve, ("x0", n))
                            if v < LEVELS - 1:
                                if v > 1:
                                    drained(dve, ("xy", n, v - 1))
                                ps, free = full(dve, ("xy", n, v))
                                dve.tensor_tensor(gd(d, "x"), gd(d, "x"), ps[:, :], ALU.subtract).then_inc(free, 1)
                            else:
                                drained(dve, ("xt_new", n, v))
                                ps, free = full(dve, ("xty", n, v))
                                dve.tensor_tensor(gd(d, "xt"), gd(d, "xt"), ps[:, :], ALU.subtract).then_inc(free, 1)
                    for d, t in enumerate(tiles):
                        n = batch(l, p, d)
                        at = t * 8 + d * 4
                        drained(dve, ("vtok", l, t))
                        ins = dve.tensor_tensor(h4(gd(d, "y")), h4(vtok[:, t, :]), wide(col(BETA + at, 4), P), ALU.mult)
                        if p == 0:
                            ins.then_inc(sem("gdn_rhs"), 1)
                            continue
                        link(ins)
                        ps, free = full(dve, ("ks", n))
                        dve.tensor_tensor(h4(gd(d, "m")), h4(ps[:, :]), wide(col(BEGC + at, 4), P), ALU.mult).then_inc(free, 1)
                        drained(dve, ("ks", n))
                        dve.tensor_tensor(gd(d, "y"), gd(d, "y"), gd(d, "m"), ALU.subtract).then_inc(sem("gdn_rhs"), 1)
                        ps, free = full(dve, ("qs", n))
                        dve.tensor_tensor(h4(gd(d, "dt")), h4(ps[:, :]), wide(col(EGC + at, 4), P), ALU.mult).then_inc(free, 1)
                        drained(dve, ("qs", n))
                    for d, t in enumerate(tiles):
                        n = batch(l, p, d)
                        at = t * 8 + d * 4
                        ps, free = full(dve, ("vnew", n))
                        if p:
                            dve.wait_ge(sem("gdn_rhs"), n + 1)
                        link(dve.tensor_copy(gd(d, "x"), ps[:, :]))
                        dve.tensor_tensor(h4(gd(d, "m")), h4(ps[:, :]), wide(col(ETAIL + at, 4), P), ALU.mult).then_inc(free, 1)
                    for d, t in enumerate(tiles):
                        n = batch(l, p, d)
                        at = t * 8 + d * 4
                        ps, free = full(dve, ("av", n))
                        if p == 0:
                            if t in seen:
                                dve.tensor_tensor(ov[:, t, :], ov[:, t, :], ps[:, :], ALU.add).then_inc(free, 1)
                            else:
                                dve.tensor_copy(ov[:, t, :], ps[:, :]).then_inc(free, 1)
                        else:
                            if t in seen:
                                link(dve.tensor_tensor(gd(d, "dt"), gd(d, "dt"), ov[:, t, :], ALU.add))
                            dve.tensor_tensor(ov[:, t, :], gd(d, "dt"), ps[:, :], ALU.add).then_inc(free, 1)
                        drained(dve, ("av", n))
                        seen.add(t)
                        if p == 2:
                            continue
                        if p == 0:
                            if l:
                                dve.wait_ge(sem("gla_out"), 64 * l)
                            ps, free = full(dve, ("ds", n))
                            dve.tensor_copy(st_out(d), ps[:, :]).then_inc(free, 1)
                        else:
                            s = s_gdn[:, d * W5:(d + 1) * W5]
                            link(dve.tensor_tensor(h4(s), h4(s), wide(col(ETOT + at, 4), P), ALU.mult))
                            ps, free = full(dve, ("ds", n))
                            dve.tensor_tensor(s, s, ps[:, :], ALU.add).then_inc(free, 1)
                finish(l, 0)

                for t in range(T):
                    ps, free = full(dve, ("glog", l, t))
                    dve.wait_ge(sem("gla_ln"), l * T + t + 1)
                    dve.scalar_tensor_tensor(out=u_gla[:, t * W5:(t + 1) * W5], in0=ps[:, :], scalar=0.0, in1=gl_ln,
                                             op0=ALU.min, op1=ALU.subtract).then_inc(free, 1)
                seen = set()
                for p, tiles in enumerate(PAIRS):
                    for name, src, key in (("q_in", 0, "gla_rel"), ("k_in", 256, "gla_rel"), ("q_dec", 0, "gla_sum"), ("k_tail", 256, "gla_tail")):
                        drained(dve, (key, l, p))
                        for d, t in enumerate(tiles):
                            w = gl(name)[:, d * 256:(d + 1) * 256]
                            ins = dve.tensor_tensor(w, w, gqkv[:, t, src:src + 256], ALU.mult)
                        ins.then_inc(sem("gla_decayed"), 1)
                    for d, t in enumerate(tiles):
                        ps, free = full(dve, ("gla_a", l, p, d))
                        if p == 0 and d == 0:
                            dve.wait_ge(sem("gla_zeroed"), l + 1)
                        dve.copy_predicated(h4(gla_at(d)), fan(c(f"sum{d}").bitcast(U32), H), h4(ps[:, :])).then_inc(free, 1)
                    for d, t in enumerate(tiles):
                        ps, free = full(dve, ("gla_av", l, p, d))
                        if t in seen:
                            dve.tensor_tensor(ov[:, t, :], ov[:, t, :], ps[:, :], ALU.add).then_inc(free, 1)
                        else:
                            if p == 0:
                                drained(dve, ("ot", l, 0, H - 1))
                            dve.tensor_copy(ov[:, t, :], ps[:, :]).then_inc(free, 1)
                        seen.add(t)
                        drained(dve, ("gla_av", l, p, d))
                    for step in range(2):
                        for d, t in enumerate(tiles):
                            ch = step if d == 0 else 1 - step
                            tok = slice(ch * HALF, (ch + 1) * HALF)
                            ps, free = full(dve, ("gla_inter", l, p, d, step))
                            dve.tensor_tensor(ov[tok, t, :], ov[tok, t, :], ps[tok, :], ALU.add).then_inc(free, 1)
                            drained(dve, ("gla_inter", l, p, d, step))
                            if p == 2 and step == 1:
                                continue
                            if step == 0:
                                drained(dve, ("gla_gt", l, p))
                            ps, free = full(dve, ("gla_ds", l, p, d, step))
                            s = gla_state(p, d)
                            for hp in range(2):
                                for hh in range(2):
                                    rr, cc = slice(hh * 64, hh * 64 + 64), slice(hp * 256 + hh * P, hp * 256 + hh * P + P)
                                    g0 = (d * 2 + hp) * 2 + ch
                                    ins = dve.scalar_tensor_tensor(out=s[rr, cc], in0=s[rr, cc], scalar=gla_gt(p)[rr, g0:g0 + 1],
                                                                   in1=ps[rr, cc], op0=ALU.mult, op1=ALU.add)
                            ins.then_inc(free, 1)
                            drained(dve, ("gla_ds", l, p, d, step))
                finish(l, 1)

                lp = par[:, l * 656 + 400:l * 656 + 656].rearrange("p (a s d) -> p a s d", a=2, s=2)
                link(dve.tensor_tensor(col(LPROD, 128).rearrange("p (a d) -> p a d", a=2), lp[:, :, 0, :], lp[:, :, 1, :], ALU.mult))
                dve.tensor_reduce(col(LAM, 2), col(LPROD, 128).rearrange("p (a d) -> p a d", a=2), AX.X, ALU.add).then_inc(sem("lam_parts"), 1)
                tmp = u_att[:, 3072:3584]
                for t in (1, 2):
                    for name, v in (("dq", dqv), ("dk", dkv)):
                        drained(dve, (name, l, t))
                        rope = c("rope", (t - 1) * P, t * P)
                        s = v[:, t, :]
                        s5 = s.rearrange("p (g r j w) -> p g r j w", g=8, r=2, j=2)
                        tp5 = tmp.rearrange("p (g r j w) -> p g r j w", g=8, r=2, j=2)
                        sin = rope[:, 64:128].rearrange("p (r j w) -> p r j w", r=2, j=2)
                        for j in range(2):
                            for r in range(2):
                                link(dve.tensor_tensor(tp5[:, :, r, j, :],
                                                       s5[:, :, r, 1 - j, :],
                                                       fan(sin[:, r, j, :], 8), ALU.mult))
                        s8 = s.rearrange("p (g w) -> p g w", g=8)
                        link(dve.tensor_tensor(s8, s8, fan(rope[:, 0:64], 8), ALU.mult))
                        dve.tensor_tensor(s, s, tmp, ALU.add).then_inc(sem("roped"), 1)
                        dve.wait_ge(sem("roped"), (l * 2 + t - 1) * 2 + (1 if name == "dq" else 2))
                mod_out(l, 1)
                dve.wait_ge(sem("lam_exp"), l + 1)
                link(dve.tensor_tensor(col(LAM, 1), col(LAM, 1), col(LAM + 1, 1), ALU.subtract))
                link(dve.tensor_scalar(col(LAM, 1), col(LAM, 1), lam_init(l), None, ALU.add))
                for m in range(T * H + 4):
                    if m < T * H:
                        n = l * T * H + m
                        nk = P if m < H else KEYS
                        for s in range(2):
                            top = col(NM + n % 2 * 2 + s, 1)
                            ps, _ = full(dve, ("sc", l, m, s))
                            link(dve.tensor_reduce(top, ps[:, 0:nk], AX.X, ALU.max))
                            dve.tensor_scalar(top, top, -DH ** -0.5, None, ALU.mult).then_inc(sem("neg_max"), 1)
                    if 0 < m <= T * H:
                        n = l * T * H + m - 1
                        nk = P if m <= H else KEYS
                        drained(dve, ("sc", l, m - 1, 0))
                        drained(dve, ("sc", l, m - 1, 1))
                        rp = RP + n % 2 * 2
                        if n > 1:
                            dve.wait_ge(sem("attn_weights"), n - 1)
                        link(dve.reciprocal(col(rp, 2), col(SUMP + n % 2 * 2, 2)))
                        link(dve.tensor_tensor(col(rp + 1, 1), col(rp + 1, 1), col(LAM, 1), ALU.mult))
                        link(dve.tensor_scalar(dp(n, 1)[:, 0:nk], dp(n, 1)[:, 0:nk], col(rp + 1, 1), None, ALU.mult))
                        if n > 1:
                            full(dve, ("wt", n - 2))
                        dve.scalar_tensor_tensor(out=dw(n % 2)[:, 0:nk], in0=dp(n, 0)[:, 0:nk], scalar=col(rp, 1), in1=dp(n, 1)[:, 0:nk],
                                                 op0=ALU.mult, op1=ALU.subtract).then_inc(sem("attn_weights"), 1)
                    if m > 3:
                        t, h = divmod(m - 4, H)
                        n = l * T * H + m - 4
                        ps, free = full(dve, ("att", n))
                        if m == 4:
                            drained(dve, ("ot", l, 1, H - 1))
                        dve.tensor_copy(ov[:, t, h * P:(h + 1) * P], ps[:, 0:P]).then_inc(free, 1)
                drained(dve, ("att", (l + 1) * T * H - 1))
                finish(l, 2)

                tmp = mtmp
                for s in range(3):
                    for t in range(T):
                        for half in range(2):
                            cut = slice(half * W5, (half + 1) * W5)
                            ps, free = full(dve, ("branch", l, s, t, half))
                            drained(dve, (("mergel", 2 * s + half), l, t))
                            if s == 0:
                                dve.tensor_tensor(mix[:, t, cut], mg[:, t, cut], ps[:, :], ALU.mult).then_inc(free, 1)
                                drained(dve, ("branch", l, s, t, half))
                            else:
                                dve.tensor_tensor(tmp, mg[:, t, cut], ps[:, :], ALU.mult).then_inc(free, 1)
                                drained(dve, ("branch", l, s, t, half))
                                ins = dve.tensor_tensor(mix[:, t, cut], mix[:, t, cut], tmp, ALU.add)
                                if s == 2 and t == T - 1 and half == 1:
                                    ins.then_inc(sem("mixed"), 1)
                                else:
                                    link(ins)
                if l + 1 < DEPTH:
                    mod_out(l + 1, 0)
                dve.wait_ge(sem("mod_out"), min(l * 2 + 3, DEPTH * 2))
                dve.memset(mod_bank[:, 0:TOK], 0.0).then_inc(sem("narrow_cleared"), 1)
                drained(dve, ("modg", l, 0, 1, 1))
                for half in range(2):
                    for t in range(T):
                        cut = slice(half * W5, (half + 1) * W5)
                        ps, free = full(dve, (("outl", half), l, t))
                        dve.tensor_tensor(tmp, gatev[:, min(t, 1), cut], ps[:, :], ALU.mult).then_inc(free, 1)
                        drained(dve, (("outl", half), l, t))
                        link(dve.scalar_tensor_tensor(out=xv[:, t, cut], in0=xv[:, t, cut], scalar=ALPHA, in1=tmp, op0=ALU.mult, op1=ALU.add))
                        statistics(t, half)
                        if half == 1:
                            variance(l * 2, t)
                            factors(l * 2, t)
                            weight(l * 2, t)
                            bias(l * 2, t)
                modulate(l, 1)

                sc, bi, cm, eq, rk, gs, gr = (RTR + at for at in (0, 48, 96, 288, 480, 528, 540))
                drained(dve, ("router", l))
                dve.wait_ge(sem("router_in"), 32)
                link(dve.tensor_tensor(col(bi, 48).rearrange("p (t e) -> p t e", t=T), col(sc, 48).rearrange("p (t e) -> p t e", t=T),
                                       fan(rbias[:, :], T), ALU.add))

                def ranks(src, n, dst):
                    v = col(src, 4 * n).rearrange("p (g f) -> p g f", g=n)
                    other = v.unsqueeze(2).broadcast_to([P, n, 4, 4])
                    own = v.unsqueeze(3).broadcast_to([P, n, 4, 4])
                    a4 = col(cm, 16 * n).rearrange("p (g e f) -> p g e f", g=n, e=4)
                    b4 = col(eq, 16 * n).rearrange("p (g e f) -> p g e f", g=n, e=4)
                    link(dve.tensor_tensor(a4, other, own, ALU.is_gt))
                    link(dve.tensor_tensor(b4, other, own, ALU.is_equal))
                    b3 = col(eq, 16 * n).rearrange("p (g w) -> p g w", g=n)
                    link(dve.tensor_tensor(b3, b3, fan(c("before"), n), ALU.mult))
                    link(dve.tensor_tensor(col(cm, 16 * n), col(cm, 16 * n), col(eq, 16 * n), ALU.add))
                    link(dve.tensor_reduce(col(dst, 4 * n), col(cm, 16 * n).rearrange("p (a f) -> p a f", f=4), AX.X, ALU.add))

                ranks(bi, T * NG, rk)
                link(dve.tensor_scalar(col(rk, 48), col(rk, 48), 1.5, None, ALU.is_lt))
                link(dve.tensor_tensor(col(bi, 48), col(bi, 48), col(rk, 48), ALU.mult))
                link(dve.tensor_reduce(col(gs, 12), col(bi, 48).rearrange("p (g f) -> p g f", f=4), AX.X, ALU.add))
                ranks(gs, T, gr)
                link(dve.tensor_scalar(col(gr, 12), col(gr, 12), 0.5, None, ALU.is_lt))
                link(dve.tensor_tensor(col(sc, 48), col(sc, 48), col(rk, 48), ALU.mult))
                link(dve.tensor_tensor(col(sc, 48).rearrange("p (g f) -> p g f", f=4), col(sc, 48).rearrange("p (g f) -> p g f", f=4),
                                       wide(col(gr, 12), 4), ALU.mult))
                link(dve.tensor_reduce(col(RS, T), col(sc, 48).rearrange("p (t e) -> p t e", t=T), AX.X, ALU.add))
                link(dve.reciprocal(col(RS, T), col(RS, T)))
                gates = col(cm, T * EP).rearrange("p (t e) -> p t e", t=T)
                places = col(cm + T * EP, T * EP).rearrange("p (t e) -> p t e", t=T)
                link(dve.memset(col(cm, T * EP), 0.0))
                link(dve.memset(col(cm + T * EP, T * EP), -1.0))
                link(dve.tensor_tensor(gates[:, :, 0:E], col(sc, 48).rearrange("p (t e) -> p t e", t=T), wide(col(RS, T), E), ALU.mult))
                dve.tensor_scalar(chosen, col(sc, 48), 0.0, None, ALU.is_gt).then_inc(sem("chosen"), 1)
                dve.memset(proj[:, T * D:2 * T * D], 0.0)
                ps, free = full(dve, ("places", l))
                dve.wait_ge(sem("chosen"), l + 1)
                link(dve.scalar_tensor_tensor(out=col(bi, 48), in0=ps[:, 0:48], scalar=1.0, in1=chosen, op0=ALU.mult, op1=ALU.mult))
                link(dve.tensor_scalar(places[:, :, 0:E], col(bi, 48).rearrange("p (t e) -> p t e", t=T), -1.0, None, ALU.add))
                num, mor, inc = (small[0:1, RTR + at:RTR + at + E] for at in (0, 16, 32))
                dve.tensor_copy(num, ps[0:1, 48:64]).then_inc(free, 1)
                drained(dve, ("places", l))
                before = before_layer(dve, l)
                gsel = col(GSEL, 2 * T).rearrange("p (t u) -> p t u", t=T)

                def pick(q, experts, firsts):
                    for u in range(2):
                        e = bass.ds(experts[u], 1)
                        dve.tensor_copy(gsel[:, :, u:u + 1], gates[:, :, e])
                        ins = dve.tensor_tensor(hot[:, :, u, :], fan(c("slots")[:, bass.ds(firsts[u], SLOTS)], T),
                                                places[:, :, e].broadcast_to([P, T, SLOTS]), ALU.is_equal)
                    ins.then_inc(sem("hot"), 1)

                def weigh(q):
                    dve.wait_ge(sem("hot"), q + (l + 1))
                    for u in range(2):
                        ins = dve.tensor_tensor(hotg[:, :, u, :], hot[:, :, u, :], wide(gsel[:, :, u], SLOTS), ALU.mult)
                    ins.then_inc(sem("hot_gated"), 1)

                def multiply(q):
                    used(dve, "gate", q)
                    ps, free = made(dve, "up", q)
                    dve.tensor_tensor(hact, ag, ps[:, :], ALU.mult).then_inc(free, 1)

                def add(q):
                    for k in range(2 * T):
                        ycut = yacc[:, k // 2, k % 2 * W5:(k % 2 + 1) * W5]
                        added(dve, q, k)
                        ps, free = made(dve, "back", q, k)
                        dve.tensor_tensor(ycut, ycut, ps[:, :], ALU.add).then_inc(free, 1)

                pick(before, (0, 1), (0, 0))
                weigh(before)
                link(dve.tensor_scalar(mor, num, float(SLOTS), None, ALU.is_gt))
                for s in range(2, TOK // SLOTS):
                    link(dve.scalar_tensor_tensor(out=mor, in0=num, scalar=float(SLOTS * s), in1=mor, op0=ALU.is_gt, op1=ALU.add))
                link(dve.tensor_tensor_scan(inc, c("ones")[0:1, 0:E], mor, 0.0, ALU.mult, ALU.add))
                nj = JOBS - E
                ja = otok[0:1, 2 * W5:2 * W5 + nj * E].rearrange("p (j e) -> p j e", j=nj)
                je, jc = (otok[0:1, 2 * W5 + at:2 * W5 + at + nj] for at in (nj * E, nj * (E + 1)))
                idx = c("slots")[0:1, 0:nj]
                link(dve.tensor_tensor(ja, fan(inc, nj), wide(idx, E), ALU.is_le))
                link(dve.tensor_reduce(je, ja, AX.X, ALU.add))
                link(dve.tensor_tensor(ja, ja, fan(mor, nj), ALU.mult))
                link(dve.tensor_reduce(jc, ja, AX.X, ALU.add))
                link(dve.tensor_tensor(jc, idx, jc, ALU.subtract))
                link(dve.tensor_scalar(jc, jc, 1.0, float(SLOTS), ALU.add, ALU.mult))
                link(dve.tensor_scalar(jc, jc, float(TOK - SLOTS), 0.0, ALU.min, ALU.max))
                pairs, total = otok[0:1, 2 * W5 + nj * (E + 2):2 * W5 + nj * (E + 3)], small[0:1, 1060:1061]
                link(dve.tensor_scalar(pairs, idx, 2.0, None, ALU.mult))
                link(dve.tensor_tensor(pairs, pairs, inc[:, E - 1:E].broadcast_to([1, nj]), ALU.is_lt))
                link(dve.tensor_reduce(num[:, 0:1], pairs, AX.X, ALU.add))
                if l:
                    dve.wait_ge(sem("experts_done"), l)
                for at in (W_AT, X_AT):
                    link(dve.tensor_copy(jobs[0:1, at:at + E], c("slots")[0:1, 0:E]))
                link(dve.tensor_scalar(jobs[0:1, S_AT:S_AT + E], c("slots")[0:1, 0:E], 0.0, None, ALU.mult))
                link(dve.tensor_copy(jobs[0:1, X_AT + E:X_AT + JOBS], je))
                link(dve.tensor_scalar(je, je, float(E - 1), None, ALU.min))
                link(dve.tensor_copy(jobs[0:1, W_AT + E:W_AT + JOBS], je))
                link(dve.tensor_copy(jobs[0:1, S_AT + E:S_AT + JOBS], jc))
                if l == 0:
                    link(dve.tensor_scalar(total, num[:, 0:1], float(E // 2), None, ALU.add))
                else:
                    link(dve.tensor_tensor(total, total, num[:, 0:1], ALU.add))
                    link(dve.tensor_scalar(total, total, float(E // 2), None, ALU.add))
                if l + 1 < DEPTH:
                    link(dve.tensor_copy(jobs[0:1, BEFORE_AT + l + 1:BEFORE_AT + l + 2], total))
                dve.tensor_scalar(jobs[0:1, TURNS_AT:TURNS_AT + 1], num[:, 0:1], float(E // 2 - 1), None, ALU.add)\
                    .then_inc(sem("jobs_listed"), 1)
                turns = turns_of(dve, l)
                made(dve, "gather", before + l, 1)
                dve.wait_ge(sem("hot_gated"), before + 1)
                pick(before + 1, (2, 3), (0, 0))
                multiply(before)
                with dve.Fori(0, turns) as i:
                    n = i + before
                    made(dve, "choice", n)
                    weigh(n + 1)
                    made(dve, "gather", n + (l + 1), 1)
                    experts, firsts = ([dve.value_load(jobs[0:1, bass.ds(i * 2 + (at + 4 + u), 1)], min_val=0, max_val=top)
                                        for u in range(2)] for at, top in ((X_AT, E), (S_AT, TOK - SLOTS)))
                    dve.wait_ge(sem("hot_gated"), n + 2)
                    pick(n + 2, experts, firsts)
                    multiply(n + 1)
                    add(n)
                last = turns + before
                added(dve, last, 2 * T - 1)
                drained(dve, ("modg", l, 1, 1, 1))
                for t in range(T):
                    link(dve.tensor_tensor(yacc[:, t, :], yacc[:, t, :], gatev[:, min(t, 1), :], ALU.mult))
                    link(dve.scalar_tensor_tensor(out=xv[:, t, :], in0=xv[:, t, :], scalar=ALPHA, in1=yacc[:, t, :], op0=ALU.mult, op1=ALU.add))
                n = l * 2 + 1
                for t in range(T):
                    cuts = [slice(half * W5, (half + 1) * W5) for half in range(2)]
                    for half in range(2):
                        ps, free = made(dve, "back", last, 2 * t + half)
                        dve.tensor_tensor(yacc[:, t, cuts[half]], gatev[:, min(t, 1), cuts[half]], ps[:, :], ALU.mult).then_inc(free, 1)
                    if t:
                        factors(n, t - 1)
                    for half in range(2):
                        used(dve, "back", last, 2 * t + half)
                        link(dve.tensor_tensor(xv[:, t, cuts[half]], xv[:, t, cuts[half]], yacc[:, t, cuts[half]], ALU.add))
                    for half in range(2):
                        statistics(t, half)
                    variance(n, t)
                    if t:
                        weight(n, t - 1)
                factors(n, T - 1)
                bias(n, 0)
                bias(n, 1)
                weight(n, T - 1)
                bias(n, T - 1)


_INS = ["x_prompt", "x_sample", "c", "state_gdn", "state_gla", "cache_k", "cache_v", "c_ctx", "w_mod", "b_mod", "w_in",
        "gdn_conv", "gdn_a_log", "gdn_dt_bias", "gdn_norm", "gla_w_gate", "gla_b_gate", "gla_norm", "diff_lambda",
        "diff_norm", "w_branch", "w_out", "ln_g", "ln_b", "router_w", "router_b", "exp_w_gate", "exp_w_up", "exp_w_down"]
_OUTS = [("y_prompt", (1, SEQ, D)), ("y_sample", (1, DEC, D)), ("new_gdn", (1, DEPTH, 2, H, P, P)),
         ("new_gla", (1, DEPTH, 2, H, GLA_DK, P)), ("new_k", (1, DEPTH, SEQ, H, P)), ("new_v", (1, DEPTH, SEQ, H, P))]


def kernel(**inputs):
    import numpy as _np
    import concourse.bacc as _bacc
    from concourse import mybir as _mybir
    from concourse.bass_utils import run_bass_kernel_spmd as _run

    nc = _bacc.Bacc("TRN2", target_bir_lowering=False, num_devices=1)
    arrays = {f"in_{n}": _np.ascontiguousarray(inputs[n]) for n in _INS}
    arrays["in_consts"] = constants()[0]
    dram = {n: nc.dram_tensor(n, v.shape, _mybir.dt.from_np(v.dtype), kind="ExternalInput").ap() for n, v in arrays.items()}
    outs = [nc.dram_tensor(n, shape, F32, kind="ExternalOutput").ap() for n, shape in _OUTS]
    program(nc, {n: dram[f"in_{n}"] for n in _INS}, dram["in_consts"], *outs)
    r = _run(nc, [arrays], core_ids=[0])
    return tuple(r.results[0][n] for n, _ in _OUTS)
```
